# Optimizing a Trainium2 kernel written in Bass

```python
import jax, jax.numpy as jnp
from jax import lax
import numpy as np

D_MODEL = 2048
BATCH = 1
SEQ = 1024
DEPTH = 1

CTX_LEN = 256
GRID_W = 64
MIX_WIDTH = D_MODEL
MLSTM_WIDTH = MIX_WIDTH // 2
N_HEADS = 4
DV = MLSTM_WIDTH // N_HEADS
DQK = DV // 2
QK_WIDTH = N_HEADS * DQK
N_DIRS = 2
GATE_COLS = N_DIRS * 2 * N_HEADS
CHUNK = 64
QK_CONV = 5
FORGET_BIAS = 3.0
POOL_WIDTH = MIX_WIDTH - MLSTM_WIDTH
POOL_WINDOWS = (2, 4, 8, 16)
POOL_GC = POOL_WIDTH // len(POOL_WINDOWS)
N_EXPERTS = 16
EC_FACTOR = 2
D_EXPERT = D_MODEL // 2
N_MOD = 6
EPS = 1e-6

K_OFF = 0
V_OFF = K_OFF + QK_WIDTH
G_OFF = V_OFF + MLSTM_WIDTH
Q_OFF = G_OFF + GATE_COLS
O_OFF = Q_OFF + QK_WIDTH
P_OFF = O_OFF + MLSTM_WIDTH
IN_COLS = P_OFF + POOL_WIDTH

kernel_name = "hybrid_mlstm_pool_ecmoe_dit_layer"

def rmsnorm(x, g):
    xf = x.astype(jnp.float32)
    y = xf * lax.rsqrt(jnp.mean(xf * xf, -1, keepdims=True) + EPS)
    return (y * g.astype(jnp.float32)).astype(x.dtype)

def short_conv(x, w):
    pad = QK_CONV // 2
    T = x.shape[1]
    xp = jnp.pad(x, ((0, 0), (pad, pad), (0, 0)))
    y = xp[:, 0:T] * w[0]
    for j in range(1, QK_CONV):
        y = y + xp[:, j:j + T] * w[j]
    return jax.nn.silu(y)

def split_heads(t, dh):
    B_, T, _ = t.shape
    return t.reshape(B_, T, N_HEADS, dh).transpose(0, 2, 1, 3)

def _rev(t):
    return jnp.flip(t, axis=2)

def zero_state(b):
    return (jnp.zeros((b, N_HEADS, DQK, DV), jnp.float32),
            jnp.zeros((b, N_HEADS, DQK), jnp.float32),
            jnp.zeros((b, N_HEADS), jnp.float32))

def mlstm_kvg(p, conv_k_w, b_gates):
    B_, T, _ = p.shape
    k = short_conv(p[..., K_OFF:V_OFF], conv_k_w) * (DQK ** -0.5)
    v = p[..., V_OFF:G_OFF]
    g = (p[..., G_OFF:Q_OFF] + b_gates).astype(jnp.float32)
    g = g.reshape(B_, T, N_DIRS, 2, N_HEADS).transpose(2, 3, 0, 4, 1)
    li = g[:, 0]
    lf = jax.nn.log_sigmoid(g[:, 1])
    return split_heads(k, DQK), split_heads(v, DV), li, lf

def mlstm_q(p, conv_q_w):
    return split_heads(short_conv(p[..., Q_OFF:O_OFF], conv_q_w), DQK)

def mlstm_chunkwise(k, v, li, lf, state0, q=None):
    B_, H, T, _ = k.shape
    nc = T // CHUNK
    kc = k.astype(jnp.float32).reshape(B_, H, nc, CHUNK, DQK)
    vc = v.astype(jnp.float32).reshape(B_, H, nc, CHUNK, DV)
    lic = li.reshape(B_, H, nc, CHUNK)
    b = jnp.cumsum(lf.reshape(B_, H, nc, CHUNK), -1)
    b_end = b[..., -1]
    a = b_end[..., None] - b + lic
    m_loc = jnp.max(a, -1)
    w = jnp.exp(a - m_loc[..., None])
    C_loc = jnp.einsum('bhnl,bhnlk,bhnlv->bhnkv', w, kc, vc)
    n_loc = jnp.einsum('bhnl,bhnlk->bhnk', w, kc)

    def step(state, inp):
        C, n, m = state
        Cl, nl, ml, be = inp
        m_new = jnp.maximum(be + m, ml)
        sp = jnp.exp(be + m - m_new)
        sl = jnp.exp(ml - m_new)
        C_new = sp[..., None, None] * C + sl[..., None, None] * Cl
        n_new = sp[..., None] * n + sl[..., None] * nl
        return (C_new, n_new, m_new), (C, n, m)

    xs = (jnp.moveaxis(C_loc, 2, 0), jnp.moveaxis(n_loc, 2, 0),
          jnp.moveaxis(m_loc, 2, 0), jnp.moveaxis(b_end, 2, 0))
    final, prev = lax.scan(step, state0, xs)
    if q is None:
        return None, final
    Cp, npv, mp = [jnp.moveaxis(s, 0, 2) for s in prev]
    qc = q.astype(jnp.float32).reshape(B_, H, nc, CHUNK, DQK)
    lower = jnp.tril(jnp.ones((CHUNK, CHUNK), bool))
    d = b[..., :, None] - b[..., None, :] + lic[..., None, :]
    d = jnp.where(lower, d, -jnp.inf)
    g = b + mp[..., None]
    m_out = jnp.maximum(g, jnp.max(d, -1))
    s = jnp.einsum('bhntk,bhnsk->bhnts', qc, kc) * jnp.exp(d - m_out[..., None])
    wi = jnp.exp(g - m_out)
    num = (jnp.einsum('bhnts,bhnsv->bhntv', s, vc)
           + wi[..., None] * jnp.einsum('bhntk,bhnkv->bhntv', qc, Cp))
    den = jnp.sum(s, -1) + wi * jnp.einsum('bhntk,bhnk->bhnt', qc, npv)
    h = num / jnp.maximum(jnp.abs(den), jnp.exp(-m_out))[..., None]
    return h.reshape(B_, H, T, DV), final

def mlstm_scans(k, v, li, lf, init, q=None):
    h_f, fin_f = mlstm_chunkwise(k, v, li[0], lf[0], init[0], q)
    h_b, fin_b = mlstm_chunkwise(_rev(k), _rev(v), _rev(li[1]), _rev(lf[1]), init[1],
                                 None if q is None else _rev(q))
    h = None if q is None else h_f + _rev(h_b)
    return h, (fin_f, fin_b)

def mlstm_out(p, h, head_g):
    B_, H, T, _ = h.shape
    h = h * lax.rsqrt(jnp.mean(h * h, -1, keepdims=True) + EPS)
    h = h.transpose(0, 2, 1, 3).reshape(B_, T, MLSTM_WIDTH).astype(p.dtype) * head_g
    return h * jax.nn.sigmoid(p[..., O_OFF:P_OFF])

def box_sum(x, w, axis):
    n = x.shape[axis]
    P = jnp.cumsum(x.astype(jnp.float32), axis)
    P = jnp.concatenate([jnp.zeros_like(lax.slice_in_dim(P, 0, 1, axis=axis)), P], axis)
    t = jnp.arange(n)
    lo = jnp.clip(t - w // 2, 0, n)
    hi = jnp.clip(t + w // 2, 0, n)
    s = jnp.take(P, hi, axis=axis) - jnp.take(P, lo, axis=axis)
    return s, (hi - lo).astype(jnp.float32)

def pool_grid(u, w):
    B_, T, C = u.shape
    rows = T // GRID_W
    g = u.reshape(B_, rows, GRID_W, C)
    s, cc = box_sum(g, w, 2)
    s, cr = box_sum(s, w, 1)
    mean = s / (cr[:, None, None] * cc[None, :, None])
    return (mean.reshape(B_, T, C) - u.astype(jnp.float32)).astype(u.dtype)

def pool_seq(u, w):
    s, cnt = box_sum(u, w, 1)
    return (s / cnt[:, None] - u.astype(jnp.float32)).astype(u.dtype)

def pool_mix(p, pool_w, pool_scale, grid):
    u = p[..., P_OFF:IN_COLS]
    outs = []
    for gi, w in enumerate(POOL_WINDOWS):
        ug = u[..., gi * POOL_GC:(gi + 1) * POOL_GC]
        d = pool_grid(ug, w) if grid else pool_seq(ug, w)
        outs.append(d @ pool_w[gi])
    return jnp.concatenate(outs, -1) * pool_scale

def expert_choice_ffn(h, w_router, w_gate, w_up, w_down):
    B_, T, D = h.shape
    cap = EC_FACTOR * T // N_EXPERTS
    aff = jax.nn.softmax(jnp.einsum('btd,de->bte', h, w_router).astype(jnp.float32), -1)
    gate, idx = lax.top_k(jnp.swapaxes(aff, 1, 2), cap)
    xs = jax.vmap(lambda hb, ib: hb[ib])(h, idx)
    a = (jax.nn.silu(jnp.einsum('becd,edf->becf', xs, w_gate))
         * jnp.einsum('becd,edf->becf', xs, w_up))
    y = jnp.einsum('becf,efd->becd', a, w_down) * gate[..., None].astype(h.dtype)
    return jax.vmap(lambda yb, ib: jnp.zeros((T, D), yb.dtype).at[ib.reshape(-1)].add(
        yb.reshape(-1, D)))(y, idx)

def setup_inputs(seed: int = 0) -> dict:
    key = jax.random.key(seed)
    ks = jax.random.split(key, 24)
    nrm = jax.random.normal
    L = DEPTH
    base_gate = jnp.asarray(np.tile(np.repeat(np.array([0.0, FORGET_BIAS], np.float32), N_HEADS), N_DIRS))
    return {
        "x": nrm(ks[0], (BATCH, SEQ, D_MODEL), jnp.float32),
        "c": nrm(ks[1], (BATCH, D_MODEL), jnp.float32),
        "ctx": nrm(ks[2], (BATCH, CTX_LEN, D_MODEL), jnp.float32),
        "c_ctx": nrm(ks[3], (D_MODEL,), jnp.float32),
        "w_mod": nrm(ks[4], (L, D_MODEL, N_MOD * D_MODEL), jnp.float32) * (0.5 * D_MODEL ** -0.5),
        "b_mod": nrm(ks[5], (L, N_MOD * D_MODEL), jnp.float32) * 0.02,
        "norm1": 1.0 + 0.1 * nrm(ks[6], (L, D_MODEL), jnp.float32),
        "w_in": nrm(ks[7], (L, D_MODEL, IN_COLS), jnp.float32) * D_MODEL ** -0.5,
        "conv_q_w": nrm(ks[8], (L, QK_CONV, QK_WIDTH), jnp.float32) * QK_CONV ** -0.5,
        "conv_k_w": nrm(ks[9], (L, QK_CONV, QK_WIDTH), jnp.float32) * QK_CONV ** -0.5,
        "b_gates": base_gate + 0.3 * nrm(ks[10], (L, GATE_COLS), jnp.float32),
        "head_g": 1.0 + 0.1 * nrm(ks[11], (L, MLSTM_WIDTH), jnp.float32),
        "pool_w": nrm(ks[12], (L, len(POOL_WINDOWS), POOL_GC, POOL_GC), jnp.float32) * POOL_GC ** -0.5,
        "pool_scale": 1.0 + 0.1 * nrm(ks[13], (L, POOL_WIDTH), jnp.float32),
        "w_out": nrm(ks[14], (L, MIX_WIDTH, D_MODEL), jnp.float32) * MIX_WIDTH ** -0.5,
        "norm2": 1.0 + 0.1 * nrm(ks[15], (L, D_MODEL), jnp.float32),
        "w_router": nrm(ks[16], (L, D_MODEL, N_EXPERTS), jnp.float32) * D_MODEL ** -0.5,
        "w_gate": nrm(ks[17], (L, N_EXPERTS, D_MODEL, D_EXPERT), jnp.float32) * D_MODEL ** -0.5,
        "w_up": nrm(ks[18], (L, N_EXPERTS, D_MODEL, D_EXPERT), jnp.float32) * D_MODEL ** -0.5,
        "w_down": nrm(ks[19], (L, N_EXPERTS, D_EXPERT, D_MODEL), jnp.float32) * D_EXPERT ** -0.5,
        "norm_f": 1.0 + 0.1 * nrm(ks[20], (D_MODEL,), jnp.float32),
    }

def reference(x, c, ctx, c_ctx, w_mod, b_mod, norm1, w_in, conv_q_w, conv_k_w, b_gates,
              head_g, pool_w, pool_scale, w_out, norm2, w_router, w_gate, w_up, w_down, norm_f):
    B_ = x.shape[0]
    xc = ctx
    for l in range(DEPTH):
        update_ctx = l < DEPTH - 1
        mod = (jax.nn.silu(c) @ w_mod[l] + b_mod[l]).reshape(B_, N_MOD, 1, D_MODEL)
        mod_c = (jax.nn.silu(c_ctx) @ w_mod[l] + b_mod[l]).reshape(N_MOD, D_MODEL)

        hc = rmsnorm(xc, norm1[l]) * (1.0 + mod_c[1]) + mod_c[0]
        pc = hc @ (w_in[l] if update_ctx else w_in[l][:, :Q_OFF])
        kc, vc, lic, lfc = mlstm_kvg(pc, conv_k_w[l], b_gates[l])
        qc = mlstm_q(pc, conv_q_w[l]) if update_ctx else None
        zs = zero_state(B_)
        hm_c, ctx_states = mlstm_scans(kc, vc, lic, lfc, (zs, zs), qc)

        h = rmsnorm(x, norm1[l]) * (1.0 + mod[:, 1]) + mod[:, 0]
        p = h @ w_in[l]
        k, v, li, lf = mlstm_kvg(p, conv_k_w[l], b_gates[l])
        hm, _ = mlstm_scans(k, v, li, lf, ctx_states, mlstm_q(p, conv_q_w[l]))
        mix = jnp.concatenate([mlstm_out(p, hm, head_g[l]),
                               pool_mix(p, pool_w[l], pool_scale[l], True)], -1) @ w_out[l]
        x = x + mod[:, 2] * mix
        if update_ctx:
            mix_c = jnp.concatenate([mlstm_out(pc, hm_c, head_g[l]),
                                     pool_mix(pc, pool_w[l], pool_scale[l], False)], -1) @ w_out[l]
            xc = xc + mod_c[2] * mix_c

        h2 = rmsnorm(x, norm2[l]) * (1.0 + mod[:, 4]) + mod[:, 3]
        x = x + mod[:, 5] * expert_choice_ffn(h2, w_router[l], w_gate[l], w_up[l], w_down[l])
        if update_ctx:
            h2c = rmsnorm(xc, norm2[l]) * (1.0 + mod_c[4]) + mod_c[3]
            xc = xc + mod_c[5] * expert_choice_ffn(h2c, w_router[l], w_gate[l], w_up[l], w_down[l])
    return rmsnorm(x, norm_f)


_drawn_inputs = setup_inputs


def setup_inputs(seed=0):
    import zlib

    import numpy as np

    out = dict(_drawn_inputs(seed))
    spreads = {}
    factors = {'ctx': 6.339, 'c_ctx': 8.0, 'b_mod': 2.898, 'head_g': 4.529, 'norm2': 3.149}
    for name, (base, spread) in spreads.items():
        noise = np.random.default_rng([zlib.crc32(name.encode()), seed]).standard_normal(out[name].shape)
        drawn = base * np.exp(spread * noise) if base else spread * noise
        out[name] = __import__('jax').numpy.asarray(drawn.astype(out[name].dtype))
    for name, factor in factors.items():
        out[name] = (out[name] * factor).astype(out[name].dtype)
    return out
```

```python
import concourse.bass as bass
from concourse import mybir
from contextlib import ExitStack


def hybrid_layer_kernel(nc, x, c, ctx, c_ctx, w_mod, b_mod, norm1, w_in, conv_q_w, conv_k_w, b_gates,
                        head_g, pool_w, pool_scale, w_out, norm2, w_router, w_gate, w_up, w_down, norm_f,
                        inv_count, out):
    fp32, u32 = mybir.dt.float32, mybir.dt.uint32
    ALU, ACT, AX = mybir.AluOpType, mybir.ActivationFunctionType, mybir.AxisListType

    P = 128
    T, D = x.shape[1], x.shape[2]
    TC = ctx.shape[1]
    KD = D // P
    NT, NC = T // P, TC // P
    NTT = NT + NC
    H = 4
    DV, DQK = 256, 128
    MW = H * DV
    PW = D - MW
    NG = 4
    GC = PW // NG
    GRID_W = 64
    ROWS = T // GRID_W
    WINDOWS = (2, 4, 8, 16)
    K_OFF, V_OFF = 0, H * DQK
    G_OFF = V_OFF + MW
    Q_OFF = G_OFF + 16
    O_OFF = Q_OFF + H * DQK
    P_OFF = O_OFF + MW
    TAPS = 5
    NMOD = 6
    EXP = w_router.shape[2]
    CAP = 2 * T // EXP
    F = w_gate.shape[3]
    KF = F // P
    EPS = 1e-6
    KSCALE = float(DQK) ** -0.5
    NEG = -1e30
    BN = 512
    NB = D // BN

    PADC = 2
    RAWN = 3 * PADC + TC + T
    CONVN = RAWN - 2 * PADC
    LAT0 = TC + PADC
    GR = 36
    LAST = (P - 1, 0)

    def chunk_of(d, j):
        if d == 0:
            return j
        return NC - 1 - j if j < NC else NTT - 1 - (j - NC)

    groups, order = [], []

    def add_group(kind, *what):
        groups.append((kind, *what))
        order.append(("group", len(groups) - 1))

    def add_step(h, i):
        if i >= 1 and i <= NTT:
            order.append(("B", h, i - 1))
        if i < NTT:
            order.append(("A", h, i))

    def after_group(h, i):
        if h < 0:
            return
        if i <= NTT:
            add_step(h, i)
        if i == NTT + 1:
            order.append(("normalise", h))
        if i == NTT + 3:
            for ft in range(2):
                for half in range(2):
                    add_group("T", h, ft, half)
            order.append(("store_mix", h))

    for h in range(H):
        i = 0
        for what in [("K", h, 0), ("K", h, 1), ("K", h, 2), ("Q", h, 0), ("Q", h, 1)] \
                + [("V", h, t) for t in range(NTT)] + [("O", h, ft, half) for ft in range(2) for half in range(2)]:
            add_group(*what)
            if what[:1] + what[2:] == ("K", 2):
                order.append(("conv", h, 0))
            if what[:1] + what[2:] == ("Q", 1):
                order.append(("conv", h, 1))
                order.append(("silu", h, 0))
            if what[:1] + what[2:] == ("V", 1):
                order.append(("silu", h, 1))
            after_group(h - 1, i)
            i += 1
    i = 0
    for g in range(NG):
        for a in range(2):
            for half in range(2):
                add_group("P", g, a, half)
                if half == 1:
                    order.append(("pool", g, a))
                if g > 0 and (a, half) == (0, 0):
                    for fo in range(2):
                        for m_half in range(2):
                            add_group("M", g - 1, fo, m_half)
                    order.append(("store_pool", g - 1))
                after_group(H - 1, i)
                i += 1
    for fo in range(2):
        for half in range(2):
            add_group("M", NG - 1, fo, half)
    order.append(("store_pool", NG - 1))

    evac, counts = [], [0, 0]
    for g in groups:
        dve = int(g[0] == "T")
        counts[dve] += 1
        evac.append((dve, counts[dve]))
    group_no = {g: n for n, g in enumerate(groups)}

    slots = [(kind, h) for h in range(H) for kind in ("KQ", "V", "O")] + [("P", g) for g in range(NG)]
    slot_no = {s: n for n, s in enumerate(slots)}
    SLOTC = 256
    slot_of = {"K": "KQ", "Q": "KQ", "V": "V", "O": "O", "P": "P"}
    last_group = {}
    for n, g in enumerate(groups):
        if g[0] in slot_of:
            last_group[slot_no[(slot_of[g[0]], g[1])]] = n

    mod_scr = nc.dram_tensor("mod_scr", [NMOD, 2, D], fp32).ap()
    mix_scr = nc.dram_tensor("mix_scr", [D, T], fp32).ap()
    x1_scr = nc.dram_tensor("x1_scr", [T, D], fp32).ap()
    xn_scr = nc.dram_tensor("xn_scr", [T, D], fp32).ap()

    x_t = x[0].rearrange("(n p) d -> n p d", p=P)
    ctx_t = ctx[0].rearrange("(n p) d -> n p d", p=P)
    w_in_v = w_in[0].rearrange("(k p) n -> p k n", p=P)
    w_out_v = w_out[0].rearrange("(k p) n -> p k n", p=P)
    w_mod_v = w_mod[0].rearrange("(p k) n -> p k n", k=KD)
    mix_v = mix_scr.rearrange("(k p) t -> p k t", p=P)
    x1_t = x1_scr.rearrange("(n p) d -> n p d", p=P)
    xn_t = xn_scr.rearrange("(n p) d -> n p d", p=P)
    out_t = out[0].rearrange("(n p) d -> n p d", p=P)

    es = ExitStack()
    with es:
        es.enter_context(nc.allow_non_contiguous_dma(reason="vectors laid out over the partitions"))

        def sem(name):
            return es.enter_context(nc.semaphore(name))

        ARENA = 52736
        arena = es.enter_context(nc.sbuf_tensor("arena", [P, ARENA], fp32))
        at = [0]

        def take(n, *dims):
            v = arena[:, at[0]:at[0] + n]
            at[0] += n
            if len(dims) == 2:
                return v.rearrange("p (a b) -> p a b", a=dims[0])
            if len(dims) == 3:
                return v.rearrange("p (a b c) -> p a b c", a=dims[0], b=dims[1])
            return v

        ident = take(P)
        small = take(128)
        ones_row = take(P)
        shift1, scale1 = take(2 * KD, 2, KD), take(2 * KD, 2, KD)
        shift2, scale2 = take(KD), take(KD)
        norm_col = take(2 * KD, 2, KD)
        top = at[0]
        hT = take(KD * T, KD, T)
        hcT = take(KD * TC, KD, TC)
        ring = take(2 * KD * SLOTC, 2, KD, SLOTC)
        kT = take(2 * CONVN, 2, CONVN)
        qT = take(2 * T, 2, T)
        v_off = at[0]
        V = take(2 * NTT * (DV + 1), 2, NTT, DV + 1)
        raw = take(RAWN)
        sig_o = take(2 * T, 2, T)
        h_sum = take(NT * DV, NT, DV)
        Dm, WI, Pm, qw, kw = (take(2 * P, 2, P) for _ in range(5))
        C = take(4 * (DV + 1), 2, 2, DV + 1)
        MxN = take(NTT * P)
        mask = take(2 * P, 2, P)
        sel = take(8 * P, 8, P)
        Acol = take(NTT * GR, NTT, GR)
        EM = take(NTT * GR, NTT, GR)
        mp_col = take(8 * NTT, 8, NTT)
        conv_w = take(2 * H * TAPS, 2, H, TAPS)
        headg_col = take(2 * H)
        pscale_col = take(2 * NG)
        pmix = take(2 * T, 2, T)
        poolw = take(2 * GC, 2, GC)
        assert at[0] <= ARENA, at[0]

        def view(lo, *dims):
            n = 1
            for v in dims:
                n *= v
            v = arena[:, lo:lo + n]
            if len(dims) == 2:
                return v.rearrange("p (a b) -> p a b", a=dims[0])
            if len(dims) == 3:
                return v.rearrange("p (a b c) -> p a b c", a=dims[0], b=dims[1])
            return v

        o = v_off
        xt = view(o, 2, D)
        o = top + KD * T + KD * TC
        mod_ring = view(o, 4, D)
        o += 4 * D
        cc = view(o, 2, KD)
        mod_row = view(o + 2 * KD, 2, D)
        assert 2 * KD + 2 * D <= 2 * CONVN + 2 * T
        LI, LF, GB, GA = (view(v_off + n * NTT * P, NTT * P) for n in range(4))
        GT = pmix.rearrange("p a b -> p (a b)")[:, 0:NTT * P]
        GX = sig_o.rearrange("p a b -> p (a b)")[:, 0:NTT * P]
        reset = raw[:, 0:NTT * P]
        wg = h_sum.rearrange("p a b -> p (a b)")[:, 0:KD * 100].rearrange("p (k c) -> p k c", k=KD)
        PADG = 8
        HW_ = GRID_W + 2 * PADG
        HR = ROWS + 2 * PADG
        o = top + KD * T
        pool_v = [view(o, HR, GRID_W), view(o + HR * GRID_W, HR, GRID_W)]
        o = top + KD * T + KD * TC + 2 * KD * SLOTC
        pool_h0 = view(o, ROWS, HW_)
        assert ROWS * HW_ <= CONVN
        pool_h1 = view(v_off, ROWS, HW_)
        o = v_off + ROWS * HW_
        inv_b = view(o, T)
        assert ROWS * HW_ + T <= NTT * (DV + 1)
        dT = [qT[:, 0, :], raw[:, 0:T]]

        at[0] = top
        mixT = take(KD * T, KD, T)
        x1 = take(NT * D, NT, D)
        wo = take(2 * KD * BN, 2, KD, BN)
        gate1_b = take(D)
        tmp = take(2 * BN, 2, BN)
        assert at[0] <= ARENA, at[0]
        xnT = view(top, 2, KD, P)
        wr = view(top + 2 * KD * P, KD, EXP)
        wrs = view(top + 2 * KD * P + KD * EXP, KD, EXP)
        o = top + 2 * KD * P + 2 * KD * EXP
        lb = view(o, EXP)
        L0 = view(o + 16, NT, EXP)
        L1 = view(o + 16 + NT * EXP, NT, EXP)
        lst = view(o + 16 + 2 * NT * EXP, 4, NT)
        o += 16 + 2 * NT * EXP + 4 * NT
        aff = view(o, T)
        top_v = view(o + T, P)
        top_f = view(o + T + P, P)
        top_i = view(o + T + 2 * P, P).bitcast(u32)
        o += T + 3 * P
        idx_all = view(o, EXP + 1).bitcast(u32)
        gate_all = view(o + EXP + 1, EXP + 1)
        idx_gather = view(o + 2 * EXP + 2, 1).bitcast(u32)
        idx_scatter = view(o + 2 * EXP + 3, 1).bitcast(u32)
        gate_now = view(o + 2 * EXP + 4, 1)
        o += 2 * EXP + 8
        gate2_b = view(o, D)
        o += D
        xs = view(o, D)
        o += D
        xsT = view(o, KD, CAP)
        o += D
        act, actT = view(top, F), view(top + F, KF, CAP)
        y = view(o, D)
        o += D
        assert o <= top + KD * T
        o = top + KD * T
        ESL = 6
        ering = [view(o + n * 4 * F, 4, F) for n in range(ESL)]
        o += ESL * 4 * F
        assert o <= ARENA
        normf_b = view(top + KD * T, D)
        ft = [view(top + KD * T + D * (1 + n), D) for n in range(8)]

        bank = [es.enter_context(nc.psum_tensor(f"bank{n}", [P, BN], fp32)) for n in range(8)]
        PR = bank[0:2]
        A_b, N_b, C_b = bank[2:4], bank[4:6], bank[6:8]

        ld_const = sem("ld_const")
        ld_x = [sem(f"ld_x_{n}") for n in range(2)]
        consts = sem("consts")
        x_stat = sem("x_stat")
        x_scaled = sem("x_scaled")
        x_tr = sem("x_tr")
        x_evA, x_evD = sem("x_evA"), sem("x_evD")
        silu_c = sem("silu_c")
        ld_mod = [sem(f"ld_mod_{n}") for n in range(4)]
        mod_used = sem("mod_used")
        ld_bmod = [sem(f"ld_bmod_{n}") for n in range(2)]
        mod_free = sem("mod_free")
        mod_sum = sem("mod_sum")
        mod_st = [sem(f"mod_st_{n}") for n in range(2)]
        ld_cols = sem("ld_cols")
        h_ready = sem("h_ready")
        ld_wg = sem("ld_wg")
        gate_mm = sem("gate_mm")
        gate_ev = sem("gate_ev")
        gact = sem("gact")
        grow = sem("grow")
        gcol_mm = sem("gcol_mm")
        gcols = sem("gcols")
        gfree = sem("gfree")
        ld_w = [sem(f"ld_w_{n}") for n in range(2)]
        grp = sem("grp")
        evA, evD = sem("evA"), sem("evD")
        conv_done = sem("conv_done")
        silu_done = sem("silu_done")
        stA = [sem(f"stA_{d}") for d in range(2)]
        expd = [sem(f"expd_{d}") for d in range(2)]
        fac = [sem(f"fac_{d}") for d in range(2)]
        stB = [sem(f"stB_{d}") for d in range(2)]
        cup = [sem(f"cup_{d}") for d in range(2)]
        hsq = sem("hsq")
        hrs = sem("hrs")
        hnorm = sem("hnorm")
        mix_st = sem("mix_st")
        pool_d = sem("pool_d")
        ld_pool = sem("ld_pool")
        pmix_st = sem("pmix_st")
        ld_mix = sem("ld_mix")
        ld_x1 = sem("ld_x1")
        ld_g1 = sem("ld_g1")
        ld_wo = [sem(f"ld_wo_{n}") for n in range(2)]
        wo_used = sem("wo_used")
        o_mm = sem("o_mm")
        o_ev = sem("o_ev")
        x1_st = sem("x1_st")
        x1_sq = sem("x1_sq")
        x1_n = sem("x1_n")
        xn_st = sem("xn_st")
        ld_r = sem("ld_r")
        wr_s = sem("wr_s")
        r_mm = sem("r_mm")
        r_ev = sem("r_ev")
        r_tr = sem("r_tr")
        rt_ev = sem("rt_ev")
        r_log = sem("r_log")
        sm_a, sm_d = sem("sm_a"), sem("sm_d")
        aff_mm, aff_ev = sem("aff_mm"), sem("aff_ev")
        topk = sem("topk")
        topk_mm, topk_ev = sem("topk_mm"), sem("topk_ev")
        idx_r = sem("idx_r")
        ld_g2 = sem("ld_g2")
        ld_e = [sem(f"ld_e_{n}") for n in range(ESL)]
        e_used = sem("e_used")
        cols_set = sem("cols_set")
        gathered = sem("gathered")
        scattered = sem("scattered")
        xs_mm, xs_evA, xs_evD = sem("xs_mm"), sem("xs_evA"), sem("xs_evD")
        g_act, a_rdy = sem("g_act"), sem("a_rdy")
        a_mm, a_ev, y_ev = sem("a_mm"), sem("a_ev"), sem("y_ev")
        ld_nf = sem("ld_nf")
        ld_f = [sem(f"ld_f_{n}") for n in range(8)]
        f_sq, f_rs, f_out = sem("f_sq"), sem("f_rs"), sem("f_out")
        out_st = sem("out_st")
        passed_sp, passed_pool = sem("passed_sp"), sem("passed_pool")
        dv = sem("dv")
        ac = sem("ac")

        ssx, rsx = small[:, 0:16], small[:, 16:32]
        bg = small[:, 32:33]
        one = small[:, 33:34]
        den = small[:, 34:36]
        ssh, rsh = small[:, 40:48], small[:, 48:56]
        mpr = small[:, 56:56 + NTT + 1]
        ss1, rs1 = small[:, 72:80], small[:, 80:88]
        ssf, rsf = small[:, 88:96], small[:, 96:104]
        eps = small[:, 104:105]

        block = es.enter_context(nc.Block())

        @block.sync
        def _(sp):
            for i in range(NTT):
                if i >= 2:
                    sp.wait_ge(x_evA, 2 * (i - 1))
                    sp.wait_ge(x_evD, 2 * (i - 1))
                sp.dma_start(xt[:, i % 2, :], ctx_t[i] if i < NC else x_t[i - NC]).then_inc(ld_x[i % 2], 16)
            for n in range(4):
                sp.dma_start(mod_ring[:, n, :], w_mod_v[:, n, 0:D]).then_inc(ld_mod[n], 16)
            with sp.Fori(0, NMOD - 1) as m:
                for n in range(4, KD + 4):
                    sp.wait_ge(mod_used, m * KD + (n - 3))
                    sp.sem_inc(passed_sp)
                    src = w_mod_v[:, n, bass.ds(m * D, D)] if n < KD else w_mod_v[:, n - KD, bass.ds(m * D + D, D)]
                    sp.dma_start(mod_ring[:, n % 4, :], src).then_inc(ld_mod[n % 4], 16)
            for n in range(4, KD):
                sp.wait_ge(mod_used, (NMOD - 1) * KD + n - 3)
                sp.dma_start(mod_ring[:, n % 4, :], w_mod_v[:, n, (NMOD - 1) * D:NMOD * D]).then_inc(ld_mod[n % 4], 16)
            sp.wait_ge(mod_used, NMOD * KD)
            for n, (kind, h) in enumerate(slots):
                if n >= 2:
                    sp.wait_ge(grp, last_group[n - 2] + 1)
                dst = ring[:, n % 2]
                if kind == "KQ":
                    sp.dma_start(dst[:, :, 0:DQK], w_in_v[:, :, K_OFF + h * DQK:K_OFF + (h + 1) * DQK]).then_inc(ld_w[n % 2], 16)
                    sp.dma_start(dst[:, :, DQK:2 * DQK], w_in_v[:, :, Q_OFF + h * DQK:Q_OFF + (h + 1) * DQK]).then_inc(ld_w[n % 2], 16)
                else:
                    off = {"V": V_OFF, "O": O_OFF, "P": P_OFF}[kind] + h * SLOTC
                    sp.dma_start(dst, w_in_v[:, :, off:off + SLOTC]).then_inc(ld_w[n % 2], 32)
            sp.wait_ge(grp, len(groups))
            sp.wait_ge(evA, counts[0])
            sp.wait_ge(evD, counts[1])
            sp.wait_ge(mix_st, 16 * H)
            sp.wait_ge(pmix_st, 16 * NG)
            for n in range(2):
                sp.dma_start(wo[:, n], w_out_v[:, :, n * BN:(n + 1) * BN]).then_inc(ld_wo[n], 16)
                if n == 0:
                    sp.dma_start(mixT[:, 0:KD // 2, :], mix_v[:, 0:KD // 2, :]).then_inc(ld_mix, 16)
                    sp.dma_start(mixT[:, KD // 2:, :], mix_v[:, KD // 2:, :]).then_inc(ld_mix, 16)
                    sp.dma_start(x1, x[0].rearrange("(n p) d -> p n d", p=P)).then_inc(ld_x1, 16)
                    sp.dma_start(gate1_b, mod_scr[2, 0:1, :].to_broadcast([P, D])).then_inc(ld_g1, 16)
            for n in range(2, NB):
                sp.wait_ge(o_mm, (n - 1) * NT)
                sp.dma_start(wo[:, n % 2], w_out_v[:, :, n * BN:(n + 1) * BN]).then_inc(ld_wo[n % 2], 16)
            sp.wait_ge(o_mm, NB * NT)
            sp.dma_start(wr, w_router[0].rearrange("(k p) e -> p k e", p=P)).then_inc(ld_r, 16)
            sp.dma_start(gate2_b, mod_scr[5, 0:1, :].to_broadcast([P, D])).then_inc(ld_g2, 16)
            wg_v = w_gate[0].rearrange("e (k p) n -> e p k n", p=P)
            wu_v = w_up[0].rearrange("e (k p) n -> e p k n", p=P)
            wd_v = w_down[0].rearrange("e (k p) n -> e p k n", p=P)

            def piece(e, i):
                if i < 4:
                    return ering[i % ESL], wg_v[e, :, 4 * i:4 * i + 4, :]
                if i < 8:
                    return ering[i % ESL], wu_v[e, :, 4 * (i - 4):4 * (i - 4) + 4, :]
                dst = ering[i % ESL].rearrange("p a b -> p (a b)").rearrange("p (a b) -> p a b", a=2)
                return dst, wd_v[e, :, 2 * (i - 8):2 * (i - 8) + 2, :]

            sp.wait_ge(x1_st, 16 * NT)
            sp.wait_ge(xn_st, 16 * NT)
            sp.wait_ge(r_tr, 4 * NT)
            for i in range(ESL):
                dst, src = piece(0, i)
                sp.dma_start(dst, src).then_inc(ld_e[i % ESL], 16)
            with sp.Fori(0, EXP - 1) as e:
                for i in range(ESL, 12 + ESL):
                    sp.wait_ge(e_used, e * 12 + (i - ESL + 1))
                    sp.sem_inc(passed_sp)
                    dst, src = piece(e, i) if i < 12 else piece(e + 1, i - 12)
                    sp.dma_start(dst, src).then_inc(ld_e[i % ESL], 16)
            for i in range(ESL, 12):
                sp.wait_ge(e_used, (EXP - 1) * 12 + (i - ESL + 1))
                dst, src = piece(EXP - 1, i)
                sp.dma_start(dst, src).then_inc(ld_e[i % ESL], 16)
            sp.wait_ge(e_used, EXP * 12)
            sp.dma_start(normf_b, norm_f.rearrange("(a d) -> a d", a=1).to_broadcast([P, D])).then_inc(ld_nf, 16)
            sp.wait_ge(scattered, 16 * EXP)
            for i in range(NT):
                sp.dma_start(ft[i], x1_t[i]).then_inc(ld_f[i], 16)
            for i in range(NT):
                sp.wait_ge(f_out, i + 1)
                sp.dma_start(out_t[i], ft[i]).then_inc(out_st, 16)
            sp.wait_ge(out_st, 16 * NT)

        @block.gpsimd
        def _(pool):
            eng = nc.gpsimd
            eng.memset(ident, 0.0)
            eng.memset(ones_row, 1.0)
            eng.memset(mask, 0.0)
            eng.memset(sel, 0.0)
            eng.memset(small, 0.0).then_inc(consts, 1)
            pool.wait_ge(consts, 1)
            eng.memset(one, 1.0)
            eng.memset(eps, EPS)
            eng.affine_select(out=ident, in_=ident, compare_op=ALU.not_equal, fill=1.0, base=0,
                              pattern=[[-1, P]], channel_multiplier=1)
            eng.affine_select(out=mask[:, 0], in_=mask[:, 0], compare_op=ALU.is_ge, fill=NEG, base=0,
                              pattern=[[1, P]], channel_multiplier=-1)
            eng.affine_select(out=mask[:, 1], in_=mask[:, 1], compare_op=ALU.is_ge, fill=NEG, base=0,
                              pattern=[[-1, P]], channel_multiplier=1)
            s4 = sel.rearrange("p (d h) n -> p d h n", d=2)
            eng.affine_select(out=s4, in_=s4, compare_op=ALU.not_equal, fill=-1.0, base=0,
                              pattern=[[-32, 2], [-1, 4], [0, P]], channel_multiplier=1).then_inc(consts, 1)
            eng.memset(wg, 0.0).then_inc(consts, 1)
            pool.wait_ge(consts, 3)
            for n, col in enumerate((0, 8, 4, 12)):
                eng.dma_start(wg[:, :, 32 * n:32 * n + 4], w_in_v[:, :, G_OFF + col:G_OFF + col + 4]).then_inc(ld_wg, 16)
                eng.dma_start(bg[32 * n:32 * n + 4, :], b_gates[0, col:col + 4].rearrange("(p a) -> p a", a=1)).then_inc(ld_wg, 16)
            for m in range(2):
                eng.dma_start(mod_row[0:2, m, :], b_mod[0:1, m * D:(m + 1) * D].to_broadcast([2, D])).then_inc(ld_bmod[m], 16)
            for m in range(NMOD):
                pool.wait_ge(mod_sum, m + 1)
                eng.dma_start(mod_scr[m], mod_row[0:2, m % 2, :]).then_inc(mod_st[m % 2], 16)
                pool.wait_ge(mod_st[m % 2], 16 * (m // 2 + 1))
                if m + 2 < NMOD:
                    eng.dma_start(mod_row[0:2, m % 2, :], b_mod[0:1, (m + 2) * D:(m + 3) * D].to_broadcast([2, D])).then_inc(ld_bmod[m % 2], 16)
                if m == 1:
                    for r in range(2):
                        eng.dma_start(shift1[:, r, :], mod_scr[0, r, :].rearrange("(k p) -> p k", p=P)).then_inc(ld_cols, 16)
                        eng.dma_start(scale1[:, r, :], mod_scr[1, r, :].rearrange("(k p) -> p k", p=P)).then_inc(ld_cols, 16)
            eng.dma_start(shift2, mod_scr[3, 0, :].rearrange("(k p) -> p k", p=P)).then_inc(ld_cols, 16)
            eng.dma_start(scale2, mod_scr[4, 0, :].rearrange("(k p) -> p k", p=P)).then_inc(ld_cols, 16)
            last = {("store_mix", h): group_no[("T", h, 1, 1)] for h in range(H)}
            last.update({("store_pool", g): group_no[("M", g, 1, 1)] for g in range(NG)})
            pooled = [0]
            for item in order:
                if item[0] == "store_mix":
                    h = item[1]
                    pool.wait_ge(evD, evac[last[item]][1])
                    eng.dma_start(mix_v[:, 2 * h:2 * h + 2, :], sig_o).then_inc(mix_st, 16)
                elif item[0] == "store_pool":
                    g = item[1]
                    pool.wait_ge(evA, evac[last[item]][1])
                    eng.dma_start(mix_v[:, 2 * H + 2 * g:2 * H + 2 * g + 2, :], pmix).then_inc(pmix_st, 16)
                elif item[0] == "pool" and item[2] == 0:
                    g = item[1]
                    if g == 0:
                        pool.wait_ge(stB[0], (H - 1) * NTT)
                        pool.wait_ge(stB[1], (H - 1) * NTT)
                    else:
                        pool.wait_ge(pool_d, 2 * g)
                        pool.wait_ge(grp, group_no[("M", g - 1, 1, 1)] + 1)
                    eng.dma_start(inv_b, inv_count[g:g + 1, :].to_broadcast([P, T])).then_inc(ld_pool, 16)
                    eng.dma_start(poolw, pool_w[0, g].rearrange("(k p) n -> p k n", p=P)).then_inc(ld_pool, 16)
            for i in range(NT):
                pool.wait_ge(o_ev, (NB - 1) * NT + i + 1)
                eng.dma_start(x1_t[i], x1[:, i, :]).then_inc(x1_st, 16)
                pool.wait_ge(x1_n, i + 1)
                eng.dma_start(xn_t[i], x1[:, i, :]).then_inc(xn_st, 16)
            pool.wait_ge(xn_st, 16 * NT)
            pool.wait_ge(x1_st, 16 * NT)
            pool.wait_ge(idx_r, 1)
            eng.indirect_dma_start(xs, None, xn_scr, bass.IndirectOffsetOnAxis(ap=idx_gather, axis=0)).then_inc(gathered, 16)
            with pool.Fori(0, EXP) as e:
                pool.wait_ge(xs_mm, e + 1)
                pool.wait_ge(idx_r, e + 2)
                pool.sem_inc(passed_pool)
                eng.indirect_dma_start(xs, None, xn_scr, bass.IndirectOffsetOnAxis(ap=idx_gather, axis=0)).then_inc(gathered, 16)
                pool.wait_ge(y_ev, e + 2)
                pool.sem_inc(passed_pool)
                eng.indirect_dma_start(x1_scr, bass.IndirectOffsetOnAxis(ap=idx_scatter, axis=0), y, None,
                                       compute_op=ALU.add).then_inc(scattered, 16)
                pool.wait_ge(scattered, (e + 1) * 16)
            pool.wait_ge(gathered, 16 * (EXP + 1))

        @block.scalar
        def _(act_e):
            sc = nc.scalar
            chain = [0]

            def link(ins):
                chain[0] += 1
                ins.then_inc(ac, 1)
                act_e.wait_ge(ac, chain[0])

            sc.dma_start(cc[:, 0, :], c[0].rearrange("(p k) -> p k", k=KD)).then_inc(ld_const, 16)
            sc.dma_start(cc[:, 1, :], c_ctx.rearrange("(p k) -> p k", k=KD)).then_inc(ld_const, 16)
            sc.dma_start(norm_col[:, 0, :], norm1[0].rearrange("(k p) -> p k", p=P)).then_inc(ld_const, 16)
            sc.dma_start(norm_col[:, 1, :], norm2[0].rearrange("(k p) -> p k", p=P)).then_inc(ld_const, 16)
            for n, w in enumerate((conv_k_w, conv_q_w)):
                for h in range(H):
                    sc.dma_start(conv_w[:, n, h, :], w[0, :, h * DQK:(h + 1) * DQK].rearrange("j p -> p j")).then_inc(ld_const, 16)
            sc.dma_start(headg_col, head_g[0].rearrange("(k p) -> p k", p=P)).then_inc(ld_const, 16)
            sc.dma_start(pscale_col, pool_scale[0].rearrange("(k p) -> p k", p=P)).then_inc(ld_const, 16)
            act_e.wait_ge(ld_const, 16 * 14)
            sc.activation(cc[:, :, :], cc[:, :, :], ACT.Silu).then_inc(silu_c, 1)
            act_e.wait_ge(consts, 2)
            for i in range(NTT):
                act_e.wait_ge(ld_x[i % 2], 16 * (i // 2 + 1))
                link(sc.activation(sig_o.rearrange("p a b -> p (a b)"), xt[:, i % 2, :], ACT.Square, accum_out=ssx[:, i:i + 1]))
                sc.activation(rsx[:, i:i + 1], ssx[:, i:i + 1], ACT.Sqrt, bias=eps, scale=1.0 / D).then_inc(x_stat, 1)
                for q in (0, 2):
                    act_e.wait_ge(x_tr, 4 * i + q + 1)
                    dst = hcT[:, 4 * q:4 * q + 4, i * P:(i + 1) * P] if i < NC else hT[:, 4 * q:4 * q + 4, (i - NC) * P:(i - NC + 1) * P]
                    sc.activation(dst, bank[(4 * i + q) % 8][:, :].rearrange("p (a b) -> p a b", a=4), ACT.Copy).then_inc(x_evA, 1)
            act_e.wait_ge(grow, 1)
            act_e.wait_ge(ld_wg, 16 * 8)
            for n, (lo, w) in enumerate(((0, TC), (TC, BN), (TC + BN, BN))):
                act_e.wait_ge(gate_mm, n + 1)
                pb = bank[n]
                for j, dst in ((0, LI), (2, LF)):
                    f, b = 32 * j, 32 * j + 32
                    sc.activation(dst[0:4, lo:lo + w], pb[f:f + 4, 0:w], ACT.Identity, bias=bg[f:f + 4, :])
                    if lo == 0:
                        rev = dst[32:36, 0:TC][:, ::-1]
                    else:
                        r0 = TC + T - (lo - TC) - w
                        rev = dst[32:36, r0:r0 + w][:, ::-1]
                    last = sc.activation(rev, pb[b:b + 4, 0:w], ACT.Identity, bias=bg[b:b + 4, :])
                last.then_inc(gate_ev, 1)
            act_e.wait_ge(gact, 1)
            link(sc.activation(GT[0:GR], GT[0:GR], ACT.Exp, scale=-1.0))
            sc.activation(GT[0:GR], GT[0:GR], ACT.Ln, bias=one[0:GR, :]).then_inc(gact, 1)
            act_e.wait_ge(gcol_mm, 1)
            sc.activation(EM, bank[1][:, 0:NTT * GR].rearrange("p (a b) -> p a b", a=NTT), ACT.Exp, scale=-1.0).then_inc(gcols, 1)
            act_e.wait_ge(gcols, 4)

            silus = 0
            for item in order:
                if item[0] == "group":
                    g = item[1]
                    kind, h = groups[g][0:2]
                    if kind == "T":
                        continue
                    par = h % 2
                    if kind == "K" and groups[g][2] == 0 and h:
                        act_e.wait_ge(conv_done, 2 * h)
                    if kind == "Q" and groups[g][2] == 0:
                        act_e.wait_ge(conv_done, 2 * h + 1)
                    if kind == "O" and h >= 1 and groups[g][2:] == (0, 0):
                        act_e.wait_ge(mix_st, 16 * h)
                    if kind == "V" and groups[g][2] == 0 and h >= 2:
                        for d in range(2):
                            act_e.wait_ge(stB[d], (h - 1) * NTT)
                    if kind == "P" and groups[g][2:] == (0, 0) and h == 0:
                        act_e.wait_ge(gfree, 1)
                    if kind == "P" and groups[g][-1] == 0 and (h, groups[g][2]) != (0, 0):
                        act_e.wait_ge(pool_d, 2 * h + groups[g][2])
                    if kind == "M" and groups[g][2:] == (0, 0) and h >= 1:
                        act_e.wait_ge(pmix_st, 16 * h)
                    act_e.wait_ge(grp, g + 1)
                    src = PR[g % 2]
                    if kind in "KQ":
                        part = groups[g][2]
                        if kind == "Q":
                            part += 1
                        if part == 0:
                            sc.activation(raw[:, PADC:PADC + TC], src[:, 0:TC], ACT.Copy).then_inc(evA, 1)
                        else:
                            lo = 2 * PADC + TC + (part - 1) * BN
                            sc.activation(raw[:, lo:lo + BN], src[:, :], ACT.Copy).then_inc(evA, 1)
                    elif kind == "V":
                        sc.activation(V[:, par, groups[g][2], 0:DV], src[:, 0:DV], ACT.Copy).then_inc(evA, 1)
                    elif kind == "O":
                        _, _, ft_, half = groups[g]
                        sc.activation(sig_o[:, ft_, half * BN:(half + 1) * BN], src[:, :], ACT.Sigmoid).then_inc(evA, 1)
                    elif kind == "P":
                        half = groups[g][3]
                        rows = ROWS // 2
                        sc.activation(pool_h0[:, half * rows:(half + 1) * rows, PADG:PADG + GRID_W],
                                      src[:, :].rearrange("p (a b) -> p a b", a=rows), ACT.Copy).then_inc(evA, 1)
                    else:
                        _, gg, fo, half = groups[g]
                        sc.activation(pmix[:, fo, half * BN:(half + 1) * BN], src[:, :], ACT.Copy,
                                      scale=pscale_col[:, 2 * gg + fo:2 * gg + fo + 1]).then_inc(evA, 1)
                elif item[0] == "silu":
                    _, h, n = item
                    act_e.wait_ge(conv_done, 2 * h + n + 1)
                    buf = kT[:, h % 2, :] if n == 0 else qT[:, h % 2, :]
                    sc.activation(buf, buf, ACT.Silu).then_inc(silu_done, 1)
                elif item[0] == "A":
                    _, h, j = item
                    for d in range(2):
                        s = h * NTT + j
                        ch, row = chunk_of(d, j), 32 * d + h
                        tl = LAST[d]
                        act_e.wait_ge(stA[d], s + 1)
                        if s:
                            act_e.wait_ge(cup[d], s)
                        pb = A_b[d]
                        a_s, mp = Acol[:, ch, row:row + 1], mp_col[:, 4 * d + h, j:j + 1]
                        if j < NC:
                            sc.activation(Dm[:, d, tl:tl + 1], pb[:, 0:1], ACT.Exp, bias=a_s)
                            sc.activation(WI[:, d, tl:tl + 1], pb[:, 0:1], ACT.Exp, bias=mp).then_inc(expd[d], 1)
                        else:
                            sc.activation(Dm[:, d, :], pb[:, P:2 * P], ACT.Exp, bias=a_s)
                            sc.activation(WI[:, d, :], pb[:, 0:P], ACT.Exp, bias=mp).then_inc(expd[d], 1)
                elif item[0] == "normalise":
                    h = item[1]
                    for d in range(2):
                        act_e.wait_ge(cup[d], (h + 1) * NTT)
                    if h:
                        act_e.wait_ge(hrs, h)
                    for t in range(NT):
                        link(sc.activation(Dm.rearrange("p a b -> p (a b)"), h_sum[:, t, :], ACT.Square, accum_out=ssh[:, t:t + 1]))
                    sc.activation(ssh, ssh, ACT.Sqrt, bias=eps, scale=1.0 / DV).then_inc(hsq, 1)

            def row_stat(i):
                act_e.wait_ge(o_ev, (NB - 1) * NT + i + 1)
                if i == 0:
                    act_e.wait_ge(o_mm, (NB - 1) * NT)
                link(sc.activation(wo[:, 0].rearrange("p a b -> p (a b)")[:, 0:D], x1[:, i, :], ACT.Square, accum_out=ss1[:, i:i + 1]))
                sc.activation(rs1[:, i:i + 1], ss1[:, i:i + 1], ACT.Sqrt, bias=eps, scale=1.0 / D).then_inc(x1_sq, 1)

            row_stat(0)
            for i in range(NT):
                if i < NT - 1:
                    row_stat(i + 1)
                for q in (0, 2):
                    act_e.wait_ge(r_tr, 4 * i + q + 1)
                    if i >= 2:
                        act_e.wait_ge(r_mm, i)
                    sc.activation(xnT[:, i % 2, 4 * q:4 * q + 4, :], bank[q][:, :].rearrange("p (a b) -> p a b", a=4), ACT.Copy).then_inc(r_ev, 1)
            act_e.wait_ge(sm_d, 1)
            sc.activation(L1, L0, ACT.Exp).then_inc(sm_a, 1)

            def xs_copy(n):
                for k in range(8):
                    last = sc.activation(xsT[:, k, :], bank[4 + k // 4][:, (k % 4) * P:(k % 4 + 1) * P], ACT.Identity,
                                         bias=shift2[:, k:k + 1], scale=scale2[:, k:k + 1])
                last.then_inc(xs_evA, 1)

            act_e.wait_ge(xs_mm, 1)
            xs_copy(0)
            with act_e.Fori(0, EXP) as e:
                act_e.wait_ge(e_used, e * 12 + 4)
                for n in range(2):
                    last = sc.activation(act[:, n * BN:(n + 1) * BN], bank[n][:, :], ACT.Silu)
                last.then_inc(g_act, 1)
                act_e.wait_ge(xs_mm, e + 2)
                xs_copy(1)
                act_e.wait_ge(a_mm, e + 1)
                last = sc.activation(actT[:, 0:4, :], bank[0][:, :].rearrange("p (a b) -> p a b", a=4), ACT.Copy)
                last.then_inc(a_ev, 1)
            for i in range(NT):
                act_e.wait_ge(ld_f[i], 16)
                link(sc.activation(view(top, D), ft[i], ACT.Square, accum_out=ssf[:, i:i + 1]))
                sc.activation(rsf[:, i:i + 1], ssf[:, i:i + 1], ACT.Sqrt, bias=eps, scale=1.0 / D).then_inc(f_sq, 1)

        @block.tensor
        def _(pe):
            te = nc.tensor
            pe.wait_ge(consts, 2)
            for i in range(NTT):
                pe.wait_ge(x_scaled, i + 1)
                for q in range(4):
                    n = 4 * i + q
                    if n >= 8:
                        pe.wait_ge(x_evD if q % 2 else x_evA, 2 * (i - 2) + q // 2 + 1)
                    for k in range(4):
                        last = te.transpose(bank[n % 8][:, k * P:(k + 1) * P], xt[:, i % 2, (4 * q + k) * P:(4 * q + k + 1) * P], ident)
                    last.then_inc(x_tr, 1)
            pe.wait_ge(silu_c, 1)
            pe.wait_ge(x_evA, 2 * NTT)
            pe.wait_ge(x_evD, 2 * NTT)
            with pe.Fori(0, NMOD // 2) as m2:
                for m in range(2):
                    pe.wait_ge(mod_free, m2 * 2 + m + 1)
                    for k in range(KD):
                        pe.wait_ge(ld_mod[k % 4], (m2 * 2 + m) * (16 * KD // 4) + 16 * (k // 4 + 1))
                        for n in range(NB):
                            last = te.matmul(bank[4 * m + n][0:2, :], cc[:, :, k], mod_ring[:, k % 4, n * BN:(n + 1) * BN],
                                             start=(k == 0), stop=(k == KD - 1))
                        last.then_inc(mod_used, 1)
            pe.wait_ge(h_ready, 1)
            pe.wait_ge(mod_sum, NMOD)
            pe.wait_ge(ld_wg, 16 * 8)
            for n, w in enumerate((TC, BN, BN)):
                for k in range(KD):
                    rhs = hcT[:, k, :] if n == 0 else hT[:, k, (n - 1) * BN:n * BN]
                    last = te.matmul(bank[n][0:100, 0:w], wg[:, k, :], rhs, start=(k == 0), stop=(k == KD - 1))
                last.then_inc(gate_mm, 1)
            pe.wait_ge(gate_ev, 3)
            pe.wait_ge(grow, 2)
            for j in range(NTT):
                te.transpose(bank[0][:, j * GR:(j + 1) * GR], GX[0:GR, j * P:(j + 1) * P], ident[0:GR, 0:GR])
                te.transpose(bank[1][:, j * GR:(j + 1) * GR], LF[0:GR, j * P:(j + 1) * P], ident[0:GR, 0:GR])
            for r in range(8):
                last = te.matmul(bank[2][:, r * NTT:(r + 1) * NTT], sel[0:GR, r, :], mpr[0:GR, 0:NTT], start=True, stop=True)
            last.then_inc(gcol_mm, 1)
            pe.wait_ge(gcols, 4)

            for item in order:
                if item[0] == "group":
                    g = item[1]
                    kind, h = groups[g][0:2]
                    par = h % 2
                    if g >= 2:
                        dve, count = evac[g - 2]
                        pe.wait_ge(evD if dve else evA, count)
                    dst = PR[g % 2]
                    if kind in slot_of:
                        s = slot_no[(slot_of[kind], h)]
                        pe.wait_ge(ld_w[s % 2], 32 * (s // 2 + 1))
                        w = ring[:, s % 2]
                    if kind in "KQ":
                        part = groups[g][2] + (kind == "Q")
                        c0 = DQK * (kind == "Q")
                        width = TC if part == 0 else BN
                        for k in range(KD):
                            rhs = hcT[:, k, :] if part == 0 else hT[:, k, (part - 1) * BN:part * BN]
                            last = te.matmul(dst[:, 0:width], w[:, k, c0:c0 + DQK], rhs, start=(k == 0), stop=(k == KD - 1))
                    elif kind == "V":
                        t = groups[g][2]
                        for k in range(KD):
                            lhs = hcT[:, k, t * P:(t + 1) * P] if t < NC else hT[:, k, (t - NC) * P:(t - NC + 1) * P]
                            last = te.matmul(dst[:, 0:DV], lhs, w[:, k, :], start=(k == 0), stop=(k == KD - 1))
                    elif kind in "OP":
                        _, _, a, half = groups[g]
                        for k in range(KD):
                            last = te.matmul(dst[:, :], w[:, k, a * P:(a + 1) * P], hT[:, k, half * BN:(half + 1) * BN],
                                             start=(k == 0), stop=(k == KD - 1))
                    elif kind == "T":
                        _, _, a, half = groups[g]
                        pe.wait_ge(hnorm, h + 1)
                        for t in range(4):
                            last = te.transpose(dst[:, t * P:(t + 1) * P], h_sum[:, 4 * half + t, a * P:(a + 1) * P], ident)
                    else:
                        _, gg, fo, half = groups[g]
                        pe.wait_ge(pool_d, 2 * gg + 2)
                        pe.wait_ge(ld_pool, 32 * (gg + 1))
                        for a in range(2):
                            last = te.matmul(dst[:, :], poolw[:, a, fo * P:(fo + 1) * P], dT[a][:, half * BN:(half + 1) * BN],
                                             start=(a == 0), stop=(a == 1))
                    last.then_inc(grp, 1)
                elif item[0] == "A":
                    _, h, j = item
                    par, s = h % 2, h * NTT + j
                    for d in range(2):
                        ch, tl, pb = chunk_of(d, j), LAST[d], A_b[d]
                        if s:
                            pe.wait_ge(fac[d], s)
                        if j == 0:
                            pe.wait_ge(silu_done, 2 * h + 2)
                        selr = sel[0:GR, 4 * d + h, :]
                        k0 = ch * P if ch < NC else LAT0 + (ch - NC) * P
                        kc = kT[:, par, k0:k0 + P]
                        if j < NC:
                            te.matmul(pb[:, 0:1], selr, MxN[0:GR, ch * P + tl:ch * P + tl + 1], start=True, stop=True)
                        else:
                            mx = MxN[0:GR, ch * P:(ch + 1) * P]
                            te.matmul(pb[:, 0:P], selr, mx, start=True, stop=True)
                            te.matmul(pb[:, P:2 * P], selr, mx, start=True, stop=False)
                            te.matmul(pb[:, P:2 * P], ident, mask[:, d], start=False, stop=True)
                            last = te.matmul(pb[:, 2 * P:3 * P], kc, qT[:, par, (ch - NC) * P:(ch - NC + 1) * P], start=True, stop=True)
                        if j < NTT - 1:
                            last = te.transpose(pb[:, 3 * P:4 * P], kc, ident)
                        last.then_inc(stA[d], 1)
                elif item[0] == "B":
                    _, h, j = item
                    par, s = h % 2, h * NTT + j
                    if j == 0:
                        pe.wait_ge(evA, evac[group_no[("V", h, NTT - 1)]][1])
                    for d in range(2):
                        ch = chunk_of(d, j)
                        pe.wait_ge(fac[d], s + 1)
                        if s:
                            pe.wait_ge(cup[d], s)
                        v = V[:, par, ch, :]
                        if j >= NC:
                            te.matmul(N_b[d][:, 0:DV + 1], Pm[:, d, :], v, start=True, stop=False)
                            last = te.matmul(N_b[d][:, 0:DV + 1], qw[:, d, :], C[:, d, j % 2, :], start=False, stop=True)
                        if j < NTT - 1:
                            last = te.matmul(C_b[d][:, 0:DV + 1], kw[:, d, :], v, start=True, stop=True)
                        last.then_inc(stB[d], 1)

            pe.wait_ge(ld_mix, 32)
            for n in range(NB):
                pe.wait_ge(ld_wo[n % 2], 16 * (n // 2 + 1))
                for i in range(NT):
                    g = n * NT + i
                    if g >= 8:
                        pe.wait_ge(o_ev, g - 7)
                    elif g == 0:
                        pe.wait_ge(evA, counts[0])
                        pe.wait_ge(evD, counts[1])
                    for k in range(KD):
                        last = te.matmul(bank[g % 8][:, :], mixT[:, k, i * P:(i + 1) * P], wo[:, n % 2, k, :],
                                         start=(k == 0), stop=(k == KD - 1))
                    last.then_inc(o_mm, 1)
            pe.wait_ge(o_ev, NB * NT)
            pe.wait_ge(wr_s, 1)
            for k in range(KD):
                last = te.matmul(bank[5][0:1, 0:EXP], shift2[:, k:k + 1], wr[:, k, :], start=(k == 0), stop=(k == KD - 1))
            last.then_inc(r_mm, 1)
            for i in range(NT):
                pe.wait_ge(x1_n, i + 1)
                for q in range(4):
                    if i:
                        pe.wait_ge(rt_ev if q % 2 else r_ev, 2 * (i - 1) + q // 2 + 1)
                    for k in range(4):
                        last = te.transpose(bank[q][:, k * P:(k + 1) * P], x1[:, i, (4 * q + k) * P:(4 * q + k + 1) * P], ident)
                    last.then_inc(r_tr, 1)
                pe.wait_ge(r_ev, 2 * i + 2)
                pe.wait_ge(rt_ev, 2 * i + 2)
                if i == 0:
                    pe.wait_ge(r_log, 1)
                for k in range(KD):
                    te.matmul(bank[4][:, i * EXP:(i + 1) * EXP], xnT[:, i % 2, k, :], wrs[:, k, :], start=(k == 0), stop=False)
                te.matmul(bank[4][:, i * EXP:(i + 1) * EXP], ones_row[0:1, :], lb[0:1, :], start=False, stop=True).then_inc(r_mm, 1)
            pe.wait_ge(sm_d, 2)
            for i in range(NT):
                last = te.transpose(bank[i // 4][0:EXP, (i % 4) * P:(i % 4 + 1) * P], L0[:, i, :], ident)
            last.then_inc(aff_mm, 1)
            pe.wait_ge(topk, 1)
            te.transpose(bank[2][:, 0:EXP], top_f[0:EXP, :], ident[0:EXP, 0:EXP])
            te.transpose(bank[2][:, EXP:2 * EXP], top_v[0:EXP, :], ident[0:EXP, 0:EXP]).then_inc(topk_mm, 1)

            def transpose_xs():
                for k in range(KD):
                    last = te.transpose(bank[4 + k // 4][:, (k % 4) * P:(k % 4 + 1) * P], xs[:, k * P:(k + 1) * P], ident)
                last.then_inc(xs_mm, 1)

            pe.wait_ge(topk_ev, 1)
            pe.wait_ge(gathered, 16)
            transpose_xs()
            with pe.Fori(0, EXP) as e:
                pe.wait_ge(xs_evA, e + 1)
                pe.wait_ge(xs_evD, e + 1)
                for half in range(2):
                    for k in range(KD):
                        i = 4 * half + k // 4
                        if k % 4 == 0:
                            pe.wait_ge(ld_e[i % ESL], e * 32 + 16 * (i // ESL + 1))
                        for n in range(2):
                            last = te.matmul(bank[2 * half + n][:, :], xsT[:, k, :], ering[i % ESL][:, k % 4, n * BN:(n + 1) * BN],
                                             start=(k == 0), stop=(k == KD - 1))
                        if k % 4 == 3:
                            last.then_inc(e_used, 1)
                pe.wait_ge(gathered, e * 16 + 32)
                pe.wait_ge(y_ev, e + 1)
                transpose_xs()
                pe.wait_ge(a_rdy, e + 1)
                for k in range(KF):
                    last = te.transpose(bank[k // 4][:, (k % 4) * P:(k % 4 + 1) * P], act[:, k * P:(k + 1) * P], ident)
                last.then_inc(a_mm, 1)
                pe.wait_ge(a_ev, e * 2 + 2)
                pe.wait_ge(xs_evA, e + 2)
                pe.wait_ge(xs_evD, e + 2)
                for k in range(KF):
                    i = 8 + k // 2
                    if k % 2 == 0:
                        pe.wait_ge(ld_e[i % ESL], e * 32 + 32)
                    wd = ering[i % ESL].rearrange("p a b -> p (a b)").rearrange("p (a b) -> p a b", a=2)
                    for n in range(NB):
                        last = te.matmul(bank[4 + n][:, :], actT[:, k, :], wd[:, k % 2, n * BN:(n + 1) * BN],
                                         start=(k == 0), stop=(k == KF - 1))
                    if k % 2 == 1:
                        last.then_inc(e_used, 1)

        @block.vector
        def _(dve):
            ve = nc.vector
            chain = [0]

            def link(ins):
                chain[0] += 1
                ins.then_inc(dv, 1)
                dve.wait_ge(dv, chain[0])

            dve.wait_ge(consts, 2)
            for i in range(NTT):
                dve.wait_ge(x_stat, i + 1)
                link(ve.reciprocal(rsx[:, i:i + 1], rsx[:, i:i + 1]))
                ve.tensor_scalar(xt[:, i % 2, :], xt[:, i % 2, :], rsx[:, i:i + 1], None, ALU.mult).then_inc(x_scaled, 1)
                for q in (1, 3):
                    dve.wait_ge(x_tr, 4 * i + q + 1)
                    dst = hcT[:, 4 * q:4 * q + 4, i * P:(i + 1) * P] if i < NC else hT[:, 4 * q:4 * q + 4, (i - NC) * P:(i - NC + 1) * P]
                    ve.tensor_copy(dst, bank[(4 * i + q) % 8][:, :].rearrange("p (a b) -> p a b", a=4)).then_inc(x_evD, 1)
            ve.memset(reset[0:GR], 1.0).then_inc(mod_free, 2)
            for m in range(NMOD):
                dve.wait_ge(ld_bmod[m % 2], 16 * (m // 2 + 1))
                dve.wait_ge(mod_used, KD * (m + 1))
                rows = mod_row[0:2, m % 2, :]
                for n in range(NB):
                    last = ve.tensor_tensor(rows[:, n * BN:(n + 1) * BN], bank[4 * (m % 2) + n][0:2, :],
                                            rows[:, n * BN:(n + 1) * BN], ALU.add)
                last.then_inc(mod_sum, 1)
                dve.wait_ge(mod_sum, m + 1)
                ve.memset(small[:, 120:121], 0.0).then_inc(mod_free, 1)
                if m == 1:
                    dve.wait_ge(ld_cols, 64)
                    dve.wait_ge(ld_const, 16 * 14)
                    for r in range(2):
                        last = ve.scalar_tensor_tensor(scale1[:, r, :], scale1[:, r, :], 1.0, norm_col[:, 0, :], ALU.add, ALU.mult)
                    link(last)
                    dve.wait_ge(x_evA, 2 * NTT)
                    for k in range(KD):
                        ve.tensor_scalar(hT[:, k, :], hT[:, k, :], scale1[:, 0, k:k + 1], shift1[:, 0, k:k + 1], ALU.mult, ALU.add)
                        last = ve.tensor_scalar(hcT[:, k, :], hcT[:, k, :], scale1[:, 1, k:k + 1], shift1[:, 1, k:k + 1], ALU.mult, ALU.add)
                    last.then_inc(h_ready, 1)
            dve.wait_ge(mod_st[0], 16 * (NMOD // 2))
            dve.wait_ge(mod_st[1], 16 * (NMOD // 2))
            ve.memset(LI[0:GR], 0.0)
            ve.memset(MxN[0:GR], 0.0)
            ve.memset(reset[0:GR].rearrange("p (a b) -> p a b", b=P)[:, :, 0:1], 0.0)
            ve.memset(LF[0:GR], 0.0).then_inc(grow, 1)
            dve.wait_ge(gate_ev, 3)
            ve.scalar_tensor_tensor(GT[0:GR], LF[0:GR], -1.0, LF[0:GR], ALU.mult, ALU.max).then_inc(gact, 1)
            dve.wait_ge(gact, 2)
            link(ve.scalar_tensor_tensor(LF[0:GR], LF[0:GR], 0.0, GT[0:GR], ALU.min, ALU.subtract))
            link(ve.tensor_tensor_scan(GB[0:GR], reset[0:GR], LF[0:GR], 0.0, ALU.mult, ALU.add))
            link(ve.tensor_tensor(GA[0:GR], LI[0:GR], GB[0:GR], ALU.subtract))
            for j in range(NTT):
                cs = slice(j * P, (j + 1) * P)
                e = (j + 1) * P - 1
                link(ve.tensor_tensor_scan(GX[0:GR, cs], GA[0:GR, cs], GA[0:GR, cs], mpr[0:GR, j:j + 1], ALU.max, ALU.max))
                link(ve.tensor_tensor(mpr[0:GR, j + 1:j + 2], GB[0:GR, e:e + 1], GX[0:GR, e:e + 1], ALU.add))
            link(ve.tensor_tensor(LI[0:GR], GB[0:GR], GX[0:GR], ALU.add))

            def natural(dst, src):
                ve.tensor_copy(dst[0:4, 0:NTT * P], src[0:4, 0:NTT * P])
                ve.tensor_copy(dst[32:36, 0:TC], src[32:36, 0:TC][:, ::-1])
                return ve.tensor_copy(dst[32:36, TC:TC + T], src[32:36, TC:TC + T][:, ::-1])

            link(natural(MxN, GX))
            natural(GX, GA)
            natural(LF, LI).then_inc(grow, 1)
            dve.wait_ge(gcol_mm, 1)
            ve.tensor_copy(Acol, bank[0][:, 0:NTT * GR].rearrange("p (a b) -> p a b", a=NTT)).then_inc(gcols, 1)
            ve.tensor_scalar(mp_col, bank[2][:, 0:8 * NTT].rearrange("p (a b) -> p a b", a=8), -1.0, None, ALU.mult).then_inc(gcols, 1)
            ve.memset(V.rearrange("p a b c -> p (a b) c")[:, :, DV:DV + 1], 1.0)
            ve.memset(raw[:, 0:PADC], 0.0)
            ve.memset(raw[:, PADC + TC:2 * PADC + TC], 0.0)
            ve.memset(raw[:, RAWN - PADC:RAWN], 0.0).then_inc(gcols, 1)

            def pooling(g, a):
                L = g + 1

                def stages(src, bufs, axis, dst, size):
                    lo, hi = 0, size
                    cur = src
                    for k in range(L):
                        back, ahead = (1, 0) if k == 0 else (1 << (k - 1), 1 << (k - 1))
                        lo, hi = lo + back, hi - ahead
                        if k == L - 1:
                            lo, hi, nxt = PADG, size - PADG, dst
                        else:
                            nxt = bufs[k % 2]
                        if axis == 1:
                            target = nxt if k == L - 1 else nxt[:, :, lo:hi]
                            link(ve.tensor_tensor(target, cur[:, :, lo - back:hi - back], cur[:, :, lo + ahead:hi + ahead], ALU.add))
                        else:
                            target = nxt if k == L - 1 else nxt[:, lo:hi, :]
                            link(ve.tensor_tensor(target, cur[:, lo - back:hi - back, :], cur[:, lo + ahead:hi + ahead, :], ALU.add))
                        cur = nxt

                wide = pool_v[1].rearrange("p a b -> p (a b)")[:, 0:ROWS * HW_].rearrange("p (a b) -> p a b", a=ROWS)
                stages(pool_h0, [pool_h1, wide], 1, pool_v[0][:, PADG:PADG + ROWS, :], HW_)
                box = pool_h1.rearrange("p a b -> p (a b)")[:, 0:T].rearrange("p (a b) -> p a b", a=ROWS)
                stages(pool_v[0], [pool_v[1], pool_v[0]], 0, box, HR)
                if L >= 3:
                    ve.memset(pool_v[0][:, 0:PADG, :], 0.0)
                    ve.memset(pool_v[0][:, PADG + ROWS:, :], 0.0)
                dve.wait_ge(ld_pool, 32 * (g + 1))
                link(ve.tensor_tensor(box, box, inv_b.rearrange("p (a b) -> p a b", a=ROWS), ALU.mult))
                if g:
                    dve.wait_ge(grp, group_no[("M", g - 1, 1, 1)] + 1)
                ve.tensor_tensor(dT[a].rearrange("p (a b) -> p a b", a=ROWS), box,
                                 pool_h0[:, :, PADG:PADG + GRID_W], ALU.subtract).then_inc(pool_d, 1)

            for item in order:
                if item[0] == "group" and groups[item[1]][0] == "T":
                    g = item[1]
                    _, h, a, half = groups[g]
                    dve.wait_ge(evA, evac[group_no[("O", h, 1, 1)]][1])
                    dve.wait_ge(grp, g + 1)
                    so = sig_o[:, a, half * BN:(half + 1) * BN]
                    ve.scalar_tensor_tensor(so, PR[g % 2][:, :], headg_col[:, 2 * h + a:2 * h + a + 1], so, ALU.mult, ALU.mult).then_inc(evD, 1)
                elif item[0] == "conv":
                    _, h, n = item
                    dve.wait_ge(evA, evac[group_no[("K", h, 2) if n == 0 else ("Q", h, 1)]][1])
                    acc = kT[:, h % 2, :] if n == 0 else qT[:, h % 2, :]
                    lo, w = (0, CONVN) if n == 0 else (LAT0, T)
                    tap = conv_w[:, n, h, :]
                    link(ve.tensor_scalar(acc, raw[:, lo:lo + w], tap[:, 0:1], None, ALU.mult))
                    for j in range(1, TAPS):
                        ins = ve.scalar_tensor_tensor(acc, raw[:, lo + j:lo + j + w], tap[:, j:j + 1], acc, ALU.mult, ALU.add)
                        if j < TAPS - 1:
                            link(ins)
                    ins.then_inc(conv_done, 1)
                elif item[0] == "A":
                    _, h, j = item
                    par, s = h % 2, h * NTT + j
                    for d in range(2):
                        ch, tl, pb = chunk_of(d, j), LAST[d], A_b[d]
                        dve.wait_ge(expd[d], s + 1)
                        if s:
                            dve.wait_ge(stB[d], s)
                        if j >= NC:
                            ve.scalar_tensor_tensor(Pm[:, d, :], pb[:, 2 * P:3 * P], KSCALE, Dm[:, d, :], ALU.mult, ALU.mult)
                            last = ve.tensor_tensor(qw[:, d, :], qT[:, par, (ch - NC) * P:(ch - NC + 1) * P], WI[:, d, :], ALU.mult)
                        if j < NTT - 1:
                            last = ve.tensor_scalar(kw[:, d, :], pb[:, 3 * P:4 * P], Dm[:, d, tl:tl + 1], KSCALE, ALU.mult, ALU.mult)
                        last.then_inc(fac[d], 1)
                elif item[0] == "B":
                    _, h, j = item
                    s = h * NTT + j
                    for d in range(2):
                        ch, tl, row = chunk_of(d, j), LAST[d], 32 * d + h
                        dve.wait_ge(stB[d], s + 1)
                        if j < NTT - 1:
                            new, old = C[:, d, (j + 1) % 2, :], C[:, d, j % 2, :]
                            if j == 0:
                                last = ve.tensor_copy(new, C_b[d][:, 0:DV + 1])
                            else:
                                last = ve.scalar_tensor_tensor(new, old, WI[:, d, tl:tl + 1], C_b[d][:, 0:DV + 1], ALU.mult, ALU.add)
                        if j >= NC:
                            num, dcol = N_b[d], den[:, d:d + 1]
                            link(ve.tensor_scalar(dcol, num[:, DV:DV + 1], -1.0, EM[:, ch, row:row + 1], ALU.mult, ALU.max))
                            link(ve.tensor_tensor(dcol, num[:, DV:DV + 1], dcol, ALU.max))
                            link(ve.reciprocal(dcol, dcol))
                            hs = h_sum[:, ch - NC, :]
                            first = j < (NTT - 1 - ch + NC if d == 0 else ch)
                            if first:
                                last = ve.tensor_scalar(hs, num[:, 0:DV], dcol, None, ALU.mult)
                            else:
                                last = ve.scalar_tensor_tensor(hs, num[:, 0:DV], dcol, hs, ALU.mult, ALU.add)
                        last.then_inc(cup[d], 1)
                        dve.wait_ge(cup[d], s + 1)
                elif item[0] == "normalise":
                    h = item[1]
                    dve.wait_ge(hsq, h + 1)
                    ve.reciprocal(rsh, ssh).then_inc(hrs, 1)
                    dve.wait_ge(hrs, h + 1)
                    for t in range(NT):
                        last = ve.tensor_scalar(h_sum[:, t, :], h_sum[:, t, :], rsh[:, t:t + 1], None, ALU.mult)
                    last.then_inc(hnorm, 1)
                    if h == H - 2:
                        dve.wait_ge(grp, group_no[("V", H - 1, NC - 1)] + 1)
                        ve.memset(pool_v[0], 0.0)
                        ve.memset(pool_h0, 0.0).then_inc(gfree, 1)
                        dve.wait_ge(gfree, 1)
                elif item[0] == "pool":
                    _, g, a = item
                    dve.wait_ge(evA, evac[group_no[("P", g, a, 1)]][1])
                    pooling(g, a)

            dve.wait_ge(ld_x1, 16)
            dve.wait_ge(ld_g1, 16)
            for n in range(NB):
                for i in range(NT):
                    g = n * NT + i
                    dve.wait_ge(o_mm, g + 1)
                    link(ve.tensor_tensor(tmp[:, g % 2, :], bank[g % 8][:, :], gate1_b[:, n * BN:(n + 1) * BN], ALU.mult))
                    xb = x1[:, i, n * BN:(n + 1) * BN]
                    ve.tensor_tensor(xb, xb, tmp[:, g % 2, :], ALU.add).then_inc(o_ev, 1)
            dve.wait_ge(ld_r, 16)
            dve.wait_ge(ld_cols, 96)
            link(ve.scalar_tensor_tensor(scale2, scale2, 1.0, norm_col[:, 1, :], ALU.add, ALU.mult))
            for k in range(KD):
                last = ve.tensor_scalar(wrs[:, k, :], wr[:, k, :], scale2[:, k:k + 1], None, ALU.mult)
            last.then_inc(wr_s, 1)
            dve.wait_ge(r_mm, 1)
            ve.tensor_copy(lb[0:1, :], bank[5][0:1, 0:EXP]).then_inc(r_log, 1)
            for i in range(NT):
                dve.wait_ge(x1_sq, i + 1)
                link(ve.reciprocal(rs1[:, i:i + 1], rs1[:, i:i + 1]))
                dve.wait_ge(x1_st, 16 * (i + 1))
                ve.tensor_scalar(x1[:, i, :], x1[:, i, :], rs1[:, i:i + 1], None, ALU.mult).then_inc(x1_n, 1)
                for q in (1, 3):
                    dve.wait_ge(r_tr, 4 * i + q + 1)
                    if i >= 2:
                        dve.wait_ge(r_mm, i)
                    ve.tensor_copy(xnT[:, i % 2, 4 * q:4 * q + 4, :], bank[q][:, :].rearrange("p (a b) -> p a b", a=4)).then_inc(rt_ev, 1)
            dve.wait_ge(r_mm, NT + 1)
            logits = bank[4][:, 0:NT * EXP].rearrange("p (a b) -> p a b", a=NT)
            link(ve.tensor_reduce(lst[:, 0, :], logits, AX.X, ALU.max))
            ve.tensor_tensor(L0, logits, lst[:, 0, :].unsqueeze(2).to_broadcast([P, NT, EXP]), ALU.subtract).then_inc(sm_d, 1)
            dve.wait_ge(sm_a, 1)
            link(ve.tensor_reduce(lst[:, 1, :], L1, AX.X, ALU.add))
            link(ve.reciprocal(lst[:, 1, :], lst[:, 1, :]))
            ve.tensor_tensor(L0, L1, lst[:, 1, :].unsqueeze(2).to_broadcast([P, NT, EXP]), ALU.mult).then_inc(sm_d, 1)
            dve.wait_ge(aff_mm, 1)
            for n in range(2):
                last = ve.tensor_copy(aff[0:EXP, n * BN:(n + 1) * BN], bank[n][0:EXP, :])
            link(last)
            for r in range(CAP // 8):
                best, at8 = top_v[0:EXP, 8 * r:8 * r + 8], top_i[0:EXP, 8 * r:8 * r + 8]
                link(ve.max(best, aff[0:EXP, :]))
                ve.max_index(at8, best, aff[0:EXP, :])
                if r < CAP // 8 - 1:
                    link(ve.match_replace(aff[0:EXP, :], best, aff[0:EXP, :], -1.0))
            link(ve.memset(small[:, 121:122], 0.0))
            ve.tensor_copy(top_f[0:EXP, :], top_i[0:EXP, :]).then_inc(topk, 1)
            dve.wait_ge(topk_mm, 1)
            ve.tensor_copy(idx_all[:, 0:EXP], bank[2][:, 0:EXP])
            ve.tensor_copy(idx_all[:, EXP:EXP + 1], bank[2][:, 0:1])
            ve.tensor_copy(gate_all[:, 0:EXP], bank[2][:, EXP:2 * EXP])
            link(ve.tensor_copy(gate_all[:, EXP:EXP + 1], bank[2][:, EXP:EXP + 1]))
            ve.tensor_copy(idx_scatter, idx_all[:, 0:1])
            ve.tensor_copy(gate_now, gate_all[:, 0:1]).then_inc(topk_ev, 1)
            ve.tensor_copy(idx_gather, idx_all[:, 0:1]).then_inc(idx_r, 1)

            def xs_copy():
                for k in range(8, KD):
                    last = ve.tensor_scalar(xsT[:, k, :], bank[4 + k // 4][:, (k % 4) * P:(k % 4 + 1) * P],
                                            scale2[:, k:k + 1], shift2[:, k:k + 1], ALU.mult, ALU.add)
                last.then_inc(xs_evD, 1)

            dve.wait_ge(xs_mm, 1)
            xs_copy()
            dve.wait_ge(ld_g2, 16)
            ve.memset(small[:, 122:123], 0.0).then_inc(y_ev, 1)
            with dve.Fori(0, EXP) as e:
                dve.wait_ge(gathered, e * 16 + 16)
                ve.memset(small[:, 123:124], 0.0)
                ve.tensor_copy(idx_gather, idx_all[:, bass.ds(e + 1, 1)]).then_inc(idx_r, 1)
                dve.wait_ge(g_act, e + 1)
                dve.wait_ge(e_used, e * 12 + 8)
                for n in range(2):
                    a_half = act[:, n * BN:(n + 1) * BN]
                    last = ve.tensor_tensor(a_half, a_half, bank[2 + n][:, :], ALU.mult)
                last.then_inc(a_rdy, 1)
                dve.wait_ge(xs_mm, e + 2)
                xs_copy()
                dve.wait_ge(a_mm, e + 1)
                ve.tensor_copy(actT[:, 4:8, :], bank[1][:, :].rearrange("p (a b) -> p a b", a=4)).then_inc(a_ev, 1)
                dve.wait_ge(e_used, e * 12 + 12)
                for n in range(NB):
                    last = ve.scalar_tensor_tensor(y[:, n * BN:(n + 1) * BN], bank[4 + n][:, :], gate_now,
                                                   gate2_b[:, n * BN:(n + 1) * BN], ALU.mult, ALU.mult)
                last.then_inc(y_ev, 1)
                dve.wait_ge(scattered, e * 16 + 16)
                ve.memset(small[:, 123:124], 0.0)
                ve.tensor_copy(idx_scatter, idx_all[:, bass.ds(e + 1, 1)])
                ve.tensor_copy(gate_now, gate_all[:, bass.ds(e + 1, 1)]).then_inc(cols_set, 1)
                dve.wait_ge(cols_set, e + 1)
            dve.wait_ge(ld_nf, 16)
            for i in range(NT):
                dve.wait_ge(f_sq, i + 1)
                link(ve.reciprocal(rsf[:, i:i + 1], rsf[:, i:i + 1]))
                ve.scalar_tensor_tensor(ft[i], ft[i], rsf[:, i:i + 1], normf_b, ALU.mult, ALU.mult).then_inc(f_out, 1)


def inverse_counts():
    import numpy as np
    grid_w, rows = 64, 16
    out = np.zeros((4, rows * grid_w), np.float32)
    for g, w in enumerate((2, 4, 8, 16)):
        def count(n):
            t = np.arange(n)
            return np.minimum(t + w // 2, n) - np.maximum(t - w // 2, 0)
        out[g] = (1.0 / (count(rows)[:, None] * count(grid_w)[None, :])).reshape(-1)
    return out


_INS = ["x", "c", "ctx", "c_ctx", "w_mod", "b_mod", "norm1", "w_in", "conv_q_w", "conv_k_w", "b_gates", "head_g",
        "pool_w", "pool_scale", "w_out", "norm2", "w_router", "w_gate", "w_up", "w_down", "norm_f"]


def kernel(**inputs):
    import numpy as _np
    import concourse.bacc as _bacc
    from concourse import mybir as _mybir
    from concourse.bass_utils import run_bass_kernel_spmd as _run

    nc = _bacc.Bacc("TRN2", target_bir_lowering=False, num_devices=1)
    arrays, args = {}, []
    for name in _INS + ["inv_count"]:
        a = inverse_counts() if name == "inv_count" else _np.ascontiguousarray(inputs[name])
        arrays[f"in_{name}_dram"] = a
        args.append(nc.dram_tensor(f"in_{name}_dram", a.shape, _mybir.dt.from_np(a.dtype), kind="ExternalInput").ap())
    shape = inputs["x"].shape
    args.append(nc.dram_tensor("out_0_dram", shape, _mybir.dt.float32, kind="ExternalOutput").ap())
    hybrid_layer_kernel(nc, *args)
    r = _run(nc, [arrays], core_ids=[0])
    return r.results[0]["out_0_dram"]
```

```python
import concourse.bass as bass
from concourse import mybir
from contextlib import ExitStack


def hybrid_layer_kernel(nc, x, c, ctx, c_ctx, w_mod, b_mod, norm1, w_in, conv_q_w, conv_k_w, b_gates,
                        head_g, pool_w, pool_scale, w_out, norm2, w_router, w_gate, w_up, w_down, norm_f,
                        inv_count, out):
    fp32, fp32r, u32 = mybir.dt.float32, mybir.dt.float32r, mybir.dt.uint32
    ALU, ACT, AX = mybir.AluOpType, mybir.ActivationFunctionType, mybir.AxisListType

    P = 128
    T, D = x.shape[1], x.shape[2]
    TC = ctx.shape[1]
    KD = D // P
    NT, NC = T // P, TC // P
    NTT = NT + NC
    H = 4
    DV, DQK = 256, 128
    MW = H * DV
    PW = D - MW
    NG = 4
    GC = PW // NG
    GRID_W = 64
    ROWS = T // GRID_W
    WINDOWS = (2, 4, 8, 16)
    K_OFF, V_OFF = 0, H * DQK
    G_OFF = V_OFF + MW
    Q_OFF = G_OFF + 16
    O_OFF = Q_OFF + H * DQK
    P_OFF = O_OFF + MW
    TAPS = 5
    NMOD = 6
    EXP = w_router.shape[2]
    CAP = 2 * T // EXP
    F = w_gate.shape[3]
    KF = F // P
    EPS = 1e-6
    KSCALE = float(DQK) ** -0.5
    NEG = -1e30
    BN = 512
    NB = D // BN
    OSL, MSL, OUL = 3, 2, 4
    ESL, USL = 8, 8

    PADC = 2
    RAWN = 3 * PADC + TC + T
    CONVN = RAWN - 2 * PADC
    LAT0 = TC + PADC
    GR = 36
    LAST = (P - 1, 0)

    def chunk_of(d, j):
        if d == 0:
            return j
        return NC - 1 - j if j < NC else NTT - 1 - (j - NC)

    MOD_PER_TILE = -(-2 * KD // NTT)

    def mod_pieces(i):
        return range(min(MOD_PER_TILE * i, 2 * KD), min(MOD_PER_TILE * (i + 1), 2 * KD))

    MACP = KD // 2
    MACS = (NMOD - 2) * NB * MACP
    groups, order, summed, macs = [], [], [], [0]

    def add_group(kind, *what):
        groups.append((kind, *what))
        order.append(("group", len(groups) - 1))
        if kind in ("T", "M"):
            return
        if summed:
            groups.append(("R", summed.pop()))
            order.append(("group", len(groups) - 1))
        for _ in range(2):
            if macs[0] < MACS and not summed:
                order.append(("mac", macs[0]))
                macs[0] += 1
                if macs[0] % MACP == 0:
                    summed.append(macs[0] // MACP - 1)

    def add_step(h, i):
        if i >= 1 and i <= NTT:
            order.append(("B", h, i - 1))
        if i < NTT:
            order.append(("A", h, i))

    def after_group(h, i):
        if h < 0:
            return
        if i <= NTT:
            add_step(h, i)
        if i == NTT + 1:
            order.append(("normalise", h))
        if i == NTT + 3:
            for ft in range(2):
                for half in range(2):
                    add_group("T", h, ft, half)
            order.append(("store_mix", h))

    for h in range(H):
        i = 0
        for what in [("K", h, 0), ("K", h, 1), ("K", h, 2), ("Q", h, 0), ("Q", h, 1)] \
                + [("V", h, t) for t in range(NTT)] + [("O", h, ft, half) for ft in range(2) for half in range(2)]:
            add_group(*what)
            if what[:1] + what[2:] == ("K", 2):
                order.append(("conv", h, 0))
            if what[:1] + what[2:] == ("Q", 1):
                order.append(("conv", h, 1))
                order.append(("silu", h, 0))
            if what[:1] + what[2:] == ("V", 1):
                order.append(("silu", h, 1))
            if h == 0 and what == ("V", 0, 3):
                order.append(("gate_columns",))
            after_group(h - 1, i)
            i += 1
    i = 0
    for g in range(NG):
        for a in range(2):
            for half in range(2):
                add_group("P", g, a, half)
                if half == 1:
                    order.append(("pool", g, a))
                if g > 0 and (a, half) == (0, 0):
                    for fo in range(2):
                        for m_half in range(2):
                            add_group("M", g - 1, fo, m_half)
                    order.append(("store_pool", g - 1))
                after_group(H - 1, i)
                i += 1
    for fo in range(2):
        for half in range(2):
            add_group("M", NG - 1, fo, half)
    order.append(("store_pool", NG - 1))

    evac, counts = [], [0, 0]
    for g in groups:
        dve = int(g[0] == "T")
        counts[dve] += 1
        evac.append((dve, counts[dve]))
    group_no = {g: n for n, g in enumerate(groups)}

    slots = [(kind, h) for h in range(H) for kind in ("KQ", "V", "O")] + [("P", g) for g in range(NG)]
    slot_no = {s: n for n, s in enumerate(slots)}
    SLOTC = 256
    slot_of = {"K": "KQ", "Q": "KQ", "V": "V", "O": "O", "P": "P"}
    last_group = {}
    for n, g in enumerate(groups):
        if g[0] in slot_of:
            last_group[slot_no[(slot_of[g[0]], g[1])]] = n

    mod_scr = nc.dram_tensor("mod_scr", [NMOD, 2, D], fp32).ap()
    mix_scr = nc.dram_tensor("mix_scr", [D, T], fp32).ap()
    x1_scr = nc.dram_tensor("x1_scr", [T, D], fp32).ap()
    xn_scr = nc.dram_tensor("xn_scr", [T, D], fp32).ap()

    x_t = x[0].rearrange("(n p) d -> n p d", p=P)
    ctx_t = ctx[0].rearrange("(n p) d -> n p d", p=P)
    w_in_v = w_in[0].rearrange("(k p) n -> p k n", p=P)
    w_out_v = w_out[0].rearrange("(k p) n -> p k n", p=P)
    w_mod_v = w_mod[0].rearrange("(p k) n -> p k n", k=KD)
    mix_v = mix_scr.rearrange("(k p) t -> p k t", p=P)
    x1_t = x1_scr.rearrange("(n p) d -> n p d", p=P)
    xn_t = xn_scr.rearrange("(n p) d -> n p d", p=P)
    out_t = out[0].rearrange("(n p) d -> n p d", p=P)

    es = ExitStack()
    with es:
        es.enter_context(nc.allow_non_contiguous_dma(reason="vectors laid out over the partitions"))

        def sem(name):
            return es.enter_context(nc.semaphore(name))

        SBUF = 53200
        KEPT = 2 * P + 128 + 10 * KD
        arena = es.enter_context(nc.sbuf_tensor("kept", [P, KEPT], fp32))
        at = [0]

        def carve(v, dims):
            if len(dims) == 2:
                return v.rearrange("p (a b) -> p a b", a=dims[0])
            if len(dims) == 3:
                return v.rearrange("p (a b c) -> p a b c", a=dims[0], b=dims[1])
            return v

        def take(n, *dims):
            at[0] += n
            return carve(arena[:, at[0] - n:at[0]], dims)

        def view(lo, *dims):
            n = 1
            for v in dims:
                n *= v
            return carve(arena[:, lo:lo + n], dims)

        ident = take(P)
        small = take(128)
        ones_row = take(P)
        shift1, scale1 = take(2 * KD, 2, KD), take(2 * KD, 2, KD)
        shift2, scale2 = take(KD), take(KD)
        norm_col = take(2 * KD, 2, KD)
        cc = take(2 * KD, 2, KD)
        assert at[0] <= KEPT
        stage = ExitStack()
        ARENA = SBUF - KEPT
        arena = stage.enter_context(nc.sbuf_tensor("stage1", [P, ARENA], fp32))
        at[0] = top = 0
        hT = take(KD * T, KD, T)
        hcT = take(KD * TC, KD, TC)
        ring = take(2 * KD * SLOTC, 2, KD, SLOTC)
        kT = take(2 * CONVN, 2, CONVN)
        qT = take(2 * T, 2, T)
        v_off = at[0]
        V = take(2 * NTT * (DV + 1), 2, NTT, DV + 1)
        raw = take(RAWN)
        sig_o = take(2 * T, 2, T)
        h_sum = take(NT * DV, NT, DV)
        Dm, WI, Pm, qw, kw = (take(2 * P, 2, P) for _ in range(5))
        C = take(4 * (DV + 1), 2, 2, DV + 1)
        MxN = take(NTT * P)
        mask = take(2 * P, 2, P)
        sel = take(8 * P, 8, P)
        Acol = take(NTT * GR, NTT, GR)
        EM = take(NTT * GR, NTT, GR)
        mp_col = take(8 * NTT, 8, NTT)
        conv_w = take(2 * H * TAPS, 2, H, TAPS)
        headg_col = take(2 * H)
        pscale_col = take(2 * NG)
        pmix = take(2 * T, 2, T)
        poolw = take(2 * GC, 2, GC)
        row_sum = take(BN)
        assert at[0] <= ARENA, at[0]

        o = v_off
        xt = view(o, 2, D)
        o = top + KD * T + KD * TC
        mod_ring = view(o, 4, D)
        o += 4 * D
        mod_row = view(o, 2, D)
        assert 2 * D <= 2 * CONVN + 2 * T
        GN = NTT * P
        assert 2 * GN <= NTT * (DV + 1) and GN <= CONVN and GN <= 2 * T
        v1 = v_off + NTT * (DV + 1)
        LI, LF = view(v1, GN), view(v1 + GN, GN)
        GB = kT[:, 1, 0:GN]
        GX = sig_o.rearrange("p a b -> p (a b)")[:, 0:GN]
        h_flat = h_sum.rearrange("p a b -> p (a b)")
        wg = h_flat[:, 0:KD * 100].rearrange("p (k c) -> p k c", k=KD)
        reset = h_flat[:, 0:GN]
        mac_ring = pmix.rearrange("p a b -> p (a b)").rearrange("p (s k n) -> p s k n", s=2, k=2)
        mac_sum = poolw.rearrange("p a b -> p (a b)")
        assert mac_sum.shape[1] == BN
        PADG = 8
        HW_ = GRID_W + 2 * PADG
        HR = ROWS + 2 * PADG
        o = top + KD * T
        pool_v = [view(o, HR, GRID_W), view(o + HR * GRID_W, HR, GRID_W)]
        o = top + KD * T + KD * TC + 2 * KD * SLOTC
        pool_h0 = view(o, ROWS, HW_)
        assert ROWS * HW_ <= CONVN
        pool_h1 = view(v_off, ROWS, HW_)
        o = v_off + ROWS * HW_
        inv_b = view(o, T)
        assert ROWS * HW_ + T <= NTT * (DV + 1)
        dT = [qT[:, 0, :], raw[:, 0:T]]

        bank = [es.enter_context(nc.psum_tensor(f"bank{n}", [P, BN], fp32)) for n in range(8)]
        PR = bank[0:2]
        A_b, N_b, C_b = bank[2:4], bank[4:6], bank[6:8]

        ld_const = sem("ld_const")
        ld_x = [sem(f"ld_x_{n}") for n in range(2)]
        consts = sem("consts")
        x_stat = sem("x_stat")
        x_scaled = sem("x_scaled")
        x_tr = sem("x_tr")
        x_evA, x_evD = sem("x_evA"), sem("x_evD")
        silu_c = sem("silu_c")
        ld_mod = [sem(f"ld_mod_{n}") for n in range(4)]
        mod_used = sem("mod_used")
        ld_bmod = sem("ld_bmod")
        mod_sum = sem("mod_sum")
        mod_col = sem("mod_col")
        s1_ready = sem("s1_ready")
        h_readyA, h_readyD = sem("h_readyA"), sem("h_readyD")
        ld_mac = [sem(f"ld_mac_{n}") for n in range(2)]
        mac_used = sem("mac_used")
        row_bias, row_st = sem("row_bias"), sem("row_st")
        ld_cols = sem("ld_cols")
        ld_wg = sem("ld_wg")
        gate_mm = sem("gate_mm")
        raw_clear = sem("raw_clear")
        gate_ev = sem("gate_ev")
        gact = sem("gact")
        grow = sem("grow")
        gcol_mm = sem("gcol_mm")
        gcols = sem("gcols")
        gfree = sem("gfree")
        ld_w = [sem(f"ld_w_{n}") for n in range(2)]
        grp = sem("grp")
        evA, evD = sem("evA"), sem("evD")
        conv_done = sem("conv_done")
        silu_done = sem("silu_done")
        stA = [sem(f"stA_{d}") for d in range(2)]
        expd = [sem(f"expd_{d}") for d in range(2)]
        fac = [sem(f"fac_{d}") for d in range(2)]
        stB = [sem(f"stB_{d}") for d in range(2)]
        cup = [sem(f"cup_{d}") for d in range(2)]
        hsq = sem("hsq")
        hrs = sem("hrs")
        hnorm = sem("hnorm")
        mix_st = sem("mix_st")
        pool_d = sem("pool_d")
        ld_pool = sem("ld_pool")
        pmix_st = sem("pmix_st")
        ld_x1, ld_g1 = sem("ld_x1"), sem("ld_g1")
        ld_mix = [sem(f"ld_mix_{n}") for n in range(MSL)]
        ld_wo = [sem(f"ld_wo_{n}") for n in range(OSL)]
        m_hi, m_lo = sem("m_hi"), sem("m_lo")
        o_hi, o_lo = sem("o_hi"), sem("o_lo")
        o_used = sem("o_used")
        o_ev = sem("o_ev")
        x1_st = [sem(f"x1_st_{n}") for n in range(NT)]
        x1_sq = sem("x1_sq")
        x1_n = sem("x1_n")
        xn_st = sem("xn_st")
        ld_r = sem("ld_r")
        wr_s = sem("wr_s")
        r_mm = sem("r_mm")
        r_ev = sem("r_ev")
        r_tr = sem("r_tr")
        rt_ev = sem("rt_ev")
        r_log = sem("r_log")
        sm_a, sm_d = sem("sm_a"), sem("sm_d")
        aff_mm = sem("aff_mm")
        topk = sem("topk")
        topk_mm, topk_ev = sem("topk_mm"), sem("topk_ev")
        idx_r = sem("idx_r")
        ld_g2 = sem("ld_g2")
        ld_e = [sem(f"ld_e_{n}") for n in range(ESL)]
        e_hi, e_lo = sem("e_hi"), sem("e_lo")
        e_used = sem("e_used")
        cols_set = sem("cols_set")
        gathered, scattered = sem("gathered"), sem("scattered")
        xs_mm = sem("xs_mm")
        xs_vA, xs_vD = sem("xs_vA"), sem("xs_vD")
        xs_hi, xs_lo = sem("xs_hi"), sem("xs_lo")
        g_act, a_rdy = sem("g_act"), sem("a_rdy")
        a_mm, a_hi, a_lo = sem("a_mm"), sem("a_hi"), sem("a_lo")
        y_ev, y_free = sem("y_ev"), sem("y_free")
        ld_nf = sem("ld_nf")
        ld_f = [sem(f"ld_f_{n}") for n in range(NT)]
        f_sq, f_out = sem("f_sq"), sem("f_out")
        out_st = sem("out_st")
        passed_sp, passed_pool = sem("passed_sp"), sem("passed_pool")
        dv, ac = sem("dv"), sem("ac")
        chains = {"dve": 0, "act": 0}

        H_DVE = 11
        ssx, rsx = small[:, 0:16], small[:, 16:32]
        bg = small[:, 32:33]
        one = small[:, 33:34]
        ones_col = ones_row[:, 0:1]
        den = small[:, 34:36]
        ssh, rsh = small[:, 40:48], small[:, 48:56]
        mpr = small[:, 56:56 + NTT + 1]
        ss1, rs1 = small[:, 72:80], small[:, 80:88]
        ssf, rsf = small[:, 88:96], small[:, 96:104]
        eps = small[:, 104:105]

        block = stage.enter_context(nc.Block())

        @block.sync
        def _(sp):
            for i in range(NTT):
                if i >= 2:
                    sp.wait_ge(x_evA, 2 * (i - 1))
                    sp.wait_ge(x_evD, 2 * (i - 1))
                sp.dma_start(xt[:, i % 2, :], ctx_t[i] if i < NC else x_t[i - NC]).then_inc(ld_x[i % 2], 16)
                for n in mod_pieces(i):
                    if n >= 4:
                        sp.wait_ge(mod_used, n - 3)
                    sp.dma_start(mod_ring[:, n % 4, :], w_mod_v[:, n % KD, (n // KD) * D:(n // KD + 1) * D]).then_inc(ld_mod[n % 4], 16)
            slot_after = {last_group[n]: n + 2 for n in range(len(slots) - 2)}

            def load_slot(n):
                kind, h = slots[n]
                dst = ring[:, n % 2]
                if kind == "KQ":
                    sp.dma_start(dst[:, :, 0:DQK], w_in_v[:, :, K_OFF + h * DQK:K_OFF + (h + 1) * DQK]).then_inc(ld_w[n % 2], 16)
                    sp.dma_start(dst[:, :, DQK:2 * DQK], w_in_v[:, :, Q_OFF + h * DQK:Q_OFF + (h + 1) * DQK]).then_inc(ld_w[n % 2], 16)
                else:
                    off = {"V": V_OFF, "O": O_OFF, "P": P_OFF}[kind] + h * SLOTC
                    sp.dma_start(dst, w_in_v[:, :, off:off + SLOTC]).then_inc(ld_w[n % 2], 32)

            def load_mac(n):
                b, k = n // MACP, 2 * (n % MACP)
                sp.dma_start(mac_ring[:, n % 2], w_mod_v[:, k:k + 2, 2 * D + b * BN:2 * D + (b + 1) * BN]).then_inc(ld_mac[n % 2], 16)

            sp.wait_ge(mod_used, 2 * KD)
            load_slot(0)
            load_slot(1)
            load_mac(0)
            load_mac(1)
            for item in order:
                if item[0] == "group" and item[1] in slot_after:
                    sp.wait_ge(grp, item[1] + 1)
                    load_slot(slot_after[item[1]])
                elif item[0] == "mac" and item[1] + 2 < MACS:
                    sp.wait_ge(mac_used, item[1] + 1)
                    load_mac(item[1] + 2)
            sp.wait_ge(mix_st, 16 * H)
            sp.wait_ge(pmix_st, 16 * NG)
            sp.wait_ge(row_st, 16 * (NMOD - 2) * NB)
            sp.wait_ge(ld_cols, 32)

        @block.gpsimd
        def _(pool):
            eng = nc.gpsimd
            eng.memset(ident, 0.0)
            eng.memset(ones_row, 1.0)
            eng.memset(mask, 0.0)
            eng.memset(sel, 0.0)
            eng.memset(small, 0.0).then_inc(consts, 1)
            pool.wait_ge(consts, 1)
            eng.memset(one, 1.0)
            eng.memset(eps, EPS)
            eng.affine_select(out=ident, in_=ident, compare_op=ALU.not_equal, fill=1.0, base=0,
                              pattern=[[-1, P]], channel_multiplier=1)
            eng.affine_select(out=mask[:, 0], in_=mask[:, 0], compare_op=ALU.is_ge, fill=NEG, base=0,
                              pattern=[[1, P]], channel_multiplier=-1)
            eng.affine_select(out=mask[:, 1], in_=mask[:, 1], compare_op=ALU.is_ge, fill=NEG, base=0,
                              pattern=[[-1, P]], channel_multiplier=1)
            s4 = sel.rearrange("p (d h) n -> p d h n", d=2)
            eng.affine_select(out=s4, in_=s4, compare_op=ALU.not_equal, fill=-1.0, base=0,
                              pattern=[[-32, 2], [-1, 4], [0, P]], channel_multiplier=1).then_inc(consts, 1)
            eng.memset(wg, 0.0).then_inc(consts, 1)
            pool.wait_ge(consts, 3)
            for n, col in enumerate((0, 8, 4, 12)):
                eng.dma_start(wg[:, :, 32 * n:32 * n + 4], w_in_v[:, :, G_OFF + col:G_OFF + col + 4]).then_inc(ld_wg, 16)
                eng.dma_start(bg[32 * n:32 * n + 4, :], b_gates[0, col:col + 4].rearrange("(p a) -> p a", a=1)).then_inc(ld_wg, 16)
            for m in range(2):
                eng.dma_start(mod_row[0:2, m, :], b_mod[0:1, m * D:(m + 1) * D].to_broadcast([2, D])).then_inc(ld_bmod, 16)
            eng.dma_start(mod_scr[2:NMOD, 0, :], b_mod[0, 2 * D:NMOD * D].rearrange("(m d) -> m d", m=NMOD - 2)).then_inc(row_bias, 16)
            pool.wait_ge(row_bias, 16)
            last = {("store_mix", h): group_no[("T", h, 1, 1)] for h in range(H)}
            last.update({("store_pool", g): group_no[("M", g, 1, 1)] for g in range(NG)})
            pooled = [0]
            for item in order:
                if item[0] == "store_mix":
                    h = item[1]
                    pool.wait_ge(evD, evac[last[item]][1])
                    eng.dma_start(mix_v[:, 2 * h:2 * h + 2, :], sig_o).then_inc(mix_st, 16)
                elif item[0] == "store_pool":
                    g = item[1]
                    pool.wait_ge(evA, evac[last[item]][1])
                    eng.dma_start(mix_v[:, 2 * H + 2 * g:2 * H + 2 * g + 2, :], pmix).then_inc(pmix_st, 16)
                elif item[0] == "group" and groups[item[1]][0] == "R":
                    b = groups[item[1]][1]
                    pool.wait_ge(evA, evac[item[1]][1])
                    eng.dma_start(mod_scr[2 + b // NB, 0:1, (b % NB) * BN:(b % NB + 1) * BN], row_sum[0:1, :],
                                  accum_op=ALU.add).then_inc(row_st, 16)
                    if b == (NMOD - 2) * NB - 1:
                        pool.wait_ge(row_st, 16 * (NMOD - 2) * NB)
                        eng.dma_start(shift2, mod_scr[3, 0, :].rearrange("(k p) -> p k", p=P)).then_inc(ld_cols, 16)
                        eng.dma_start(scale2, mod_scr[4, 0, :].rearrange("(k p) -> p k", p=P)).then_inc(ld_cols, 16)
                elif item[0] == "pool" and item[2] == 0:
                    g = item[1]
                    if g == 0:
                        pool.wait_ge(stB[0], (H - 1) * NTT)
                        pool.wait_ge(stB[1], (H - 1) * NTT)
                    else:
                        pool.wait_ge(pool_d, 2 * g)
                        pool.wait_ge(grp, group_no[("M", g - 1, 1, 1)] + 1)
                    eng.dma_start(inv_b, inv_count[g:g + 1, :].to_broadcast([P, T])).then_inc(ld_pool, 16)
                    eng.dma_start(poolw, pool_w[0, g].rearrange("(k p) n -> p k n", p=P)).then_inc(ld_pool, 16)

        @block.scalar
        def _(act_e):
            sc = nc.scalar

            def link(ins):
                chains["act"] += 1
                ins.then_inc(ac, 1)
                act_e.wait_ge(ac, chains["act"])

            sc.dma_start(cc[:, 0, :], c[0].rearrange("(p k) -> p k", k=KD)).then_inc(ld_const, 16)
            sc.dma_start(cc[:, 1, :], c_ctx.rearrange("(p k) -> p k", k=KD)).then_inc(ld_const, 16)
            sc.dma_start(norm_col[:, 0, :], norm1[0].rearrange("(k p) -> p k", p=P)).then_inc(ld_const, 16)
            sc.dma_start(norm_col[:, 1, :], norm2[0].rearrange("(k p) -> p k", p=P)).then_inc(ld_const, 16)
            for n, w in enumerate((conv_k_w, conv_q_w)):
                for h in range(H):
                    sc.dma_start(conv_w[:, n, h, :], w[0, :, h * DQK:(h + 1) * DQK].rearrange("j p -> p j")).then_inc(ld_const, 16)
            sc.dma_start(headg_col, head_g[0].rearrange("(k p) -> p k", p=P)).then_inc(ld_const, 16)
            sc.dma_start(pscale_col, pool_scale[0].rearrange("(k p) -> p k", p=P)).then_inc(ld_const, 16)
            act_e.wait_ge(ld_const, 16 * 14)
            sc.activation(cc[:, :, :], cc[:, :, :], ACT.Silu).then_inc(silu_c, 1)
            act_e.wait_ge(consts, 2)
            for i in range(NTT):
                act_e.wait_ge(ld_x[i % 2], 16 * (i // 2 + 1))
                link(sc.activation(sig_o.rearrange("p a b -> p (a b)"), xt[:, i % 2, :], ACT.Square, accum_out=ssx[:, i:i + 1]))
                sc.activation(rsx[:, i:i + 1], ssx[:, i:i + 1], ACT.Sqrt, bias=eps, scale=1.0 / D).then_inc(x_stat, 1)
                for q in (0, 2):
                    act_e.wait_ge(x_tr, 4 * i + q + 1)
                    dst = hcT[:, 4 * q:4 * q + 4, i * P:(i + 1) * P] if i < NC else hT[:, 4 * q:4 * q + 4, (i - NC) * P:(i - NC + 1) * P]
                    sc.activation(dst, bank[4 + q][:, :].rearrange("p (a b) -> p a b", a=4), ACT.Copy).then_inc(x_evA, 1)
            act_e.wait_ge(s1_ready, 1)
            act_e.wait_ge(x_evD, 2 * NTT)
            act_e.wait_ge(x_evA, 2 * NTT)
            for k in range(H_DVE, KD):
                last = sc.activation(hT[:, k, :], hT[:, k, :], ACT.Identity, bias=shift1[:, 0, k:k + 1], scale=scale1[:, 0, k:k + 1])
            last.then_inc(h_readyA, 1)
            act_e.wait_ge(grow, 1)
            act_e.wait_ge(ld_wg, 16 * 8)
            for n, (lo, w) in enumerate(((0, TC), (TC, BN), (TC + BN, BN))):
                act_e.wait_ge(gate_mm, n + 1)
                pb = bank[2 + n]
                for j, dst in ((0, LI), (2, LF)):
                    f, b = 32 * j, 32 * j + 32
                    sc.activation(dst[0:4, lo:lo + w], pb[f:f + 4, 0:w], ACT.Identity, bias=bg[f:f + 4, :])
                    if lo == 0:
                        rev = dst[32:36, 0:TC][:, ::-1]
                    else:
                        r0 = TC + T - (lo - TC) - w
                        rev = dst[32:36, r0:r0 + w][:, ::-1]
                    last = sc.activation(rev, pb[b:b + 4, 0:w], ACT.Identity, bias=bg[b:b + 4, :])
                last.then_inc(gate_ev, 1)
            act_e.wait_ge(gact, 1)
            link(sc.activation(GX[0:GR], GX[0:GR], ACT.Exp, scale=-1.0))
            sc.activation(GX[0:GR], GX[0:GR], ACT.Ln, bias=one[0:GR, :]).then_inc(gact, 1)

            for item in order:
                if item[0] == "gate_columns":
                    act_e.wait_ge(gcol_mm, 1)
                    sc.activation(EM, bank[6][:, 0:NTT * GR].rearrange("p (a b) -> p a b", a=NTT), ACT.Exp, scale=-1.0).then_inc(gcols, 1)
                elif item[0] == "group":
                    g = item[1]
                    kind, h = groups[g][0:2]
                    if kind == "T":
                        continue
                    par = h % 2
                    if kind == "K" and groups[g][2] == 0 and h:
                        act_e.wait_ge(conv_done, 2 * h)
                    if kind == "Q" and groups[g][2] == 0:
                        act_e.wait_ge(conv_done, 2 * h + 1)
                    if kind == "O" and h >= 1 and groups[g][2:] == (0, 0):
                        act_e.wait_ge(mix_st, 16 * h)
                    if kind == "K" and (h, groups[g][2]) == (0, 0):
                        act_e.wait_ge(raw_clear, 1)
                    if kind == "V" and (h, groups[g][2]) == (1, 0):
                        act_e.wait_ge(gcols, 4)
                    if kind == "R" and h >= 1:
                        act_e.wait_ge(row_st, 16 * h)
                    if kind == "V" and groups[g][2] == 0 and h >= 2:
                        for d in range(2):
                            act_e.wait_ge(stB[d], (h - 1) * NTT)
                    if kind == "P" and groups[g][2:] == (0, 0) and h == 0:
                        act_e.wait_ge(gfree, 1)
                    if kind == "P" and groups[g][-1] == 0 and (h, groups[g][2]) != (0, 0):
                        act_e.wait_ge(pool_d, 2 * h + groups[g][2])
                    if kind == "M" and groups[g][2:] == (0, 0) and h >= 1:
                        act_e.wait_ge(pmix_st, 16 * h)
                    act_e.wait_ge(grp, g + 1)
                    src = PR[g % 2]
                    if kind == "R":
                        sc.activation(row_sum[0:1, :], src[0:1, :], ACT.Copy).then_inc(evA, 1)
                    elif kind in "KQ":
                        part = groups[g][2]
                        if kind == "Q":
                            part += 1
                        if part == 0:
                            sc.activation(raw[:, PADC:PADC + TC], src[:, 0:TC], ACT.Copy).then_inc(evA, 1)
                        else:
                            lo = 2 * PADC + TC + (part - 1) * BN
                            sc.activation(raw[:, lo:lo + BN], src[:, :], ACT.Copy).then_inc(evA, 1)
                    elif kind == "V":
                        sc.activation(V[:, par, groups[g][2], 0:DV], src[:, 0:DV], ACT.Copy).then_inc(evA, 1)
                    elif kind == "O":
                        _, _, ft_, half = groups[g]
                        sc.activation(sig_o[:, ft_, half * BN:(half + 1) * BN], src[:, :], ACT.Sigmoid).then_inc(evA, 1)
                    elif kind == "P":
                        half = groups[g][3]
                        rows = ROWS // 2
                        sc.activation(pool_h0[:, half * rows:(half + 1) * rows, PADG:PADG + GRID_W],
                                      src[:, :].rearrange("p (a b) -> p a b", a=rows), ACT.Copy).then_inc(evA, 1)
                    else:
                        _, gg, fo, half = groups[g]
                        sc.activation(pmix[:, fo, half * BN:(half + 1) * BN], src[:, :], ACT.Copy,
                                      scale=pscale_col[:, 2 * gg + fo:2 * gg + fo + 1]).then_inc(evA, 1)
                elif item[0] == "silu":
                    _, h, n = item
                    act_e.wait_ge(conv_done, 2 * h + n + 1)
                    buf = kT[:, h % 2, :] if n == 0 else qT[:, h % 2, :]
                    sc.activation(buf, buf, ACT.Silu).then_inc(silu_done, 1)
                elif item[0] == "A":
                    _, h, j = item
                    for d in range(2):
                        s = h * NTT + j
                        ch, row = chunk_of(d, j), 32 * d + h
                        tl = LAST[d]
                        act_e.wait_ge(stA[d], s + 1)
                        if s:
                            act_e.wait_ge(cup[d], s)
                        pb = A_b[d]
                        a_s, mp = Acol[:, ch, row:row + 1], mp_col[:, 4 * d + h, j:j + 1]
                        if j < NC:
                            sc.activation(Dm[:, d, tl:tl + 1], pb[:, 0:1], ACT.Exp, bias=a_s)
                            sc.activation(WI[:, d, tl:tl + 1], pb[:, 0:1], ACT.Exp, bias=mp).then_inc(expd[d], 1)
                        else:
                            sc.activation(Dm[:, d, :], pb[:, P:2 * P], ACT.Exp, bias=a_s)
                            sc.activation(WI[:, d, :], pb[:, 0:P], ACT.Exp, bias=mp).then_inc(expd[d], 1)
                elif item[0] == "normalise":
                    h = item[1]
                    for d in range(2):
                        act_e.wait_ge(cup[d], (h + 1) * NTT)
                    if h:
                        act_e.wait_ge(hrs, h)
                    for t in range(NT):
                        link(sc.activation(Dm.rearrange("p a b -> p (a b)"), h_sum[:, t, :], ACT.Square, accum_out=ssh[:, t:t + 1]))
                    sc.activation(ssh, ssh, ACT.Sqrt, bias=eps, scale=1.0 / DV).then_inc(hsq, 1)


        @block.tensor
        def _(pe):
            te = nc.tensor
            pe.wait_ge(consts, 2)
            for i in range(NTT):
                pe.wait_ge(x_scaled, i + 1)
                for q in range(4):
                    if i:
                        pe.wait_ge(x_evD if q % 2 else x_evA, 2 * (i - 1) + q // 2 + 1)
                    for k in range(4):
                        last = te.transpose(bank[4 + q][:, k * P:(k + 1) * P], xt[:, i % 2, (4 * q + k) * P:(4 * q + k + 1) * P], ident)
                    last.then_inc(x_tr, 1)
                if i == 0:
                    pe.wait_ge(silu_c, 1)
                for m in mod_pieces(i):
                    k = m % KD
                    if m == KD:
                        pe.wait_ge(mod_sum, 1)
                    pe.wait_ge(ld_mod[m % 4], 16 * (m // 4 + 1))
                    for n in range(NB):
                        last = te.matmul(bank[n][0:2, :], cc[:, :, k], mod_ring[:, m % 4, n * BN:(n + 1) * BN],
                                         start=(k == 0), stop=(k == KD - 1))
                    last.then_inc(mod_used, 1)
            pe.wait_ge(mod_sum, 2)
            for m in range(2):
                for k in range(KD):
                    last = te.matmul(bank[0][:, 2 * (m * KD + k):2 * (m * KD + k) + 2], mod_row[0:2, m, k * P:(k + 1) * P],
                                     ident[0:2, 0:2], start=True, stop=True)
            last.then_inc(mod_col, 1)
            pe.wait_ge(h_readyA, 1)
            pe.wait_ge(h_readyD, 1)
            pe.wait_ge(ld_wg, 16 * 8)
            for n, w in enumerate((TC, BN, BN)):
                for k in range(KD):
                    rhs = hcT[:, k, :] if n == 0 else hT[:, k, (n - 1) * BN:n * BN]
                    last = te.matmul(bank[2 + n][0:100, 0:w], wg[:, k, :], rhs, start=(k == 0), stop=(k == KD - 1))
                last.then_inc(gate_mm, 1)

            for item in order:
                if item[0] == "gate_columns":
                    pe.wait_ge(grow, 2)
                    for j in range(NTT):
                        te.transpose(bank[5][:, j * GR:(j + 1) * GR], GX[0:GR, j * P:(j + 1) * P], ident[0:GR, 0:GR])
                        te.transpose(bank[6][:, j * GR:(j + 1) * GR], GB[0:GR, j * P:(j + 1) * P], ident[0:GR, 0:GR])
                    for r in range(8):
                        last = te.matmul(bank[7][:, r * NTT:(r + 1) * NTT], sel[0:GR, r, :], mpr[0:GR, 0:NTT], start=True, stop=True)
                    last.then_inc(gcol_mm, 1)
                elif item[0] == "group":
                    g = item[1]
                    kind, h = groups[g][0:2]
                    par = h % 2
                    if g >= 2:
                        dve, count = evac[g - 2]
                        pe.wait_ge(evD if dve else evA, count)
                    dst = PR[g % 2]
                    if kind in slot_of:
                        s = slot_no[(slot_of[kind], h)]
                        pe.wait_ge(ld_w[s % 2], 32 * (s // 2 + 1))
                        w = ring[:, s % 2]
                    if kind == "R":
                        pe.wait_ge(mac_used, MACP * (h + 1))
                        last = te.matmul(dst[0:1, :], ones_col, mac_sum, start=True, stop=True)
                    elif kind in "KQ":
                        part = groups[g][2] + (kind == "Q")
                        c0 = DQK * (kind == "Q")
                        width = TC if part == 0 else BN
                        for k in range(KD):
                            rhs = hcT[:, k, :] if part == 0 else hT[:, k, (part - 1) * BN:part * BN]
                            last = te.matmul(dst[:, 0:width], w[:, k, c0:c0 + DQK], rhs, start=(k == 0), stop=(k == KD - 1))
                    elif kind == "V":
                        t = groups[g][2]
                        for k in range(KD):
                            lhs = hcT[:, k, t * P:(t + 1) * P] if t < NC else hT[:, k, (t - NC) * P:(t - NC + 1) * P]
                            last = te.matmul(dst[:, 0:DV], lhs, w[:, k, :], start=(k == 0), stop=(k == KD - 1))
                    elif kind in "OP":
                        _, _, a, half = groups[g]
                        for k in range(KD):
                            last = te.matmul(dst[:, :], w[:, k, a * P:(a + 1) * P], hT[:, k, half * BN:(half + 1) * BN],
                                             start=(k == 0), stop=(k == KD - 1))
                    elif kind == "T":
                        _, _, a, half = groups[g]
                        pe.wait_ge(hnorm, h + 1)
                        for t in range(4):
                            last = te.transpose(dst[:, t * P:(t + 1) * P], h_sum[:, 4 * half + t, a * P:(a + 1) * P], ident)
                    else:
                        _, gg, fo, half = groups[g]
                        pe.wait_ge(pool_d, 2 * gg + 2)
                        pe.wait_ge(ld_pool, 32 * (gg + 1))
                        for a in range(2):
                            last = te.matmul(dst[:, :], poolw[:, a, fo * P:(fo + 1) * P], dT[a][:, half * BN:(half + 1) * BN],
                                             start=(a == 0), stop=(a == 1))
                    last.then_inc(grp, 1)
                elif item[0] == "A":
                    _, h, j = item
                    par, s = h % 2, h * NTT + j
                    for d in range(2):
                        ch, tl, pb = chunk_of(d, j), LAST[d], A_b[d]
                        if s:
                            pe.wait_ge(fac[d], s)
                        if j == 0:
                            pe.wait_ge(silu_done, 2 * h + 2)
                            pe.wait_ge(gcols, 4)
                        selr = sel[0:GR, 4 * d + h, :]
                        k0 = ch * P if ch < NC else LAT0 + (ch - NC) * P
                        kc = kT[:, par, k0:k0 + P]
                        if j < NC:
                            te.matmul(pb[:, 0:1], selr, MxN[0:GR, ch * P + tl:ch * P + tl + 1], start=True, stop=True)
                        else:
                            mx = MxN[0:GR, ch * P:(ch + 1) * P]
                            te.matmul(pb[:, 0:P], selr, mx, start=True, stop=True)
                            te.matmul(pb[:, P:2 * P], selr, mx, start=True, stop=False)
                            te.matmul(pb[:, P:2 * P], ident, mask[:, d], start=False, stop=True)
                            last = te.matmul(pb[:, 2 * P:3 * P], kc, qT[:, par, (ch - NC) * P:(ch - NC + 1) * P], start=True, stop=True)
                        if j < NTT - 1:
                            last = te.transpose(pb[:, 3 * P:4 * P], kc, ident)
                        last.then_inc(stA[d], 1)
                elif item[0] == "B":
                    _, h, j = item
                    par, s = h % 2, h * NTT + j
                    if j == 0:
                        pe.wait_ge(evA, evac[group_no[("V", h, NTT - 1)]][1])
                    for d in range(2):
                        ch = chunk_of(d, j)
                        pe.wait_ge(fac[d], s + 1)
                        if s:
                            pe.wait_ge(cup[d], s)
                        v = V[:, par, ch, :]
                        if j >= NC:
                            te.matmul(N_b[d][:, 0:DV + 1], Pm[:, d, :], v, start=True, stop=False)
                            last = te.matmul(N_b[d][:, 0:DV + 1], qw[:, d, :], C[:, d, j % 2, :], start=False, stop=True)
                        if j < NTT - 1:
                            last = te.matmul(C_b[d][:, 0:DV + 1], kw[:, d, :], v, start=True, stop=True)
                        last.then_inc(stB[d], 1)


        @block.vector
        def _(dve):
            ve = nc.vector

            def link(ins):
                chains["dve"] += 1
                ins.then_inc(dv, 1)
                dve.wait_ge(dv, chains["dve"])

            def mod_bias(m):
                dve.wait_ge(mod_used, KD * (m + 1))
                for n in range(NB):
                    rows = mod_row[0:2, m, n * BN:(n + 1) * BN]
                    last = ve.tensor_tensor(rows, bank[n][0:2, :], rows, ALU.add)
                last.then_inc(mod_sum, 1)

            dve.wait_ge(consts, 2)
            for i in range(NTT):
                dve.wait_ge(x_stat, i + 1)
                link(ve.reciprocal(rsx[:, i:i + 1], rsx[:, i:i + 1]))
                ve.tensor_scalar(xt[:, i % 2, :], xt[:, i % 2, :], rsx[:, i:i + 1], None, ALU.mult).then_inc(x_scaled, 1)
                for q in (1, 3):
                    dve.wait_ge(x_tr, 4 * i + q + 1)
                    dst = hcT[:, 4 * q:4 * q + 4, i * P:(i + 1) * P] if i < NC else hT[:, 4 * q:4 * q + 4, (i - NC) * P:(i - NC + 1) * P]
                    ve.tensor_copy(dst, bank[4 + q][:, :].rearrange("p (a b) -> p a b", a=4)).then_inc(x_evD, 1)
                if i == (KD - 1) // MOD_PER_TILE:
                    dve.wait_ge(ld_bmod, 32)
                    mod_bias(0)
            mod_bias(1)
            dve.wait_ge(mod_col, 1)
            dve.wait_ge(ld_const, 16 * 14)
            cols = bank[0][:, 0:4 * KD].rearrange("p (m k r) -> p m r k", m=2, k=KD)
            ve.tensor_copy(shift1, cols[:, 0])
            for r in range(2):
                last = ve.scalar_tensor_tensor(scale1[:, r, :], cols[:, 1, r, :], 1.0, norm_col[:, 0, :], ALU.add, ALU.mult)
            last.then_inc(s1_ready, 1)
            dve.wait_ge(s1_ready, 1)
            dve.wait_ge(x_evA, 2 * NTT)
            for k in range(KD):
                if k < H_DVE:
                    ve.tensor_scalar(hT[:, k, :], hT[:, k, :], scale1[:, 0, k:k + 1], shift1[:, 0, k:k + 1], ALU.mult, ALU.add)
                last = ve.tensor_scalar(hcT[:, k, :], hcT[:, k, :], scale1[:, 1, k:k + 1], shift1[:, 1, k:k + 1], ALU.mult, ALU.add)
            last.then_inc(h_readyD, 1)
            ve.memset(LI[0:GR], 0.0)
            ve.memset(MxN[0:GR], 0.0)
            ve.memset(LF[0:GR], 0.0).then_inc(grow, 1)
            ve.memset(raw[:, 0:PADC], 0.0)
            ve.memset(raw[:, PADC + TC:2 * PADC + TC], 0.0)
            ve.memset(raw[:, RAWN - PADC:RAWN], 0.0).then_inc(raw_clear, 1)
            ve.memset(V[:, 0, :, DV:DV + 1], 1.0)
            dve.wait_ge(gate_ev, 3)
            link(ve.memset(reset[0:GR], 1.0))
            ve.memset(reset[0:GR].rearrange("p (a b) -> p a b", b=P)[:, :, 0:1], 0.0)
            ve.scalar_tensor_tensor(GX[0:GR], LF[0:GR], -1.0, LF[0:GR], ALU.mult, ALU.max).then_inc(gact, 1)
            dve.wait_ge(gact, 2)
            link(ve.scalar_tensor_tensor(LF[0:GR], LF[0:GR], 0.0, GX[0:GR], ALU.min, ALU.subtract))
            link(ve.tensor_tensor_scan(GB[0:GR], reset[0:GR], LF[0:GR], 0.0, ALU.mult, ALU.add))
            link(ve.tensor_tensor(LI[0:GR], LI[0:GR], GB[0:GR], ALU.subtract))
            for j in range(NTT):
                cs = slice(j * P, (j + 1) * P)
                e = (j + 1) * P - 1
                link(ve.tensor_tensor_scan(GX[0:GR, cs], LI[0:GR, cs], LI[0:GR, cs], mpr[0:GR, j:j + 1], ALU.max, ALU.max))
                link(ve.tensor_tensor(mpr[0:GR, j + 1:j + 2], GB[0:GR, e:e + 1], GX[0:GR, e:e + 1], ALU.add))
            link(ve.tensor_tensor(LF[0:GR], GB[0:GR], GX[0:GR], ALU.add))

            def natural(dst, src):
                ve.tensor_copy(dst[0:4, 0:GN], src[0:4, 0:GN])
                ve.tensor_copy(dst[32:36, 0:TC], src[32:36, 0:TC][:, ::-1])
                return ve.tensor_copy(dst[32:36, TC:TC + T], src[32:36, TC:TC + T][:, ::-1])

            link(natural(MxN, GX))
            natural(GX, LI)
            natural(GB, LF).then_inc(grow, 1)

            def pooling(g, a):
                L = g + 1

                def stages(src, bufs, axis, dst, size):
                    lo, hi = 0, size
                    cur = src
                    for k in range(L):
                        back, ahead = (1, 0) if k == 0 else (1 << (k - 1), 1 << (k - 1))
                        lo, hi = lo + back, hi - ahead
                        if k == L - 1:
                            lo, hi, nxt = PADG, size - PADG, dst
                        else:
                            nxt = bufs[k % 2]
                        if axis == 1:
                            target = nxt if k == L - 1 else nxt[:, :, lo:hi]
                            link(ve.tensor_tensor(target, cur[:, :, lo - back:hi - back], cur[:, :, lo + ahead:hi + ahead], ALU.add))
                        else:
                            target = nxt if k == L - 1 else nxt[:, lo:hi, :]
                            link(ve.tensor_tensor(target, cur[:, lo - back:hi - back, :], cur[:, lo + ahead:hi + ahead, :], ALU.add))
                        cur = nxt

                wide = pool_v[1].rearrange("p a b -> p (a b)")[:, 0:ROWS * HW_].rearrange("p (a b) -> p a b", a=ROWS)
                stages(pool_h0, [pool_h1, wide], 1, pool_v[0][:, PADG:PADG + ROWS, :], HW_)
                box = pool_h1.rearrange("p a b -> p (a b)")[:, 0:T].rearrange("p (a b) -> p a b", a=ROWS)
                stages(pool_v[0], [pool_v[1], pool_v[0]], 0, box, HR)
                if L >= 3:
                    ve.memset(pool_v[0][:, 0:PADG, :], 0.0)
                    ve.memset(pool_v[0][:, PADG + ROWS:, :], 0.0)
                dve.wait_ge(ld_pool, 32 * (g + 1))
                link(ve.tensor_tensor(box, box, inv_b.rearrange("p (a b) -> p a b", a=ROWS), ALU.mult))
                if g:
                    dve.wait_ge(grp, group_no[("M", g - 1, 1, 1)] + 1)
                ve.tensor_tensor(dT[a].rearrange("p (a b) -> p a b", a=ROWS), box,
                                 pool_h0[:, :, PADG:PADG + GRID_W], ALU.subtract).then_inc(pool_d, 1)

            for item in order:
                if item[0] == "gate_columns":
                    dve.wait_ge(gcol_mm, 1)
                    ve.tensor_copy(Acol, bank[5][:, 0:NTT * GR].rearrange("p (a b) -> p a b", a=NTT)).then_inc(gcols, 1)
                    ve.tensor_scalar(mp_col, bank[7][:, 0:8 * NTT].rearrange("p (a b) -> p a b", a=8), -1.0, None, ALU.mult).then_inc(gcols, 1)
                    ve.memset(V[:, 1, :, DV:DV + 1], 1.0).then_inc(gcols, 1)
                elif item[0] == "mac":
                    n = item[1]
                    dve.wait_ge(ld_mac[n % 2], 16 * (n // 2 + 1))
                    if n % MACP == 0 and n:
                        dve.wait_ge(grp, group_no[("R", n // MACP - 1)] + 1)
                    for q in range(2):
                        k = 2 * (n % MACP) + q
                        src, by = mac_ring[:, n % 2, q, :], cc[:, 0, k:k + 1]
                        if k == 0:
                            link(ve.tensor_scalar(mac_sum, src, by, None, ALU.mult))
                        elif q == 0:
                            dve.wait_ge(mac_used, n)
                            link(ve.scalar_tensor_tensor(mac_sum, src, by, mac_sum, ALU.mult, ALU.add))
                        else:
                            ve.scalar_tensor_tensor(mac_sum, src, by, mac_sum, ALU.mult, ALU.add).then_inc(mac_used, 1)
                elif item[0] == "group" and groups[item[1]][0] == "T":
                    g = item[1]
                    _, h, a, half = groups[g]
                    dve.wait_ge(evA, evac[group_no[("O", h, 1, 1)]][1])
                    dve.wait_ge(grp, g + 1)
                    so = sig_o[:, a, half * BN:(half + 1) * BN]
                    ve.scalar_tensor_tensor(so, PR[g % 2][:, :], headg_col[:, 2 * h + a:2 * h + a + 1], so, ALU.mult, ALU.mult).then_inc(evD, 1)
                elif item[0] == "conv":
                    _, h, n = item
                    dve.wait_ge(evA, evac[group_no[("K", h, 2) if n == 0 else ("Q", h, 1)]][1])
                    acc = kT[:, h % 2, :] if n == 0 else qT[:, h % 2, :]
                    lo, w = (0, CONVN) if n == 0 else (LAT0, T)
                    tap = conv_w[:, n, h, :]
                    link(ve.tensor_scalar(acc, raw[:, lo:lo + w], tap[:, 0:1], None, ALU.mult))
                    for j in range(1, TAPS):
                        ins = ve.scalar_tensor_tensor(acc, raw[:, lo + j:lo + j + w], tap[:, j:j + 1], acc, ALU.mult, ALU.add)
                        if j < TAPS - 1:
                            link(ins)
                    ins.then_inc(conv_done, 1)
                elif item[0] == "A":
                    _, h, j = item
                    par, s = h % 2, h * NTT + j
                    for d in range(2):
                        ch, tl, pb = chunk_of(d, j), LAST[d], A_b[d]
                        dve.wait_ge(expd[d], s + 1)
                        if s:
                            dve.wait_ge(stB[d], s)
                        if j >= NC:
                            ve.scalar_tensor_tensor(Pm[:, d, :], pb[:, 2 * P:3 * P], KSCALE, Dm[:, d, :], ALU.mult, ALU.mult)
                            last = ve.tensor_tensor(qw[:, d, :], qT[:, par, (ch - NC) * P:(ch - NC + 1) * P], WI[:, d, :], ALU.mult)
                        if j < NTT - 1:
                            last = ve.tensor_scalar(kw[:, d, :], pb[:, 3 * P:4 * P], Dm[:, d, tl:tl + 1], KSCALE, ALU.mult, ALU.mult)
                        last.then_inc(fac[d], 1)
                elif item[0] == "B":
                    _, h, j = item
                    s = h * NTT + j
                    for d in range(2):
                        ch, tl, row = chunk_of(d, j), LAST[d], 32 * d + h
                        dve.wait_ge(stB[d], s + 1)
                        if j < NTT - 1:
                            new, old = C[:, d, (j + 1) % 2, :], C[:, d, j % 2, :]
                            if j == 0:
                                last = ve.tensor_copy(new, C_b[d][:, 0:DV + 1])
                            else:
                                last = ve.scalar_tensor_tensor(new, old, WI[:, d, tl:tl + 1], C_b[d][:, 0:DV + 1], ALU.mult, ALU.add)
                        if j >= NC:
                            num, dcol = N_b[d], den[:, d:d + 1]
                            link(ve.tensor_scalar(dcol, num[:, DV:DV + 1], -1.0, EM[:, ch, row:row + 1], ALU.mult, ALU.max))
                            link(ve.tensor_tensor(dcol, num[:, DV:DV + 1], dcol, ALU.max))
                            link(ve.reciprocal(dcol, dcol))
                            hs = h_sum[:, ch - NC, :]
                            first = j < (NTT - 1 - ch + NC if d == 0 else ch)
                            if first:
                                last = ve.tensor_scalar(hs, num[:, 0:DV], dcol, None, ALU.mult)
                            else:
                                last = ve.scalar_tensor_tensor(hs, num[:, 0:DV], dcol, hs, ALU.mult, ALU.add)
                        last.then_inc(cup[d], 1)
                        dve.wait_ge(cup[d], s + 1)
                elif item[0] == "normalise":
                    h = item[1]
                    dve.wait_ge(hsq, h + 1)
                    ve.reciprocal(rsh, ssh).then_inc(hrs, 1)
                    dve.wait_ge(hrs, h + 1)
                    for t in range(NT):
                        last = ve.tensor_scalar(h_sum[:, t, :], h_sum[:, t, :], rsh[:, t:t + 1], None, ALU.mult)
                    last.then_inc(hnorm, 1)
                    if h == H - 2:
                        dve.wait_ge(grp, group_no[("V", H - 1, NC - 1)] + 1)
                        ve.memset(pool_v[0], 0.0)
                        ve.memset(pool_h0, 0.0).then_inc(gfree, 1)
                        dve.wait_ge(gfree, 1)
                elif item[0] == "pool":
                    _, g, a = item
                    dve.wait_ge(evA, evac[group_no[("P", g, a, 1)]][1])
                    pooling(g, a)


        stage.close()

        stage = ExitStack()
        UN = 2 * BN
        PARTS = 2 * OUL * UN + 2 * KD * BN
        parts = stage.enter_context(nc.sbuf_tensor("parts", [P, PARTS], fp32r))
        ARENA = SBUF - KEPT - PARTS
        arena = stage.enter_context(nc.sbuf_tensor("stage2", [P, ARENA], fp32))
        o_unit = carve(parts[:, 0:2 * OUL * UN], (OUL, 2, UN))
        mix = parts[:, 2 * OUL * UN:PARTS].rearrange("p (s k t) -> p s k t", s=2, k=KD)
        e_unit = carve(parts[:, 0:2 * USL * UN], (USL, 2, UN))
        o = 2 * USL * UN
        xsT = parts[:, o:o + 2 * D].rearrange("p (s k t) -> p s k t", s=2, k=KD)
        actT = parts[:, o + 2 * D:o + 2 * D + 2 * F].rearrange("p (s k t) -> p s k t", s=2, k=KF)
        assert o + 2 * D + 2 * F <= PARTS and CAP == P
        at[0] = 0
        x1 = take(NT * D, NT, D)
        raw_w = take(OSL * 2 * UN, OSL, 2, UN)
        raw_m = take(MSL * 2 * BN, MSL, 2, BN)
        gate1_b = take(D)
        tmp = take(2 * BN, 2, BN)
        assert at[0] <= ARENA, at[0]
        at[0] = NT * D
        xnT = take(2 * D, 2, KD, P)
        squares = take(D)
        aff, top_v, top_f, top_i = squares[:, 0:T], squares[:, T:T + P], squares[:, T + P:T + 2 * P], squares[:, T + 2 * P:T + 3 * P]
        top_i = top_i.bitcast(u32)
        wr, wrs = take(KD * EXP, KD, EXP), take(KD * EXP, KD, EXP)
        lb = take(EXP)
        L0, L1 = take(NT * EXP, NT, EXP), take(NT * EXP, NT, EXP)
        lst = take(4 * NT, 4, NT)
        idx_all, gate_all = take(EXP + 1).bitcast(u32), take(EXP + 1)
        idx_gather, idx_scatter, gate_now = take(1).bitcast(u32), take(1).bitcast(u32), take(1)
        assert at[0] <= NT * D + (OSL * 2 * UN + MSL * 2 * BN)
        e_raw = view(0, ESL, 2, UN)
        assert ESL * 2 * UN <= NT * D
        xs, y = view(NT * D, D), view(NT * D + D, D)
        act = aff[:, 0:F]
        gate2_b = gate1_b
        ft = [view(D * n, D) for n in range(NT)]
        normf_b = xs
        f_squares = y

        OU = 4 * KD
        EU = 2 * KD + 2 * KF
        EPC = EU // 2
        SIL, XV, ACTP, XP = 20, 28, 36, 40
        AHEAD = 4

        block = stage.enter_context(nc.Block())

        @block.sync
        def _(sp):
            w_out_k = w_out[0].rearrange("(k p) n -> p k n", p=P)
            for q in range(OU // 2):
                c2, kk = q // (KD // 2), 2 * (q % (KD // 2))
                th, ch = c2 // 2, c2 % 2
                if ch == 0:
                    m = th * (KD // 2) + kk // 2
                    if m >= MSL:
                        sp.wait_ge(m_lo, m - MSL + 1)
                    sp.dma_start(raw_m[:, m % MSL], mix_v[:, kk:kk + 2, th * BN:(th + 1) * BN]).then_inc(ld_mix[m % MSL], 16)
                if q >= OSL:
                    sp.wait_ge(o_lo, 2 * (q - OSL + 1))
                sp.dma_start(raw_w[:, q % OSL], w_out_k[:, kk:kk + 2, ch * UN:(ch + 1) * UN]).then_inc(ld_wo[q % OSL], 16)
                if q == OSL:
                    sp.dma_start(gate1_b, mod_scr[2, 0:1, :].to_broadcast([P, D])).then_inc(ld_g1, 16)
                    sp.dma_start(x1, x[0].rearrange("(n p) d -> p n d", p=P)).then_inc(ld_x1, 16)
            sp.wait_ge(o_lo, OU)
            sp.wait_ge(m_lo, KD)
            sp.dma_start(wr, w_router[0].rearrange("(k p) e -> p k e", p=P)).then_inc(ld_r, 16)
            sp.wait_ge(o_ev, 4 * 2 * NB)
            sp.dma_start(gate2_b, mod_scr[5, 0:1, :].to_broadcast([P, D])).then_inc(ld_g2, 16)
            wg_v = w_gate[0].rearrange("e (k p) n -> e p k n", p=P)
            wu_v = w_up[0].rearrange("e (k p) n -> e p k n", p=P)
            wd_v = w_down[0].rearrange("e (k p) (a n) -> e p k a n", p=P, a=2)

            def load_piece(e, i):
                if i < KD // 2:
                    src = wg_v[e, :, 2 * i:2 * i + 2, :]
                elif i < KD:
                    src = wu_v[e, :, 2 * i - KD:2 * i - KD + 2, :]
                else:
                    src = wd_v[e, :, i - KD, :, :]
                sp.dma_start(e_raw[:, i % ESL], src).then_inc(ld_e[i % ESL], 16)

            sp.wait_ge(xn_st, 16 * NT)
            sp.wait_ge(r_tr, 4 * NT)
            for i in range(ESL):
                load_piece(0, i)
            with sp.Fori(0, EXP - 1) as e:
                for i in range(ESL, EPC + ESL):
                    sp.wait_ge(e_lo, e * EU + 2 * (i - ESL + 1))
                    sp.sem_inc(passed_sp)
                    load_piece(e if i < EPC else e + 1, i % EPC)
            for i in range(ESL, EPC):
                sp.wait_ge(e_lo, (EXP - 1) * EU + 2 * (i - ESL + 1))
                load_piece(EXP - 1, i)
            sp.wait_ge(e_lo, EXP * EU)
            sp.wait_ge(xs_lo, EXP)
            sp.dma_start(normf_b, norm_f.rearrange("(a d) -> a d", a=1).to_broadcast([P, D])).then_inc(ld_nf, 16)
            sp.wait_ge(scattered, 16 * EXP)
            for i in range(NT):
                sp.dma_start(ft[i], x1_t[i]).then_inc(ld_f[i], 16)
            for i in range(NT):
                sp.wait_ge(f_out, i + 1)
                sp.dma_start(out_t[i], ft[i]).then_inc(out_st, 16)
            sp.wait_ge(out_st, 16 * NT)

        @block.gpsimd
        def _(pool):
            eng = nc.gpsimd
            for i in range(NT):
                pool.wait_ge(o_ev, 2 * 2 * NB * (i // 4) + 2 * NB + 2 * (i % 4) + 2)
                eng.dma_start(x1_t[i], x1[:, i, :]).then_inc(x1_st[i], 16)
            for i in range(NT):
                pool.wait_ge(x1_n, i + 1)
                eng.dma_start(xn_t[i], x1[:, i, :]).then_inc(xn_st, 16)
            pool.wait_ge(xn_st, 16 * NT)
            pool.wait_ge(idx_r, 1)
            pool.sem_inc(y_free)
            eng.indirect_dma_start(xs, None, xn_scr, bass.IndirectOffsetOnAxis(ap=idx_gather, axis=0)).then_inc(gathered, 16)

            def scatter(e):
                pool.wait_ge(y_ev, e + 2)
                pool.sem_inc(passed_pool)
                eng.indirect_dma_start(x1_scr, bass.IndirectOffsetOnAxis(ap=idx_scatter, axis=0), y, None,
                                       compute_op=ALU.add).then_inc(scattered, 16)
                pool.wait_ge(scattered, e * 16 + 16)
                pool.sem_inc(y_free)

            with pool.Fori(0, EXP - 1) as e:
                pool.wait_ge(xs_lo, e + 1)
                pool.wait_ge(idx_r, e + 2)
                pool.sem_inc(passed_pool)
                eng.indirect_dma_start(xs, None, xn_scr, bass.IndirectOffsetOnAxis(ap=idx_gather, axis=0)).then_inc(gathered, 16)
                scatter(e)
            scatter(EXP - 1)

        @block.scalar
        def _(act_e):
            sc = nc.scalar

            def link(ins):
                chains["act"] += 1
                ins.then_inc(ac, 1)
                act_e.wait_ge(ac, chains["act"])

            for u in range(OU):
                c2, k = u // KD, u % KD
                th, ch, q = c2 // 2, c2 % 2, u // 2
                if ch == 0 and k % 2 == 0:
                    m = th * (KD // 2) + k // 2
                    act_e.wait_ge(ld_mix[m % MSL], 16 * (m // MSL + 1))
                    if th:
                        act_e.wait_ge(o_used, KD + k + 2)
                    sc.activation(mix[:, 0, k:k + 2, :], raw_m[:, m % MSL], ACT.Copy).then_inc(m_hi, 1)
                if k % 2 == 0:
                    act_e.wait_ge(ld_wo[q % OSL], 16 * (q // OSL + 1))
                if u >= OUL:
                    act_e.wait_ge(o_used, u - OUL + 1)
                sc.activation(o_unit[:, u % OUL, 0, :], raw_w[:, q % OSL, u % 2, :], ACT.Copy).then_inc(o_hi, 1)

            def row_stat(i):
                act_e.wait_ge(o_ev, 2 * 2 * NB * (i // 4) + 2 * NB + 2 * (i % 4) + 2)
                if i == 0:
                    act_e.wait_ge(o_lo, OU)
                    act_e.wait_ge(m_lo, KD)
                link(sc.activation(squares, x1[:, i, :], ACT.Square, accum_out=ss1[:, i:i + 1]))
                sc.activation(rs1[:, i:i + 1], ss1[:, i:i + 1], ACT.Sqrt, bias=eps, scale=1.0 / D).then_inc(x1_sq, 1)

            row_stat(0)
            for i in range(NT):
                if i < NT - 1:
                    row_stat(i + 1)
                for q in (0, 2):
                    act_e.wait_ge(r_tr, 4 * i + q + 1)
                    if i >= 2:
                        act_e.wait_ge(r_mm, i)
                    sc.activation(xnT[:, i % 2, 4 * q:4 * q + 4, :], bank[q][:, :].rearrange("p (a b) -> p a b", a=4), ACT.Copy).then_inc(r_ev, 1)
            act_e.wait_ge(sm_d, 1)
            sc.activation(L1, L0, ACT.Exp).then_inc(sm_a, 1)

            def high(e, u):
                if u % 2 == 0:
                    p = u // 2
                    act_e.wait_ge(ld_e[p % ESL], e * (16 * EPC // ESL) + 16 * (p // ESL + 1))
                act_e.wait_ge(e_used, e * EU + u + 1)
                sc.activation(e_unit[:, u % USL, 0, :], e_raw[:, (u // 2) % ESL, u % 2, :], ACT.Copy).then_inc(e_hi, 1)

            def xs_value():
                for k in range(KD // 2):
                    last = sc.activation(xs[:, k * P:(k + 1) * P], bank[4 + k // 4][:, (k % 4) * P:(k % 4 + 1) * P], ACT.Identity,
                                         bias=shift2[:, k:k + 1], scale=scale2[:, k:k + 1])
                last.then_inc(xs_vA, 1)

            def xs_high(n):
                act_e.wait_ge(xs_vA, n)
                act_e.wait_ge(xs_vD, n)
                sc.activation(xsT[:, 0], xs.rearrange("p (k t) -> p k t", k=KD), ACT.Copy).then_inc(xs_hi, 1)

            def expert(e, last):
                for u in range(EU):
                    if u == SIL:
                        act_e.wait_ge(e_used, e * EU + KD + USL)
                        for n in range(2):
                            ins = sc.activation(act[:, n * BN:(n + 1) * BN], bank[n][:, :], ACT.Silu)
                        ins.then_inc(g_act, 1)
                    if u == XV and not last:
                        act_e.wait_ge(xs_mm, e + 2)
                        xs_value()
                    if u == ACTP:
                        for n in range(2):
                            act_e.wait_ge(a_mm, e * 2 + n + 1)
                            sc.activation(actT[:, 0, 4 * n:4 * n + 4, :], bank[n][:, :].rearrange("p (a b) -> p a b", a=4),
                                          ACT.Copy).then_inc(a_hi, 1)
                    if u == XP and not last:
                        xs_high(e + 2)
                    high(e, u)

            act_e.wait_ge(xs_mm, 1)
            xs_value()
            xs_high(1)
            with act_e.Fori(0, EXP - 1) as e:
                expert(e, False)
            expert(EXP - 1, True)
            act_e.wait_ge(scattered, 16 * EXP)
            for i in range(NT):
                act_e.wait_ge(ld_f[i], 16)
                link(sc.activation(f_squares, ft[i], ACT.Square, accum_out=ssf[:, i:i + 1]))
                sc.activation(rsf[:, i:i + 1], ssf[:, i:i + 1], ACT.Sqrt, bias=eps, scale=1.0 / D).then_inc(f_sq, 1)

        @block.tensor
        def _(pe):
            te = nc.tensor

            def product(banks, a, b, first, last):
                for step, (p, q) in enumerate(((0, 0), (0, 1), (1, 0))):
                    for n in range(2):
                        ins = te.matmul(banks[n][:, :], a[p], b[:, q, n * BN:(n + 1) * BN],
                                        start=(first and step == 0), stop=(last and step == 2))
                return ins

            for u in range(OU):
                c2, k = u // KD, u % KD
                if c2 % 2 == 0 and k % 2 == 0:
                    pe.wait_ge(m_lo, (c2 // 2) * (KD // 2) + k // 2 + 1)
                pe.wait_ge(o_lo, u + 1)
                for i in range(4):
                    if k == 0 and c2:
                        pe.wait_ge(o_ev, 8 * (c2 - 1) + 2 * i + 2)
                    last = product(bank[2 * i:2 * i + 2], [mix[:, s, k, i * P:(i + 1) * P] for s in range(2)], o_unit[:, u % OUL],
                                   k == 0, k == KD - 1)
                last.then_inc(o_used, 1)
            pe.wait_ge(o_ev, 4 * 8)
            pe.wait_ge(wr_s, 1)
            for k in range(KD):
                last = te.matmul(bank[5][0:1, 0:EXP], shift2[:, k:k + 1], wr[:, k, :], start=(k == 0), stop=(k == KD - 1))
            last.then_inc(r_mm, 1)
            for i in range(NT):
                pe.wait_ge(x1_n, i + 1)
                for q in range(4):
                    if i:
                        pe.wait_ge(rt_ev if q % 2 else r_ev, 2 * (i - 1) + q // 2 + 1)
                    for k in range(4):
                        last = te.transpose(bank[q][:, k * P:(k + 1) * P], x1[:, i, (4 * q + k) * P:(4 * q + k + 1) * P], ident)
                    last.then_inc(r_tr, 1)
                pe.wait_ge(r_ev, 2 * i + 2)
                pe.wait_ge(rt_ev, 2 * i + 2)
                if i == 0:
                    pe.wait_ge(r_log, 1)
                for k in range(KD):
                    te.matmul(bank[4][:, i * EXP:(i + 1) * EXP], xnT[:, i % 2, k, :], wrs[:, k, :], start=(k == 0), stop=False)
                te.matmul(bank[4][:, i * EXP:(i + 1) * EXP], ones_row[0:1, :], lb[0:1, :], start=False, stop=True).then_inc(r_mm, 1)
            pe.wait_ge(sm_d, 2)
            for i in range(NT):
                last = te.transpose(bank[i // 4][0:EXP, (i % 4) * P:(i % 4 + 1) * P], L0[:, i, :], ident)
            last.then_inc(aff_mm, 1)
            pe.wait_ge(topk, 1)
            te.transpose(bank[2][:, 0:EXP], top_f[0:EXP, :], ident[0:EXP, 0:EXP]).then_inc(e_used, USL)
            te.transpose(bank[2][:, EXP:2 * EXP], top_v[0:EXP, :], ident[0:EXP, 0:EXP]).then_inc(topk_mm, 1)

            def transpose_xs():
                for k in range(KD):
                    last = te.transpose(bank[4 + k // 4][:, (k % 4) * P:(k % 4 + 1) * P], xs[:, k * P:(k + 1) * P], ident)
                last.then_inc(xs_mm, 1)

            def expert(e, final):
                pe.wait_ge(xs_lo, e + 1)
                for u in range(2 * KD):
                    half, k = u // KD, u % KD
                    if u == SIL and not final:
                        pe.wait_ge(gathered, e * 16 + 32)
                        pe.wait_ge(y_ev, e + 1)
                        transpose_xs()
                    pe.wait_ge(e_lo, e * EU + u + 1)
                    last = product(bank[2 * half:2 * half + 2], [xsT[:, s, k, :] for s in range(2)], e_unit[:, u % USL],
                                   k == 0, k == KD - 1)
                    last.then_inc(e_used, 1)
                pe.wait_ge(a_rdy, e + 1)
                for k in range(KF):
                    last = te.transpose(bank[k // 4][:, (k % 4) * P:(k % 4 + 1) * P], act[:, k * P:(k + 1) * P], ident)
                    if k % 4 == 3:
                        last.then_inc(a_mm, 1)
                if not final:
                    pe.wait_ge(xs_vA, e + 2)
                    pe.wait_ge(xs_vD, e + 2)
                else:
                    pe.wait_ge(y_ev, EXP)
                for u in range(2 * KD, EU):
                    k, half = (u - 2 * KD) // 2, u % 2
                    if half == 0 and k % 4 == 0:
                        pe.wait_ge(a_lo, e * 2 + k // 4 + 1)
                    pe.wait_ge(e_lo, e * EU + u + 1)
                    last = product(bank[4 + 2 * half:6 + 2 * half], [actT[:, s, k, :] for s in range(2)], e_unit[:, u % USL],
                                   k == 0, k == KF - 1)
                    last.then_inc(e_used, 1)

            pe.wait_ge(topk_ev, 1)
            pe.wait_ge(gathered, 16)
            transpose_xs()
            with pe.Fori(0, EXP - 1) as e:
                expert(e, False)
            expert(EXP - 1, True)

        @block.vector
        def _(dve):
            ve = nc.vector

            def link(ins):
                chains["dve"] += 1
                ins.then_inc(dv, 1)
                dve.wait_ge(dv, chains["dve"])

            def add_block(c2):
                th, ch = c2 // 2, c2 % 2
                dve.wait_ge(o_used, (c2 + 1) * KD)
                for b in range(8):
                    i, n = 4 * th + b // 2, 2 * ch + b % 2
                    link(ve.tensor_tensor(tmp[:, b % 2, :], bank[b][:, :], gate1_b[:, n * BN:(n + 1) * BN], ALU.mult))
                    xb = x1[:, i, n * BN:(n + 1) * BN]
                    ve.tensor_tensor(xb, xb, tmp[:, b % 2, :], ALU.add).then_inc(o_ev, 1)

            for u in range(OU):
                c2, k = u // KD, u % KD
                th, ch, q = c2 // 2, c2 % 2, u // 2
                if ch == 0 and k % 2 == 0:
                    m = th * (KD // 2) + k // 2
                    dve.wait_ge(m_hi, m + 1)
                    ve.tensor_tensor(mix[:, 1, k:k + 2, :], raw_m[:, m % MSL], mix[:, 0, k:k + 2, :].bitcast(fp32), ALU.subtract).then_inc(m_lo, 1)
                dve.wait_ge(o_hi, u + 1)
                ve.tensor_tensor(o_unit[:, u % OUL, 1, :], raw_w[:, q % OSL, u % 2, :], o_unit[:, u % OUL, 0, :].bitcast(fp32),
                                 ALU.subtract).then_inc(o_lo, 1)
                if u == KD + 1:
                    dve.wait_ge(ld_x1, 16)
                    dve.wait_ge(ld_g1, 16)
                if c2 and k == 1:
                    add_block(c2 - 1)
            add_block(3)
            dve.wait_ge(ld_r, 16)
            link(ve.scalar_tensor_tensor(scale2, scale2, 1.0, norm_col[:, 1, :], ALU.add, ALU.mult))
            for k in range(KD):
                last = ve.tensor_scalar(wrs[:, k, :], wr[:, k, :], scale2[:, k:k + 1], None, ALU.mult)
            last.then_inc(wr_s, 1)
            dve.wait_ge(r_mm, 1)
            ve.tensor_copy(lb[0:1, :], bank[5][0:1, 0:EXP]).then_inc(r_log, 1)
            for i in range(NT):
                dve.wait_ge(x1_sq, i + 1)
                link(ve.reciprocal(rs1[:, i:i + 1], rs1[:, i:i + 1]))
                dve.wait_ge(x1_st[i], 16)
                ve.tensor_scalar(x1[:, i, :], x1[:, i, :], rs1[:, i:i + 1], None, ALU.mult).then_inc(x1_n, 1)
                for q in (1, 3):
                    dve.wait_ge(r_tr, 4 * i + q + 1)
                    if i >= 2:
                        dve.wait_ge(r_mm, i)
                    ve.tensor_copy(xnT[:, i % 2, 4 * q:4 * q + 4, :], bank[q][:, :].rearrange("p (a b) -> p a b", a=4)).then_inc(rt_ev, 1)
            dve.wait_ge(r_mm, NT + 1)
            logits = bank[4][:, 0:NT * EXP].rearrange("p (a b) -> p a b", a=NT)
            link(ve.tensor_reduce(lst[:, 0, :], logits, AX.X, ALU.max))
            ve.tensor_tensor(L0, logits, lst[:, 0, :].unsqueeze(2).to_broadcast([P, NT, EXP]), ALU.subtract).then_inc(sm_d, 1)
            dve.wait_ge(sm_a, 1)
            link(ve.tensor_reduce(lst[:, 1, :], L1, AX.X, ALU.add))
            link(ve.reciprocal(lst[:, 1, :], lst[:, 1, :]))
            ve.tensor_tensor(L0, L1, lst[:, 1, :].unsqueeze(2).to_broadcast([P, NT, EXP]), ALU.mult).then_inc(sm_d, 1)
            dve.wait_ge(aff_mm, 1)
            for n in range(2):
                last = ve.tensor_copy(aff[0:EXP, n * BN:(n + 1) * BN], bank[n][0:EXP, :])
            link(last)
            for r in range(CAP // 8):
                best, at8 = top_v[0:EXP, 8 * r:8 * r + 8], top_i[0:EXP, 8 * r:8 * r + 8]
                link(ve.max(best, aff[0:EXP, :]))
                ve.max_index(at8, best, aff[0:EXP, :])
                if r < CAP // 8 - 1:
                    link(ve.match_replace(aff[0:EXP, :], best, aff[0:EXP, :], -1.0))
            link(ve.memset(small[:, 121:122], 0.0))
            ve.tensor_copy(top_f[0:EXP, :], top_i[0:EXP, :]).then_inc(topk, 1)
            dve.wait_ge(topk_mm, 1)
            ve.tensor_copy(idx_all[:, 0:EXP], bank[2][:, 0:EXP])
            ve.tensor_copy(idx_all[:, EXP:EXP + 1], bank[2][:, 0:1])
            ve.tensor_copy(gate_all[:, 0:EXP], bank[2][:, EXP:2 * EXP])
            link(ve.tensor_copy(gate_all[:, EXP:EXP + 1], bank[2][:, EXP:EXP + 1]))
            ve.tensor_copy(idx_gather, idx_all[:, 0:1]).then_inc(idx_r, 1)
            ve.memset(small[:, 122:123], 0.0).then_inc(topk_ev, 1)
            ve.memset(small[:, 124:125], 0.0).then_inc(y_ev, 1)

            def low(e, u):
                dve.wait_ge(e_hi, e * EU + u + 1)
                ve.tensor_tensor(e_unit[:, u % USL, 1, :], e_raw[:, (u // 2) % ESL, u % 2, :], e_unit[:, u % USL, 0, :].bitcast(fp32),
                                 ALU.subtract).then_inc(e_lo, 1)

            def xs_value():
                for k in range(KD // 2, KD):
                    last = ve.tensor_scalar(xs[:, k * P:(k + 1) * P], bank[4 + k // 4][:, (k % 4) * P:(k % 4 + 1) * P],
                                            scale2[:, k:k + 1], shift2[:, k:k + 1], ALU.mult, ALU.add)
                last.then_inc(xs_vD, 1)

            def xs_low(n):
                dve.wait_ge(xs_hi, n)
                ve.tensor_tensor(xsT[:, 1], xs.rearrange("p (k t) -> p k t", k=KD), xsT[:, 0].bitcast(fp32), ALU.subtract).then_inc(xs_lo, 1)

            def results(e):
                dve.wait_ge(y_free, e + 1)
                ve.memset(small[:, 123:124], 0.0)
                ve.tensor_copy(idx_scatter, idx_all[:, bass.ds(e, 1)])
                ve.tensor_copy(gate_now, gate_all[:, bass.ds(e, 1)]).then_inc(cols_set, 1)
                dve.wait_ge(cols_set, e + 1)
                dve.wait_ge(e_used, e * EU + EU + USL)
                for n in range(NB):
                    last = ve.scalar_tensor_tensor(y[:, n * BN:(n + 1) * BN], bank[4 + n][:, :], gate_now,
                                                   gate2_b[:, n * BN:(n + 1) * BN], ALU.mult, ALU.mult)
                last.then_inc(y_ev, 1)

            def expert(e, final):
                for u in range(AHEAD, EU + 1):
                    if u == XV and not final:
                        dve.wait_ge(xs_mm, e + 2)
                        xs_value()
                    if u == ACTP:
                        dve.wait_ge(g_act, e + 1)
                        dve.wait_ge(e_used, e * EU + 2 * KD + USL)
                        for n in range(2):
                            a_half = act[:, n * BN:(n + 1) * BN]
                            last = ve.tensor_tensor(a_half, a_half, bank[2 + n][:, :], ALU.mult)
                        last.then_inc(a_rdy, 1)
                        for n in range(2):
                            dve.wait_ge(a_hi, e * 2 + n + 1)
                            ve.tensor_tensor(actT[:, 1, 4 * n:4 * n + 4, :], bank[n][:, :].rearrange("p (a b) -> p a b", a=4),
                                             actT[:, 0, 4 * n:4 * n + 4, :].bitcast(fp32), ALU.subtract).then_inc(a_lo, 1)
                    if u == XP and not final:
                        xs_low(e + 2)
                        ve.memset(small[:, 123:124], 0.0)
                        ve.tensor_copy(idx_gather, idx_all[:, bass.ds(e + 2, 1)]).then_inc(idx_r, 1)
                    if u < EU:
                        low(e, u)
                if not final:
                    for u in range(AHEAD):
                        low(e + 1, u)
                results(e)

            dve.wait_ge(xs_mm, 1)
            xs_value()
            xs_low(1)
            ve.tensor_copy(idx_gather, idx_all[:, 1:2]).then_inc(idx_r, 1)
            dve.wait_ge(ld_g2, 16)
            for u in range(AHEAD):
                low(0, u)
            with dve.Fori(0, EXP - 1) as e:
                expert(e, False)
            expert(EXP - 1, True)
            dve.wait_ge(ld_nf, 16)
            for i in range(NT):
                dve.wait_ge(f_sq, i + 1)
                link(ve.reciprocal(rsf[:, i:i + 1], rsf[:, i:i + 1]))
                ve.scalar_tensor_tensor(ft[i], ft[i], rsf[:, i:i + 1], normf_b, ALU.mult, ALU.mult).then_inc(f_out, 1)
        stage.close()


def inverse_counts():
    import numpy as np
    grid_w, rows = 64, 16
    out = np.zeros((4, rows * grid_w), np.float32)
    for g, w in enumerate((2, 4, 8, 16)):
        def count(n):
            t = np.arange(n)
            return np.minimum(t + w // 2, n) - np.maximum(t - w // 2, 0)
        out[g] = (1.0 / (count(rows)[:, None] * count(grid_w)[None, :])).reshape(-1)
    return out


_INS = ["x", "c", "ctx", "c_ctx", "w_mod", "b_mod", "norm1", "w_in", "conv_q_w", "conv_k_w", "b_gates", "head_g",
        "pool_w", "pool_scale", "w_out", "norm2", "w_router", "w_gate", "w_up", "w_down", "norm_f"]


def kernel(**inputs):
    import numpy as _np
    import concourse.bacc as _bacc
    from concourse import mybir as _mybir
    from concourse.bass_utils import run_bass_kernel_spmd as _run

    nc = _bacc.Bacc("TRN2", target_bir_lowering=False, num_devices=1)
    arrays, args = {}, []
    for name in _INS + ["inv_count"]:
        a = inverse_counts() if name == "inv_count" else _np.ascontiguousarray(inputs[name])
        arrays[f"in_{name}_dram"] = a
        args.append(nc.dram_tensor(f"in_{name}_dram", a.shape, _mybir.dt.from_np(a.dtype), kind="ExternalInput").ap())
    shape = inputs["x"].shape
    args.append(nc.dram_tensor("out_0_dram", shape, _mybir.dt.float32, kind="ExternalOutput").ap())
    hybrid_layer_kernel(nc, *args)
    r = _run(nc, [arrays], core_ids=[0])
    return r.results[0]["out_0_dram"]
```

```python
import concourse.bass as bass
from concourse import mybir
from contextlib import ExitStack


def hybrid_layer_kernel(nc, x, c, ctx, c_ctx, w_mod, b_mod, norm1, w_in, conv_q_w, conv_k_w, b_gates,
                        head_g, pool_w, pool_scale, w_out, norm2, w_router, w_gate, w_up, w_down, norm_f,
                        inv_count, out):
    fp32, fp32r, u32 = mybir.dt.float32, mybir.dt.float32r, mybir.dt.uint32
    ALU, ACT, AX = mybir.AluOpType, mybir.ActivationFunctionType, mybir.AxisListType

    P = 128
    T, D = x.shape[1], x.shape[2]
    TC = ctx.shape[1]
    KD = D // P
    NT, NC = T // P, TC // P
    NTT = NT + NC
    H = 4
    DV, DQK = 256, 128
    MW = H * DV
    PW = D - MW
    NG = 4
    GC = PW // NG
    GRID_W = 64
    ROWS = T // GRID_W
    WINDOWS = (2, 4, 8, 16)
    K_OFF, V_OFF = 0, H * DQK
    G_OFF = V_OFF + MW
    Q_OFF = G_OFF + 16
    O_OFF = Q_OFF + H * DQK
    P_OFF = O_OFF + MW
    TAPS = 5
    NMOD = 6
    EXP = w_router.shape[2]
    CAP = 2 * T // EXP
    F = w_gate.shape[3]
    KF = F // P
    EPS = 1e-6
    KSCALE = float(DQK) ** -0.5
    BN = 512
    NB = D // BN
    OSL, MSL, OUL = 2, 2, 4
    ESL, USL = 8, 8

    PADC = 2
    RAWN = 3 * PADC + TC + T
    CONVN = RAWN - 2 * PADC
    LAT0 = TC + PADC
    GR = 36
    LAST = (P - 1, 0)

    def chunk_of(d, j):
        if d == 0:
            return j
        return NC - 1 - j if j < NC else NTT - 1 - (j - NC)

    def mod_pieces(i):
        return range(2 * KD * i // NTT, 2 * KD * (i + 1) // NTT)

    MACP = KD // 2
    MACS = (NMOD - 2) * NB * MACP
    groups, order, summed, macs = [], [], [], [0]

    def add_group(kind, *what):
        groups.append((kind, *what))
        order.append(("group", len(groups) - 1))
        if kind in ("T", "M"):
            return
        if summed:
            groups.append(("R", summed.pop()))
            order.append(("group", len(groups) - 1))
        for _ in range(0 if kind in "KQ" and what[0] == 0 else 2):
            if macs[0] < MACS and not summed:
                order.append(("mac", macs[0]))
                macs[0] += 1
                if macs[0] % MACP == 0:
                    summed.append(macs[0] // MACP - 1)

    def add_step(h, i):
        if i >= 1 and i <= NTT:
            order.append(("B", h, i - 1))
        if i < NTT:
            order.append(("A", h, i))

    def after_group(h, i):
        if h < 0:
            return
        if i <= NTT:
            add_step(h, i)
        if i == NTT + 1:
            order.append(("normalise", h))
        if i == NTT + 3:
            for ft in range(2):
                for half in range(2):
                    add_group("T", h, ft, half)
            order.append(("store_mix", h))

    for h in range(H):
        i = 0
        KQ = [("K", h, 0), ("K", h, 1), ("K", h, 2), ("Q", h, 0), ("Q", h, 1)]
        VS = [("V", h, t) for t in range(NTT)]
        for what in (KQ + VS if h else VS + KQ) + [("O", h, ft, half) for ft in range(2) for half in range(2)]:
            add_group(*what)
            if what == ("V", 0, NTT - 1):
                order.append(("gate_rows",))
            if what[:1] + what[2:] == ("K", 2):
                order.append(("conv", h, 0))
            if what[:1] + what[2:] == ("Q", 1):
                order.append(("conv", h, 1))
                order.append(("silu", h, 0))
            if what[:1] + what[2:] == (("V", 1) if h else ("O", 0, 0)):
                order.append(("silu", h, 1))
            if what == ("Q", 0, 1):
                order.append(("gate_columns",))
            after_group(h - 1, i)
            i += 1
    assert macs[0] == MACS and not summed
    i = 0
    for g in range(NG):
        for a in range(2):
            for half in range(2):
                add_group("P", g, a, half)
                if half == 1:
                    order.append(("pool", g, a))
                if g > 0 and (a, half) == (0, 0):
                    for fo in range(2):
                        for m_half in range(2):
                            add_group("M", g - 1, fo, m_half)
                    order.append(("store_pool", g - 1))
                after_group(H - 1, i)
                i += 1
    for fo in range(2):
        for half in range(2):
            add_group("M", NG - 1, fo, half)
    order.append(("store_pool", NG - 1))

    evac, counts = [], [0, 0]
    for g in groups:
        dve = int(g[0] == "T")
        counts[dve] += 1
        evac.append((dve, counts[dve]))
    group_no = {g: n for n, g in enumerate(groups)}

    POOL_ORDER = (3, 2, 1, 0)
    slots = [(kind, h) for h in range(H) for kind in ("KQ", "V", "O") if (kind, h) != ("V", 0)] + [("P", g) for g in range(NG)]
    slot_no = {s: n for n, s in enumerate(slots)}
    SLOTC = 256
    slot_of = {"K": "KQ", "Q": "KQ", "V": "V", "O": "O", "P": "P"}
    last_group = {}
    for n, g in enumerate(groups):
        if g[0] in slot_of and g[:2] != ("V", 0):
            last_group[slot_no[(slot_of[g[0]], g[1])]] = n

    mod_scr = nc.dram_tensor("mod_scr", [NMOD, 2, D], fp32).ap()
    mix_scr = nc.dram_tensor("mix_scr", [D, T], fp32).ap()
    x1_scr = nc.dram_tensor("x1_scr", [T, D], fp32).ap()
    xn_scr = nc.dram_tensor("xn_scr", [T, D], fp32).ap()

    x_t = x[0].rearrange("(n p) d -> n p d", p=P)
    ctx_t = ctx[0].rearrange("(n p) d -> n p d", p=P)
    w_in_v = w_in[0].rearrange("(k p) n -> p k n", p=P)
    w_mod_v = w_mod[0].rearrange("(p k) n -> p k n", k=KD)
    mix_v = mix_scr.rearrange("(k p) t -> p k t", p=P)
    x1_t = x1_scr.rearrange("(n p) d -> n p d", p=P)
    xn_t = xn_scr.rearrange("(n p) d -> n p d", p=P)
    out_t = out[0].rearrange("(n p) d -> n p d", p=P)

    es = ExitStack()
    with es:
        es.enter_context(nc.allow_non_contiguous_dma(reason="vectors laid out over the partitions"))

        def sem(name):
            return es.enter_context(nc.semaphore(name))

        SBUF = 53200
        KEPT = 2 * P + 128 + 10 * KD
        arena = es.enter_context(nc.sbuf_tensor("kept", [P, KEPT], fp32))
        at = [0]

        def carve(v, dims):
            if len(dims) == 2:
                return v.rearrange("p (a b) -> p a b", a=dims[0])
            if len(dims) == 3:
                return v.rearrange("p (a b c) -> p a b c", a=dims[0], b=dims[1])
            return v

        def take(n, *dims):
            at[0] += n
            return carve(arena[:, at[0] - n:at[0]], dims)

        def view(lo, *dims):
            n = 1
            for v in dims:
                n *= v
            return carve(arena[:, lo:lo + n], dims)

        ident = take(P)
        small = take(128)
        ones_row = take(P)
        shift1, scale1 = take(2 * KD, 2, KD), take(2 * KD, 2, KD)
        shift2, scale2 = take(KD), take(KD)
        norm_col = take(2 * KD, 2, KD)
        cc = take(2 * KD, 2, KD)
        assert at[0] <= KEPT
        stage = ExitStack()
        ARENA = SBUF - KEPT
        arena = stage.enter_context(nc.sbuf_tensor("stage1", [P, ARENA], fp32))
        at[0] = top = 0
        hT = take(KD * T, KD, T)
        hcT = take(KD * TC, KD, TC)
        ring = take(2 * KD * SLOTC, 2, KD, SLOTC)
        kT = take(2 * CONVN, 2, CONVN)
        qT = take(2 * T, 2, T)
        v_off = at[0]
        V = take(2 * NTT * (DV + 1), 2, NTT, DV + 1)
        raw = take(RAWN)
        sig_o = take(2 * T, 2, T)
        h_sum = take(NT * DV, NT, DV)
        Dm, WI, Pm, qw, kw = (take(2 * P, 2, P) for _ in range(5))
        C = take(4 * (DV + 1), 2, 2, DV + 1)
        MxN = take(NTT * P)
        sel = take(8 * P, 8, P)
        Acol = take(NTT * GR, NTT, GR)
        EM = take(NTT * GR, NTT, GR)
        mp_col = take(8 * NTT, 8, NTT)
        conv_w = take(2 * H * TAPS, 2, H, TAPS)
        headg_col = take(2 * H)
        pscale_col = take(2 * NG)
        pmix = take(2 * T, 2, T)
        poolw = take(2 * GC, 2, GC)
        row_sum = take(BN)
        assert at[0] <= ARENA, at[0]

        o = v_off
        xt = view(o, 2, D)
        o = top + KD * T + KD * TC
        mod_ring = view(o, 4, D)
        o += 4 * D
        mod_row = view(o, 2, D)
        assert 2 * D <= 2 * CONVN + 2 * T
        GN = NTT * P
        assert 2 * GN <= NTT * (DV + 1) and GN <= CONVN and GN <= 2 * T
        v1 = v_off + NTT * (DV + 1)
        LI, LF = view(v1, GN), view(v1 + GN, GN)
        GB = kT[:, 1, 0:GN]
        GX = sig_o.rearrange("p a b -> p (a b)")[:, 0:GN]
        h_flat = h_sum.rearrange("p a b -> p (a b)")
        g_tok = h_flat[:, 0:NTT * P].rearrange("p (t c) -> p t c", t=NTT)
        VG = DV + 16
        w_vg = view(v1, KD, VG)
        assert KD * VG <= NTT * (DV + 1) + RAWN + 2 * T
        reset = h_flat[:, 0:GN]
        mac_ring = pmix.rearrange("p a b -> p (a b)").rearrange("p (s k n) -> p s k n", s=2, k=2)
        mac_sum = poolw.rearrange("p a b -> p (a b)")
        assert mac_sum.shape[1] == BN
        PADG = 8
        HW_ = GRID_W + 2 * PADG
        HR = ROWS + 2 * PADG
        o = top + KD * T
        pool_v = [view(o, HR, GRID_W), view(o + HR * GRID_W, HR, GRID_W)]
        o = top + KD * T + KD * TC + 2 * KD * SLOTC
        pool_h0 = view(o, ROWS, HW_)
        assert ROWS * HW_ <= CONVN
        pool_h1 = view(v_off, ROWS, HW_)
        o = v_off + ROWS * HW_
        inv_b = view(o, T)
        assert ROWS * HW_ + T <= NTT * (DV + 1)
        dT = [qT[:, 0, :], raw[:, 0:T]]

        bank = [es.enter_context(nc.psum_tensor(f"bank{n}", [P, BN], fp32)) for n in range(8)]
        PR = bank[0:2]
        A_b, N_b, C_b = bank[2:4], bank[4:6], bank[6:8]

        ld_c = sem("ld_c")
        ld_const = sem("ld_const")
        ld_x = [sem(f"ld_x_{n}") for n in range(2)]
        consts = sem("consts")
        x_stat = sem("x_stat")
        x_scaled = sem("x_scaled")
        x_tr = sem("x_tr")
        x_evA, x_evD = sem("x_evA"), sem("x_evD")
        silu_c = sem("silu_c")
        ld_mod = [sem(f"ld_mod_{n}") for n in range(4)]
        mod_used = sem("mod_used")
        ld_bmod = sem("ld_bmod")
        mod_sum = sem("mod_sum")
        mod_col = sem("mod_col")
        s1_ready = sem("s1_ready")
        h_readyA, h_readyD = sem("h_readyA"), sem("h_readyD")
        ld_mac = [sem(f"ld_mac_{n}") for n in range(2)]
        mac_used = sem("mac_used")
        row_bias, row_st = sem("row_bias"), sem("row_st")
        ld_cols = sem("ld_cols")
        ld_vg, ld_bg = sem("ld_vg"), sem("ld_bg")
        gate_mm = sem("gate_mm")
        raw_clear = sem("raw_clear")
        gate_ev = sem("gate_ev")
        gact = sem("gact")
        grow = sem("grow")
        gcol_mm = sem("gcol_mm")
        gcols = sem("gcols")
        gfree = sem("gfree")
        ld_w = [sem(f"ld_w_{n}") for n in range(2)]
        grp = sem("grp")
        evA, evD = sem("evA"), sem("evD")
        conv_done = sem("conv_done")
        silu_done = sem("silu_done")
        stA = [sem(f"stA_{d}") for d in range(2)]
        expd = [sem(f"expd_{d}") for d in range(2)]
        masked = [sem(f"masked_{d}") for d in range(2)]
        fac = [sem(f"fac_{d}") for d in range(2)]
        stB = [sem(f"stB_{d}") for d in range(2)]
        cup = [sem(f"cup_{d}") for d in range(2)]
        hsq = sem("hsq")
        hrs = sem("hrs")
        hnorm = sem("hnorm")
        mix_st = sem("mix_st")
        pool_d = sem("pool_d")
        ld_pool = sem("ld_pool")
        pmix_st = sem("pmix_st")
        ld_x1, ld_g1 = sem("ld_x1"), sem("ld_g1")
        ld_mix = [sem(f"ld_mix_{n}") for n in range(MSL)]
        ld_wo = [sem(f"ld_wo_{n}") for n in range(OSL)]
        m_hi, m_lo = sem("m_hi"), sem("m_lo")
        o_hi, o_lo = sem("o_hi"), sem("o_lo")
        o_used = sem("o_used")
        o_tile = sem("o_tile")
        o_ev = sem("o_ev")
        x1_st = [sem(f"x1_st_{n}") for n in range(NT)]
        x1_sq = sem("x1_sq")
        x1_n = sem("x1_n")
        xn_st = sem("xn_st")
        ld_r = sem("ld_r")
        wr_s = sem("wr_s")
        r_bias, r_mm = sem("r_bias"), sem("r_mm")
        r_ev = sem("r_ev")
        r_tr = sem("r_tr")
        rt_ev = sem("rt_ev")
        r_log = sem("r_log")
        sm_a, sm_d = sem("sm_a"), sem("sm_d")
        aff_mm = sem("aff_mm")
        topk = sem("topk")
        topk_mm, topk_ev = sem("topk_mm"), sem("topk_ev")
        idx_r = sem("idx_r")
        ld_g2 = sem("ld_g2")
        ld_e = [sem(f"ld_e_{n}") for n in range(ESL)]
        e_hi, e_lo = sem("e_hi"), sem("e_lo")
        e_used = sem("e_used")
        cols_set = sem("cols_set")
        gathered, scattered = sem("gathered"), sem("scattered")
        xs_mm = sem("xs_mm")
        xs_vA, xs_vD = sem("xs_vA"), sem("xs_vD")
        xs_hi, xs_lo = sem("xs_hi"), sem("xs_lo")
        g_act, a_rdy = sem("g_act"), sem("a_rdy")
        a_mm, a_hi, a_lo = sem("a_mm"), sem("a_hi"), sem("a_lo")
        y_ev, y_free = sem("y_ev"), sem("y_free")
        ld_nf = sem("ld_nf")
        ld_f = [sem(f"ld_f_{n}") for n in range(NT)]
        f_sq, f_out = sem("f_sq"), sem("f_out")
        out_st = sem("out_st")
        passed_sp, passed_pool = sem("passed_sp"), sem("passed_pool")
        dv, ac = sem("dv"), sem("ac")
        chains = {"dve": 0, "act": 0}

        H_DVE = 11
        ssx, rsx = small[:, 0:16], small[:, 16:32]
        bg = small[:, 32:33]
        one = small[:, 33:34]
        ones_col = ones_row[:, 0:1]
        den = small[:, 34:36]
        ssh, rsh = small[:, 40:48], small[:, 48:56]
        mpr = small[:, 56:56 + NTT + 1]
        ss1, rs1 = small[:, 72:80], small[:, 80:88]
        ssf, rsf = small[:, 88:96], small[:, 96:104]
        eps = small[:, 104:105]

        block = stage.enter_context(nc.Block())

        @block.sync
        def _(sp):
            for i in range(NTT):
                if i >= 2:
                    sp.wait_ge(x_evA, 2 * (i - 1))
                    sp.wait_ge(x_evD, 2 * (i - 1))
                if i:
                    sp.dma_start(xt[:, i % 2, :], ctx_t[i] if i < NC else x_t[i - NC]).then_inc(ld_x[i % 2], 16)
                for n in mod_pieces(i):
                    if n == 1:
                        sp.dma_start(xt[:, 0, :], ctx_t[0]).then_inc(ld_x[0], 16)
                    if n >= 4:
                        sp.wait_ge(mod_used, n - 3)
                    sp.dma_start(mod_ring[:, n % 4, :], w_mod_v[:, n % KD, (n // KD) * D:(n // KD + 1) * D]).then_inc(ld_mod[n % 4], 16)
            slot_after = {last_group[n]: n + 2 for n in range(len(slots) - 2)}

            def load_slot(n):
                kind, h = slots[n]
                dst = ring[:, n % 2]
                if kind == "KQ":
                    sp.dma_start(dst[:, :, 0:DQK], w_in_v[:, :, K_OFF + h * DQK:K_OFF + (h + 1) * DQK]).then_inc(ld_w[n % 2], 16)
                    sp.dma_start(dst[:, :, DQK:2 * DQK], w_in_v[:, :, Q_OFF + h * DQK:Q_OFF + (h + 1) * DQK]).then_inc(ld_w[n % 2], 16)
                else:
                    off = {"V": V_OFF, "O": O_OFF, "P": P_OFF}[kind] + (POOL_ORDER[h] if kind == "P" else h) * SLOTC
                    sp.dma_start(dst, w_in_v[:, :, off:off + SLOTC]).then_inc(ld_w[n % 2], 32)

            def load_mac(n):
                b, k = n // MACP, 2 * (n % MACP)
                sp.dma_start(mac_ring[:, n % 2], w_mod_v[:, k:k + 2, 2 * D + b * BN:2 * D + (b + 1) * BN]).then_inc(ld_mac[n % 2], 16)

            sp.wait_ge(x_evA, 2 * NTT)
            sp.wait_ge(x_evD, 2 * NTT)
            sp.dma_start(w_vg[:, :, 0:DV], w_in_v[:, :, V_OFF:V_OFF + DV]).then_inc(ld_vg, 16)
            sp.dma_start(w_vg[:, :, DV:VG], w_in_v[:, :, G_OFF:G_OFF + 16]).then_inc(ld_vg, 16)
            sp.wait_ge(mod_used, 2 * KD)
            load_slot(0)
            load_slot(1)
            load_mac(0)
            load_mac(1)
            for item in order:
                if item[0] == "group" and item[1] in slot_after:
                    sp.wait_ge(grp, item[1] + 1)
                    load_slot(slot_after[item[1]])
                elif item[0] == "mac" and item[1] + 2 < MACS:
                    sp.wait_ge(mac_used, item[1] + 1)
                    load_mac(item[1] + 2)
            sp.wait_ge(mix_st, 16 * H)
            sp.wait_ge(pmix_st, 16 * (NG - 1))
            sp.wait_ge(row_st, 16 * (NMOD - 2) * NB)
            sp.wait_ge(ld_cols, 32)

        @block.gpsimd
        def _(pool):
            eng = nc.gpsimd
            eng.memset(ident, 0.0)
            eng.memset(ones_row, 1.0)
            eng.memset(sel, 0.0)
            eng.memset(small, 0.0).then_inc(consts, 1)
            pool.wait_ge(consts, 1)
            eng.memset(one, 1.0)
            eng.memset(eps, EPS)
            eng.affine_select(out=ident, in_=ident, compare_op=ALU.not_equal, fill=1.0, base=0,
                              pattern=[[-1, P]], channel_multiplier=1)
            s4 = sel.rearrange("p (d h) n -> p d h n", d=2)
            eng.affine_select(out=s4, in_=s4, compare_op=ALU.not_equal, fill=-1.0, base=0,
                              pattern=[[-32, 2], [-1, 4], [0, P]], channel_multiplier=1).then_inc(consts, 1)
            eng.memset(g_tok, 0.0).then_inc(consts, 1)
            for n, col in enumerate((0, 8, 4, 12)):
                eng.dma_start(bg[32 * n:32 * n + 4, :], b_gates[0, col:col + 4].rearrange("(p a) -> p a", a=1)).then_inc(ld_bg, 16)
            for m in range(2):
                eng.dma_start(mod_row[0:2, m, :], b_mod[0:1, m * D:(m + 1) * D].to_broadcast([2, D])).then_inc(ld_bmod, 16)
            eng.dma_start(mod_scr[2:NMOD, 0, :], b_mod[0, 2 * D:NMOD * D].rearrange("(m d) -> m d", m=NMOD - 2)).then_inc(row_bias, 16)
            pool.wait_ge(row_bias, 16)
            last = {("store_mix", h): group_no[("T", h, 1, 1)] for h in range(H)}
            last.update({("store_pool", g): group_no[("M", g, 1, 1)] for g in range(NG)})
            for item in order:
                if item[0] == "store_mix":
                    h = item[1]
                    pool.wait_ge(evD, evac[last[item]][1])
                    eng.dma_start(mix_v[:, 2 * h:2 * h + 2, :], sig_o).then_inc(mix_st, 16)
                elif item[0] == "store_pool":
                    g = item[1]
                    pool.wait_ge(evA, evac[last[item]][1])
                    k = 2 * (H + POOL_ORDER[g])
                    eng.dma_start(mix_v[:, k:k + 2, :], pmix).then_inc(pmix_st, 16)
                elif item[0] == "group" and groups[item[1]][0] == "R":
                    b = groups[item[1]][1]
                    pool.wait_ge(evA, evac[item[1]][1])
                    eng.dma_start(mod_scr[2 + b // NB, 0:1, (b % NB) * BN:(b % NB + 1) * BN], row_sum[0:1, :],
                                  accum_op=ALU.add).then_inc(row_st, 16)
                    if b == (NMOD - 2) * NB - 1:
                        pool.wait_ge(row_st, 16 * (NMOD - 2) * NB)
                        eng.dma_start(shift2, mod_scr[3, 0, :].rearrange("(k p) -> p k", p=P)).then_inc(ld_cols, 16)
                        eng.dma_start(scale2, mod_scr[4, 0, :].rearrange("(k p) -> p k", p=P)).then_inc(ld_cols, 16)
                elif item[0] == "A" and item[2] >= NC:
                    _, h, j = item
                    for d in range(2):
                        pool.wait_ge(expd[d], h * NTT + j + 1)
                        eng.affine_select(out=Dm[:, d, :], in_=Dm[:, d, :], compare_op=ALU.is_ge, fill=0.0, base=0,
                                          pattern=[[1 - 2 * d, P]], channel_multiplier=2 * d - 1).then_inc(masked[d], 1)
                elif item[0] == "pool" and item[2] == 0:
                    g = item[1]
                    if g == 0:
                        pool.wait_ge(stB[0], (H - 1) * NTT)
                        pool.wait_ge(stB[1], (H - 1) * NTT)
                    else:
                        pool.wait_ge(pool_d, 2 * g)
                        pool.wait_ge(grp, group_no[("M", g - 1, 1, 1)] + 1)
                    eng.dma_start(inv_b, inv_count[POOL_ORDER[g]:POOL_ORDER[g] + 1, :].to_broadcast([P, T])).then_inc(ld_pool, 16)
                    eng.dma_start(poolw, pool_w[0, POOL_ORDER[g]].rearrange("(k p) n -> p k n", p=P)).then_inc(ld_pool, 16)

        @block.scalar
        def _(act_e):
            sc = nc.scalar

            def link(ins):
                chains["act"] += 1
                ins.then_inc(ac, 1)
                act_e.wait_ge(ac, chains["act"])

            sc.dma_start(cc[:, 0, :], c[0].rearrange("(p k) -> p k", k=KD)).then_inc(ld_c, 16)
            sc.dma_start(cc[:, 1, :], c_ctx.rearrange("(p k) -> p k", k=KD)).then_inc(ld_c, 16)
            act_e.wait_ge(ld_c, 32)
            sc.activation(cc[:, :, :], cc[:, :, :], ACT.Silu).then_inc(silu_c, 1)
            act_e.wait_ge(consts, 2)
            for i in range(NTT):
                if i == 2:
                    sc.dma_start(norm_col[:, 0, :], norm1[0].rearrange("(k p) -> p k", p=P)).then_inc(ld_const, 16)
                    sc.dma_start(norm_col[:, 1, :], norm2[0].rearrange("(k p) -> p k", p=P)).then_inc(ld_const, 16)
                    for n, w in enumerate((conv_k_w, conv_q_w)):
                        for h in range(H):
                            sc.dma_start(conv_w[:, n, h, :], w[0, :, h * DQK:(h + 1) * DQK].rearrange("j p -> p j")).then_inc(ld_const, 16)
                    sc.dma_start(headg_col, head_g[0].rearrange("(k p) -> p k", p=P)).then_inc(ld_const, 16)
                    sc.dma_start(pscale_col, pool_scale[0].rearrange("(k p) -> p k", p=P)).then_inc(ld_const, 16)
                act_e.wait_ge(ld_x[i % 2], 16 * (i // 2 + 1))
                link(sc.activation(sig_o.rearrange("p a b -> p (a b)"), xt[:, i % 2, :], ACT.Square, accum_out=ssx[:, i:i + 1]))
                sc.activation(rsx[:, i:i + 1], ssx[:, i:i + 1], ACT.Sqrt, bias=eps, scale=1.0 / D).then_inc(x_stat, 1)
                for q in (0, 2):
                    act_e.wait_ge(x_tr, 4 * i + q + 1)
                    dst = hcT[:, 4 * q:4 * q + 4, i * P:(i + 1) * P] if i < NC else hT[:, 4 * q:4 * q + 4, (i - NC) * P:(i - NC + 1) * P]
                    sc.activation(dst, bank[4 + q][:, :].rearrange("p (a b) -> p a b", a=4), ACT.Copy).then_inc(x_evA, 1)
            act_e.wait_ge(s1_ready, 1)
            act_e.wait_ge(x_evD, 2 * NTT)
            act_e.wait_ge(x_evA, 2 * NTT)
            for k in range(H_DVE, KD):
                sc.activation(hT[:, k, :], hT[:, k, :], ACT.Identity, bias=shift1[:, 0, k:k + 1],
                              scale=scale1[:, 0, k:k + 1]).then_inc(h_readyA, 1)

            for item in order:
                if item[0] == "gate_rows":
                    act_e.wait_ge(grow, 1)
                    act_e.wait_ge(ld_bg, 16 * 4)
                    for n, (lo, w) in enumerate(((0, TC), (TC, BN), (TC + BN, BN))):
                        act_e.wait_ge(gate_mm, n + 1)
                        pb = bank[2 + n]
                        for j, dst in ((0, LI), (2, LF)):
                            f, b = 32 * j, 32 * j + 32
                            sc.activation(dst[0:4, lo:lo + w], pb[f:f + 4, 0:w], ACT.Identity, bias=bg[f:f + 4, :])
                            if lo == 0:
                                rev = dst[32:36, 0:TC][:, ::-1]
                            else:
                                r0 = TC + T - (lo - TC) - w
                                rev = dst[32:36, r0:r0 + w][:, ::-1]
                            last = sc.activation(rev, pb[b:b + 4, 0:w], ACT.Identity, bias=bg[b:b + 4, :])
                        last.then_inc(gate_ev, 1)
                    act_e.wait_ge(gact, 1)
                    link(sc.activation(GX[0:GR], GX[0:GR], ACT.Exp, scale=-1.0))
                    sc.activation(GX[0:GR], GX[0:GR], ACT.Ln, bias=one[0:GR, :]).then_inc(gact, 1)
                elif item[0] == "gate_columns":
                    act_e.wait_ge(gcol_mm, 1)
                    sc.activation(EM, bank[6][:, 0:NTT * GR].rearrange("p (a b) -> p a b", a=NTT), ACT.Exp, scale=-1.0).then_inc(gcols, 1)
                elif item[0] == "group":
                    g = item[1]
                    kind, h = groups[g][0:2]
                    if kind == "T":
                        continue
                    par = h % 2
                    if kind == "K" and groups[g][2] == 0 and h:
                        act_e.wait_ge(conv_done, 2 * h)
                    if kind == "Q" and groups[g][2] == 0:
                        act_e.wait_ge(conv_done, 2 * h + 1)
                    if kind == "O" and h >= 1 and groups[g][2:] == (0, 0):
                        act_e.wait_ge(mix_st, 16 * h)
                    if kind == "K" and (h, groups[g][2]) == (0, 0):
                        act_e.wait_ge(raw_clear, 1)
                    if kind == "O" and (h, groups[g][2:]) == (0, (0, 0)):
                        act_e.wait_ge(gcol_mm, 1)
                    if kind == "V" and (h, groups[g][2]) == (1, 0):
                        act_e.wait_ge(gcols, 4)
                    if kind == "R" and h >= 1:
                        act_e.wait_ge(row_st, 16 * h)
                    if kind == "V" and groups[g][2] == 0 and h >= 2:
                        for d in range(2):
                            act_e.wait_ge(stB[d], (h - 1) * NTT)
                    if kind == "P" and groups[g][2:] == (0, 0) and h == 0:
                        act_e.wait_ge(gfree, 1)
                    if kind == "P" and groups[g][-1] == 0 and (h, groups[g][2]) != (0, 0):
                        act_e.wait_ge(pool_d, 2 * h + groups[g][2])
                    if kind == "M" and groups[g][2:] == (0, 0) and h >= 1:
                        act_e.wait_ge(pmix_st, 16 * h)
                    act_e.wait_ge(grp, g + 1)
                    src = PR[g % 2]
                    if kind == "R":
                        sc.activation(row_sum[0:1, :], src[0:1, :], ACT.Copy).then_inc(evA, 1)
                    elif kind in "KQ":
                        part = groups[g][2]
                        if kind == "Q":
                            part += 1
                        if part == 0:
                            sc.activation(raw[:, PADC:PADC + TC], src[:, 0:TC], ACT.Copy).then_inc(evA, 1)
                        else:
                            lo = 2 * PADC + TC + (part - 1) * BN
                            sc.activation(raw[:, lo:lo + BN], src[:, :], ACT.Copy).then_inc(evA, 1)
                    elif kind == "V":
                        t = groups[g][2]
                        if h == 0:
                            if t == 0:
                                act_e.wait_ge(consts, 3)
                            sc.activation(g_tok[:, t].rearrange("p (i d x) -> p d i x", i=2, d=2)[:, :, :, 0:4],
                                          src[:, DV:VG].rearrange("p (d i x) -> p d i x", d=2, i=2), ACT.Copy)
                        sc.activation(V[:, par, t, 0:DV], src[:, 0:DV], ACT.Copy).then_inc(evA, 1)
                    elif kind == "O":
                        _, _, ft_, half = groups[g]
                        sc.activation(sig_o[:, ft_, half * BN:(half + 1) * BN], src[:, :], ACT.Sigmoid).then_inc(evA, 1)
                    elif kind == "P":
                        half = groups[g][3]
                        rows = ROWS // 2
                        sc.activation(pool_h0[:, half * rows:(half + 1) * rows, PADG:PADG + GRID_W],
                                      src[:, :].rearrange("p (a b) -> p a b", a=rows), ACT.Copy).then_inc(evA, 1)
                    else:
                        _, gg, fo, half = groups[g]
                        gg = POOL_ORDER[gg]
                        sc.activation(pmix[:, fo, half * BN:(half + 1) * BN], src[:, :], ACT.Copy,
                                      scale=pscale_col[:, 2 * gg + fo:2 * gg + fo + 1]).then_inc(evA, 1)
                elif item[0] == "silu":
                    _, h, n = item
                    act_e.wait_ge(conv_done, 2 * h + n + 1)
                    buf = kT[:, h % 2, :] if n == 0 else qT[:, h % 2, :]
                    sc.activation(buf, buf, ACT.Silu).then_inc(silu_done, 1)
                elif item[0] == "A":
                    _, h, j = item
                    for d in range(2):
                        s = h * NTT + j
                        ch, row = chunk_of(d, j), 32 * d + h
                        tl = LAST[d]
                        act_e.wait_ge(stA[d], s + 1)
                        if s:
                            act_e.wait_ge(cup[d], s)
                        pb = A_b[d]
                        a_s, mp = Acol[:, ch, row:row + 1], mp_col[:, 4 * d + h, j:j + 1]
                        if j < NC:
                            sc.activation(Dm[:, d, tl:tl + 1], pb[:, 0:1], ACT.Exp, bias=a_s)
                            sc.activation(WI[:, d, tl:tl + 1], pb[:, 0:1], ACT.Exp, bias=mp).then_inc(expd[d], 1)
                        else:
                            sc.activation(Dm[:, d, :], pb[:, 0:P], ACT.Exp, bias=a_s)
                            sc.activation(WI[:, d, :], pb[:, 0:P], ACT.Exp, bias=mp).then_inc(expd[d], 1)
                elif item[0] == "normalise":
                    h = item[1]
                    for d in range(2):
                        act_e.wait_ge(cup[d], (h + 1) * NTT)
                    if h:
                        act_e.wait_ge(hrs, h)
                    for t in range(NT):
                        link(sc.activation(Dm.rearrange("p a b -> p (a b)"), h_sum[:, t, :], ACT.Square, accum_out=ssh[:, t:t + 1]))
                    sc.activation(ssh, ssh, ACT.Sqrt, bias=eps, scale=1.0 / DV).then_inc(hsq, 1)


        @block.tensor
        def _(pe):
            te = nc.tensor
            pe.wait_ge(silu_c, 1)
            for i in range(NTT):
                for m in mod_pieces(i):
                    k = m % KD
                    pe.wait_ge(ld_mod[m % 4], 16 * (m // 4 + 1))
                    for n in range(NB):
                        if m == KD:
                            pe.wait_ge(mod_sum, n + 1)
                        last = te.matmul(bank[n][0:2, :], cc[:, :, k], mod_ring[:, m % 4, n * BN:(n + 1) * BN],
                                         start=(k == 0), stop=(k == KD - 1))
                    last.then_inc(mod_used, 1)
                if i == 0:
                    pe.wait_ge(consts, 2)
                pe.wait_ge(x_scaled, i + 1)
                for q in range(4):
                    if i:
                        pe.wait_ge(x_evD if q % 2 else x_evA, 2 * (i - 1) + q // 2 + 1)
                    for k in range(4):
                        last = te.transpose(bank[4 + q][:, k * P:(k + 1) * P], xt[:, i % 2, (4 * q + k) * P:(4 * q + k + 1) * P], ident)
                    last.then_inc(x_tr, 1)
            pe.wait_ge(mod_sum, 2 * NB)
            for m in range(2):
                for k in range(KD):
                    last = te.transpose(bank[0][:, 2 * (m * KD + k):2 * (m * KD + k) + 2], mod_row[0:2, m, k * P:(k + 1) * P],
                                        ident[0:2, 0:2])
            last.then_inc(mod_col, 1)

            for item in order:
                if item[0] == "gate_rows":
                    pe.wait_ge(evA, evac[group_no[("V", 0, NTT - 1)]][1])
                    for n, (lo, w) in enumerate(((0, TC), (TC, BN), (TC + BN, BN))):
                        for t in range(w // P):
                            last = te.transpose(bank[2 + n][0:100, t * P:(t + 1) * P], g_tok[:, lo // P + t, 0:100], ident)
                        last.then_inc(gate_mm, 1)
                elif item[0] == "gate_columns":
                    pe.wait_ge(grow, 2)
                    for j in range(NTT):
                        te.transpose(bank[5][:, j * GR:(j + 1) * GR], GX[0:GR, j * P:(j + 1) * P], ident[0:GR, 0:GR])
                        te.transpose(bank[6][:, j * GR:(j + 1) * GR], GB[0:GR, j * P:(j + 1) * P], ident[0:GR, 0:GR])
                    for r in range(8):
                        last = te.matmul(bank[7][:, r * NTT:(r + 1) * NTT], sel[0:GR, r, :], mpr[0:GR, 0:NTT], start=True, stop=True)
                    last.then_inc(gcol_mm, 1)
                elif item[0] == "group":
                    g = item[1]
                    kind, h = groups[g][0:2]
                    par = h % 2
                    if g >= 2:
                        dve, count = evac[g - 2]
                        pe.wait_ge(evD if dve else evA, count)
                    dst = PR[g % 2]
                    if (kind, h) == ("V", 0):
                        if groups[g][2] == 0:
                            pe.wait_ge(ld_vg, 32)
                        w = w_vg
                    elif kind in slot_of:
                        s = slot_no[(slot_of[kind], h)]
                        pe.wait_ge(ld_w[s % 2], 32 * (s // 2 + 1))
                        w = ring[:, s % 2]
                    if kind == "R":
                        pe.wait_ge(mac_used, MACP * (h + 1))
                        last = te.matmul(dst[0:1, :], ones_col, mac_sum, start=True, stop=True)
                    elif kind in "KQ":
                        part = groups[g][2] + (kind == "Q")
                        c0 = DQK * (kind == "Q")
                        width = TC if part == 0 else BN
                        for k in range(KD):
                            rhs = hcT[:, k, :] if part == 0 else hT[:, k, (part - 1) * BN:part * BN]
                            last = te.matmul(dst[:, 0:width], w[:, k, c0:c0 + DQK], rhs, start=(k == 0), stop=(k == KD - 1))
                    elif kind == "V":
                        t = groups[g][2]
                        width = VG if h == 0 else DV
                        for k in range(KD):
                            if h == 0 and t == 0:
                                pe.wait_ge(h_readyD, k + 1)
                            elif h == 0 and t == NC and k < H_DVE:
                                pe.wait_ge(h_readyD, KD + k + 1)
                            elif h == 0 and t == NC:
                                pe.wait_ge(h_readyA, k - H_DVE + 1)
                            lhs = hcT[:, k, t * P:(t + 1) * P] if t < NC else hT[:, k, (t - NC) * P:(t - NC + 1) * P]
                            last = te.matmul(dst[:, 0:width], lhs, w[:, k, :], start=(k == 0), stop=(k == KD - 1))
                    elif kind in "OP":
                        _, _, a, half = groups[g]
                        for k in range(KD):
                            last = te.matmul(dst[:, :], w[:, k, a * P:(a + 1) * P], hT[:, k, half * BN:(half + 1) * BN],
                                             start=(k == 0), stop=(k == KD - 1))
                    elif kind == "T":
                        _, _, a, half = groups[g]
                        pe.wait_ge(hnorm, h + 1)
                        for t in range(4):
                            last = te.transpose(dst[:, t * P:(t + 1) * P], h_sum[:, 4 * half + t, a * P:(a + 1) * P], ident)
                    else:
                        _, gg, fo, half = groups[g]
                        pe.wait_ge(pool_d, 2 * gg + 2)
                        pe.wait_ge(ld_pool, 32 * (gg + 1))
                        for a in range(2):
                            last = te.matmul(dst[:, :], poolw[:, a, fo * P:(fo + 1) * P], dT[a][:, half * BN:(half + 1) * BN],
                                             start=(a == 0), stop=(a == 1))
                    last.then_inc(grp, 1)
                elif item[0] == "A":
                    _, h, j = item
                    par, s = h % 2, h * NTT + j
                    for d in range(2):
                        ch, tl, pb = chunk_of(d, j), LAST[d], A_b[d]
                        if s:
                            pe.wait_ge(fac[d], s)
                        if j == 0:
                            pe.wait_ge(silu_done, 2 * h + 2)
                            pe.wait_ge(gcols, 4)
                        selr = sel[0:GR, 4 * d + h, :]
                        k0 = ch * P if ch < NC else LAT0 + (ch - NC) * P
                        kc = kT[:, par, k0:k0 + P]
                        if j < NC:
                            te.matmul(pb[:, 0:1], selr, MxN[0:GR, ch * P + tl:ch * P + tl + 1], start=True, stop=True)
                        else:
                            mx = MxN[0:GR, ch * P:(ch + 1) * P]
                            te.matmul(pb[:, 0:P], selr, mx, start=True, stop=True)
                            last = te.matmul(pb[:, P:2 * P], kc, qT[:, par, (ch - NC) * P:(ch - NC + 1) * P], start=True, stop=True)
                        if j < NTT - 1:
                            last = te.transpose(pb[:, 2 * P:3 * P], kc, ident)
                        last.then_inc(stA[d], 1)
                elif item[0] == "B":
                    _, h, j = item
                    par, s = h % 2, h * NTT + j
                    if j == 0:
                        pe.wait_ge(evA, evac[group_no[("V", h, NTT - 1)]][1])
                    for d in range(2):
                        ch = chunk_of(d, j)
                        pe.wait_ge(fac[d], s + 1)
                        if s:
                            pe.wait_ge(cup[d], s)
                        v = V[:, par, ch, :]
                        if j >= NC:
                            te.matmul(N_b[d][:, 0:DV + 1], Pm[:, d, :], v, start=True, stop=False)
                            last = te.matmul(N_b[d][:, 0:DV + 1], qw[:, d, :], C[:, d, j % 2, :], start=False, stop=True)
                        if j < NTT - 1:
                            last = te.matmul(C_b[d][:, 0:DV + 1], kw[:, d, :], v, start=True, stop=True)
                        last.then_inc(stB[d], 1)


        @block.vector
        def _(dve):
            ve = nc.vector

            def link(ins):
                chains["dve"] += 1
                ins.then_inc(dv, 1)
                dve.wait_ge(dv, chains["dve"])

            def mod_bias(m):
                dve.wait_ge(mod_used, KD * (m + 1))
                for n in range(NB):
                    rows = mod_row[0:2, m, n * BN:(n + 1) * BN]
                    ve.tensor_tensor(rows, bank[n][0:2, :], rows, ALU.add).then_inc(mod_sum, 1)

            dve.wait_ge(consts, 2)
            for i in range(NTT):
                dve.wait_ge(x_stat, i + 1)
                link(ve.reciprocal(rsx[:, i:i + 1], rsx[:, i:i + 1]))
                ve.tensor_scalar(xt[:, i % 2, :], xt[:, i % 2, :], rsx[:, i:i + 1], None, ALU.mult).then_inc(x_scaled, 1)
                if KD - 1 in mod_pieces(i):
                    dve.wait_ge(ld_bmod, 32)
                    mod_bias(0)
                if i == NTT - 1:
                    mod_bias(1)
                for q in (1, 3):
                    dve.wait_ge(x_tr, 4 * i + q + 1)
                    dst = hcT[:, 4 * q:4 * q + 4, i * P:(i + 1) * P] if i < NC else hT[:, 4 * q:4 * q + 4, (i - NC) * P:(i - NC + 1) * P]
                    ve.tensor_copy(dst, bank[4 + q][:, :].rearrange("p (a b) -> p a b", a=4)).then_inc(x_evD, 1)
            dve.wait_ge(mod_col, 1)
            dve.wait_ge(ld_const, 16 * 12)
            cols = bank[0][:, 0:4 * KD].rearrange("p (m k r) -> p m r k", m=2, k=KD)
            ve.tensor_copy(shift1, cols[:, 0])
            for r in range(2):
                last = ve.scalar_tensor_tensor(scale1[:, r, :], cols[:, 1, r, :], 1.0, norm_col[:, 0, :], ALU.add, ALU.mult)
            last.then_inc(s1_ready, 1)
            dve.wait_ge(s1_ready, 1)
            dve.wait_ge(x_evA, 2 * NTT)
            for k in range(KD):
                ve.tensor_scalar(hcT[:, k, :], hcT[:, k, :], scale1[:, 1, k:k + 1], shift1[:, 1, k:k + 1], ALU.mult, ALU.add).then_inc(h_readyD, 1)
            for k in range(H_DVE):
                ve.tensor_scalar(hT[:, k, :], hT[:, k, :], scale1[:, 0, k:k + 1], shift1[:, 0, k:k + 1], ALU.mult, ALU.add).then_inc(h_readyD, 1)
            ve.memset(V[:, 0, :, DV:DV + 1], 1.0)

            def pooling(g, a):
                L = POOL_ORDER[g] + 1

                def stages(src, bufs, axis, dst, size):
                    lo, hi = 0, size
                    cur = src
                    for k in range(L):
                        back, ahead = (1, 0) if k == 0 else (1 << (k - 1), 1 << (k - 1))
                        lo, hi = lo + back, hi - ahead
                        if k == L - 1:
                            lo, hi, nxt = PADG, size - PADG, dst
                        else:
                            nxt = bufs[k % 2]
                        if axis == 1:
                            target = nxt if k == L - 1 else nxt[:, :, lo:hi]
                            link(ve.tensor_tensor(target, cur[:, :, lo - back:hi - back], cur[:, :, lo + ahead:hi + ahead], ALU.add))
                        else:
                            target = nxt if k == L - 1 else nxt[:, lo:hi, :]
                            link(ve.tensor_tensor(target, cur[:, lo - back:hi - back, :], cur[:, lo + ahead:hi + ahead, :], ALU.add))
                        cur = nxt

                wide = pool_v[1].rearrange("p a b -> p (a b)")[:, 0:ROWS * HW_].rearrange("p (a b) -> p a b", a=ROWS)
                stages(pool_h0, [pool_h1, wide], 1, pool_v[0][:, PADG:PADG + ROWS, :], HW_)
                box = pool_h1.rearrange("p a b -> p (a b)")[:, 0:T].rearrange("p (a b) -> p a b", a=ROWS)
                stages(pool_v[0], [pool_v[1], pool_v[0]], 0, box, HR)
                if L >= 3:
                    ve.memset(pool_v[0][:, 0:PADG, :], 0.0)
                    ve.memset(pool_v[0][:, PADG + ROWS:, :], 0.0)
                dve.wait_ge(ld_pool, 32 * (g + 1))
                link(ve.tensor_tensor(box, box, inv_b.rearrange("p (a b) -> p a b", a=ROWS), ALU.mult))
                if g:
                    dve.wait_ge(grp, group_no[("M", g - 1, 1, 1)] + 1)
                ve.tensor_tensor(dT[a].rearrange("p (a b) -> p a b", a=ROWS), box,
                                 pool_h0[:, :, PADG:PADG + GRID_W], ALU.subtract).then_inc(pool_d, 1)

            for item in order:
                if item[0] == "gate_rows":
                    dve.wait_ge(grp, group_no[("V", 0, NTT - 1)] + 1)
                    ve.memset(LI[0:GR], 0.0)
                    ve.memset(MxN[0:GR], 0.0)
                    ve.memset(LF[0:GR], 0.0).then_inc(grow, 1)
                    ve.memset(raw[:, 0:PADC], 0.0)
                    ve.memset(raw[:, PADC + TC:2 * PADC + TC], 0.0)
                    ve.memset(raw[:, RAWN - PADC:RAWN], 0.0).then_inc(raw_clear, 1)
                    dve.wait_ge(gate_ev, 3)
                    link(ve.memset(reset[0:GR], 1.0))
                    ve.memset(reset[0:GR].rearrange("p (a b) -> p a b", b=P)[:, :, 0:1], 0.0)
                    ve.scalar_tensor_tensor(GX[0:GR], LF[0:GR], -1.0, LF[0:GR], ALU.mult, ALU.max).then_inc(gact, 1)
                    dve.wait_ge(gact, 2)
                    link(ve.scalar_tensor_tensor(LF[0:GR], LF[0:GR], 0.0, GX[0:GR], ALU.min, ALU.subtract))
                    link(ve.tensor_tensor_scan(GB[0:GR], reset[0:GR], LF[0:GR], 0.0, ALU.mult, ALU.add))
                    link(ve.tensor_tensor(LI[0:GR], LI[0:GR], GB[0:GR], ALU.subtract))
                    for j in range(NTT):
                        cs = slice(j * P, (j + 1) * P)
                        e = (j + 1) * P - 1
                        link(ve.tensor_tensor_scan(GX[0:GR, cs], LI[0:GR, cs], LI[0:GR, cs], mpr[0:GR, j:j + 1], ALU.max, ALU.max))
                        link(ve.tensor_tensor(mpr[0:GR, j + 1:j + 2], GB[0:GR, e:e + 1], GX[0:GR, e:e + 1], ALU.add))
                    link(ve.tensor_tensor(LF[0:GR], GB[0:GR], GX[0:GR], ALU.add))

                    def natural(dst, src):
                        ve.tensor_copy(dst[0:4, 0:GN], src[0:4, 0:GN])
                        ve.tensor_copy(dst[32:36, 0:TC], src[32:36, 0:TC][:, ::-1])
                        return ve.tensor_copy(dst[32:36, TC:TC + T], src[32:36, TC:TC + T][:, ::-1])

                    link(natural(MxN, GX))
                    natural(GX, LI)
                    natural(GB, LF).then_inc(grow, 1)
                elif item[0] == "gate_columns":
                    dve.wait_ge(gcol_mm, 1)
                    ve.tensor_copy(Acol, bank[5][:, 0:NTT * GR].rearrange("p (a b) -> p a b", a=NTT)).then_inc(gcols, 1)
                    ve.tensor_scalar(mp_col, bank[7][:, 0:8 * NTT].rearrange("p (a b) -> p a b", a=8), -1.0, None, ALU.mult).then_inc(gcols, 1)
                    ve.memset(V[:, 1, :, DV:DV + 1], 1.0).then_inc(gcols, 1)
                elif item[0] == "mac":
                    n = item[1]
                    dve.wait_ge(ld_mac[n % 2], 16 * (n // 2 + 1))
                    if n % MACP == 0 and n:
                        dve.wait_ge(grp, group_no[("R", n // MACP - 1)] + 1)
                    for q in range(2):
                        k = 2 * (n % MACP) + q
                        src, by = mac_ring[:, n % 2, q, :], cc[:, 0, k:k + 1]
                        if k == 0:
                            link(ve.tensor_scalar(mac_sum, src, by, None, ALU.mult))
                        elif q == 0:
                            dve.wait_ge(mac_used, n)
                            link(ve.scalar_tensor_tensor(mac_sum, src, by, mac_sum, ALU.mult, ALU.add))
                        else:
                            ve.scalar_tensor_tensor(mac_sum, src, by, mac_sum, ALU.mult, ALU.add).then_inc(mac_used, 1)
                elif item[0] == "group" and groups[item[1]][0] == "T":
                    g = item[1]
                    _, h, a, half = groups[g]
                    dve.wait_ge(evA, evac[group_no[("O", h, 1, 1)]][1])
                    dve.wait_ge(grp, g + 1)
                    so = sig_o[:, a, half * BN:(half + 1) * BN]
                    ve.scalar_tensor_tensor(so, PR[g % 2][:, :], headg_col[:, 2 * h + a:2 * h + a + 1], so, ALU.mult, ALU.mult).then_inc(evD, 1)
                elif item[0] == "conv":
                    _, h, n = item
                    dve.wait_ge(evA, evac[group_no[("K", h, 2) if n == 0 else ("Q", h, 1)]][1])
                    acc = kT[:, h % 2, :] if n == 0 else qT[:, h % 2, :]
                    lo, w = (0, CONVN) if n == 0 else (LAT0, T)
                    tap = conv_w[:, n, h, :]
                    link(ve.tensor_scalar(acc, raw[:, lo:lo + w], tap[:, 0:1], None, ALU.mult))
                    for j in range(1, TAPS):
                        ins = ve.scalar_tensor_tensor(acc, raw[:, lo + j:lo + j + w], tap[:, j:j + 1], acc, ALU.mult, ALU.add)
                        if j < TAPS - 1:
                            link(ins)
                    ins.then_inc(conv_done, 1)
                elif item[0] == "A":
                    _, h, j = item
                    par, s = h % 2, h * NTT + j
                    for d in range(2):
                        ch, tl, pb = chunk_of(d, j), LAST[d], A_b[d]
                        if j < NC:
                            dve.wait_ge(expd[d], s + 1)
                        else:
                            dve.wait_ge(masked[d], h * NT + j - NC + 1)
                        if s:
                            dve.wait_ge(stB[d], s)
                        if j >= NC:
                            ve.scalar_tensor_tensor(Pm[:, d, :], pb[:, P:2 * P], KSCALE, Dm[:, d, :], ALU.mult, ALU.mult)
                            last = ve.tensor_tensor(qw[:, d, :], qT[:, par, (ch - NC) * P:(ch - NC + 1) * P], WI[:, d, :], ALU.mult)
                        if j < NTT - 1:
                            last = ve.tensor_scalar(kw[:, d, :], pb[:, 2 * P:3 * P], Dm[:, d, tl:tl + 1], KSCALE, ALU.mult, ALU.mult)
                        last.then_inc(fac[d], 1)
                elif item[0] == "B":
                    _, h, j = item
                    s = h * NTT + j
                    for d in range(2):
                        ch, tl, row = chunk_of(d, j), LAST[d], 32 * d + h
                        dve.wait_ge(stB[d], s + 1)
                        if j < NTT - 1:
                            new, old = C[:, d, (j + 1) % 2, :], C[:, d, j % 2, :]
                            if j == 0:
                                last = ve.tensor_copy(new, C_b[d][:, 0:DV + 1])
                            else:
                                last = ve.scalar_tensor_tensor(new, old, WI[:, d, tl:tl + 1], C_b[d][:, 0:DV + 1], ALU.mult, ALU.add)
                        if j >= NC:
                            num, dcol = N_b[d], den[:, d:d + 1]
                            link(ve.tensor_scalar(dcol, num[:, DV:DV + 1], -1.0, EM[:, ch, row:row + 1], ALU.mult, ALU.max))
                            link(ve.tensor_tensor(dcol, num[:, DV:DV + 1], dcol, ALU.max))
                            link(ve.reciprocal(dcol, dcol))
                            hs = h_sum[:, ch - NC, :]
                            first = j < (NTT - 1 - ch + NC if d == 0 else ch)
                            if first:
                                last = ve.tensor_scalar(hs, num[:, 0:DV], dcol, None, ALU.mult)
                            else:
                                last = ve.scalar_tensor_tensor(hs, num[:, 0:DV], dcol, hs, ALU.mult, ALU.add)
                        last.then_inc(cup[d], 1)
                        dve.wait_ge(cup[d], s + 1)
                elif item[0] == "normalise":
                    h = item[1]
                    dve.wait_ge(hsq, h + 1)
                    ve.reciprocal(rsh, ssh).then_inc(hrs, 1)
                    dve.wait_ge(hrs, h + 1)
                    for t in range(NT):
                        last = ve.tensor_scalar(h_sum[:, t, :], h_sum[:, t, :], rsh[:, t:t + 1], None, ALU.mult)
                    last.then_inc(hnorm, 1)
                    if h == H - 2:
                        dve.wait_ge(grp, group_no[("V", H - 1, NC - 1)] + 1)
                        ve.memset(pool_v[0], 0.0)
                        ve.memset(pool_h0, 0.0).then_inc(gfree, 1)
                        dve.wait_ge(gfree, 1)
                elif item[0] == "pool":
                    _, g, a = item
                    dve.wait_ge(evA, evac[group_no[("P", g, a, 1)]][1])
                    pooling(g, a)


        stage.close()

        stage = ExitStack()
        UN = 2 * BN
        PARTS = 2 * OUL * UN + 2 * KD * BN
        parts = stage.enter_context(nc.sbuf_tensor("parts", [P, PARTS], fp32r))
        ARENA = SBUF - KEPT - PARTS
        arena = stage.enter_context(nc.sbuf_tensor("stage2", [P, ARENA], fp32))
        o_unit = carve(parts[:, 0:2 * OUL * UN], (OUL, 2, UN))
        mix = parts[:, 2 * OUL * UN:PARTS].rearrange("p (s k t) -> p s k t", s=2, k=KD)
        e_unit = carve(parts[:, 0:2 * USL * UN], (USL, 2, UN))
        o = 2 * USL * UN
        xsT = parts[:, o:o + 2 * D].rearrange("p (s k t) -> p s k t", s=2, k=KD)
        actT = parts[:, o + 2 * D:o + 2 * D + 2 * F].rearrange("p (s k t) -> p s k t", s=2, k=KF)
        assert o + 2 * D + 2 * F <= PARTS and CAP == P
        at[0] = 0
        x1 = take(NT * D, NT, D)
        raw_w = take(OSL * 2 * UN, OSL, 2, UN)
        raw_m = take(MSL * 2 * BN, MSL, 2, BN)
        gate1_b = take(D)
        tmp = take(2 * BN, 2, BN)
        squares = take(D)
        wr = take(KD * EXP, KD, EXP)
        lb = take(EXP)
        assert at[0] <= ARENA, at[0]
        at[0] = NT * D
        xnT = take(2 * D, 2, KD, P)
        L0, L1 = take(NT * EXP, NT, EXP), take(NT * EXP, NT, EXP)
        lst = take(4 * NT, 4, NT)
        HALF = 32
        affinity = take(NT * HALF, NT // 2, 2 * HALF)
        idx_all, gate_all = take(EXP + 1).bitcast(u32), take(EXP + 1)
        idx_gather, idx_scatter, gate_now = take(1).bitcast(u32), take(1).bitcast(u32), take(1)
        assert at[0] <= NT * D + (OSL * 2 * UN + MSL * 2 * BN)
        aff = squares[:, 0:T // 2]
        top_v, top_i, top_f, v_second, f_second, first_wins = (squares[:, T + n * P:T + (n + 1) * P] for n in range(6))
        top_i = top_i.bitcast(u32)
        e_raw = view(0, ESL, 2, UN)
        assert ESL * 2 * UN <= NT * D
        xs, y = view(NT * D, D), view(NT * D + D, D)
        act = squares[:, 0:F]
        gate2_b = gate1_b
        ft = [view(D * n, D) for n in range(NT)]
        normf_b = xs
        f_squares = y

        OU = 4 * KD
        K_ORDER = list(range(2 * H)) + [2 * (H + g) + a for g in POOL_ORDER for a in range(2)]
        EU = 2 * KD + 2 * KF
        EPC = EU // 2
        SIL, XV, ACTP, XP = 20, 28, 36, 40
        AHEAD = 4

        block = stage.enter_context(nc.Block())

        @block.sync
        def _(sp):
            w_out_k = w_out[0].rearrange("(k p) n -> p k n", p=P)
            sp.dma_start(wr, w_router[0].rearrange("(k p) e -> p k e", p=P)).then_inc(ld_r, 16)
            for q in range(OU // 2):
                c2, kk = q // (KD // 2), K_ORDER[2 * (q % (KD // 2))]
                th, ch = c2 // 2, c2 % 2
                if q == KD // 2 - 1:
                    sp.wait_ge(pmix_st, 16 * NG)
                if ch == 0:
                    m = th * (KD // 2) + q % (KD // 2)
                    if m >= MSL:
                        sp.wait_ge(m_lo, m - MSL + 1)
                    sp.dma_start(raw_m[:, m % MSL], mix_v[:, kk:kk + 2, th * BN:(th + 1) * BN]).then_inc(ld_mix[m % MSL], 16)
                if q >= OSL:
                    sp.wait_ge(o_lo, 2 * (q - OSL + 1))
                sp.dma_start(raw_w[:, q % OSL], w_out_k[:, kk:kk + 2, ch * UN:(ch + 1) * UN]).then_inc(ld_wo[q % OSL], 16)
                if q == OSL:
                    sp.dma_start(gate1_b, mod_scr[2, 0:1, :].to_broadcast([P, D])).then_inc(ld_g1, 16)
                    sp.dma_start(x1, x[0].rearrange("(n p) d -> p n d", p=P)).then_inc(ld_x1, 16)
            sp.wait_ge(o_ev, 4 * 2 * NB)
            sp.dma_start(gate2_b, mod_scr[5, 0:1, :].to_broadcast([P, D])).then_inc(ld_g2, 16)
            wg_v = w_gate[0].rearrange("e (k p) n -> e p k n", p=P)
            wu_v = w_up[0].rearrange("e (k p) n -> e p k n", p=P)
            wd_v = w_down[0].rearrange("e (k p) (a n) -> e p k a n", p=P, a=2)

            def load_piece(e, i):
                if i < KD // 2:
                    src = wg_v[e, :, 2 * i:2 * i + 2, :]
                elif i < KD:
                    src = wu_v[e, :, 2 * i - KD:2 * i - KD + 2, :]
                else:
                    src = wd_v[e, :, i - KD, :, :]
                sp.dma_start(e_raw[:, i % ESL], src).then_inc(ld_e[i % ESL], 16)

            sp.wait_ge(xn_st, 16 * NT)
            sp.wait_ge(r_tr, 4 * NT)
            for i in range(ESL):
                load_piece(0, i)
            with sp.Fori(0, EXP - 1) as e:
                for i in range(ESL, EPC + ESL):
                    sp.wait_ge(e_lo, e * EU + 2 * (i - ESL + 1))
                    sp.sem_inc(passed_sp)
                    load_piece(e if i < EPC else e + 1, i % EPC)
            for i in range(ESL, EPC):
                sp.wait_ge(e_lo, (EXP - 1) * EU + 2 * (i - ESL + 1))
                load_piece(EXP - 1, i)
            sp.wait_ge(e_lo, EXP * EU)
            sp.wait_ge(xs_lo, EXP)
            sp.dma_start(normf_b, norm_f.rearrange("(a d) -> a d", a=1).to_broadcast([P, D])).then_inc(ld_nf, 16)
            sp.wait_ge(scattered, 16 * EXP)
            for i in range(NT):
                sp.dma_start(ft[i], x1_t[i]).then_inc(ld_f[i], 16)
            for i in range(NT):
                sp.wait_ge(f_out, i + 1)
                sp.dma_start(out_t[i], ft[i]).then_inc(out_st, 16)
            sp.wait_ge(out_st, 16 * NT)

        @block.gpsimd
        def _(pool):
            eng = nc.gpsimd
            for i in range(NT):
                pool.wait_ge(o_ev, 2 * 2 * NB * (i // 4) + 2 * NB + 2 * (i % 4) + 2)
                eng.dma_start(x1_t[i], x1[:, i, :]).then_inc(x1_st[i], 16)
                if i % 4 == 3:
                    for j in range(i - 3, i + 1):
                        pool.wait_ge(x1_n, j + 1)
                        eng.dma_start(xn_t[j], x1[:, j, :]).then_inc(xn_st, 16)
            pool.wait_ge(xn_st, 16 * NT)
            pool.wait_ge(idx_r, 1)
            pool.sem_inc(y_free)
            eng.indirect_dma_start(xs, None, xn_scr, bass.IndirectOffsetOnAxis(ap=idx_gather, axis=0)).then_inc(gathered, 16)

            def scatter(e):
                pool.wait_ge(y_ev, e + 2)
                pool.sem_inc(passed_pool)
                eng.indirect_dma_start(x1_scr, bass.IndirectOffsetOnAxis(ap=idx_scatter, axis=0), y, None,
                                       compute_op=ALU.add).then_inc(scattered, 16)
                pool.wait_ge(scattered, e * 16 + 16)
                pool.sem_inc(y_free)

            with pool.Fori(0, EXP - 1) as e:
                pool.wait_ge(xs_lo, e + 1)
                pool.wait_ge(idx_r, e + 2)
                pool.sem_inc(passed_pool)
                eng.indirect_dma_start(xs, None, xn_scr, bass.IndirectOffsetOnAxis(ap=idx_gather, axis=0)).then_inc(gathered, 16)
                scatter(e)
            scatter(EXP - 1)

        @block.scalar
        def _(act_e):
            sc = nc.scalar

            def link(ins):
                chains["act"] += 1
                ins.then_inc(ac, 1)
                act_e.wait_ge(ac, chains["act"])

            def row_stat(i):
                act_e.wait_ge(o_ev, 2 * 2 * NB * (i // 4) + 2 * NB + 2 * (i % 4) + 2)
                link(sc.activation(squares, x1[:, i, :], ACT.Square, accum_out=ss1[:, i:i + 1]))
                sc.activation(rs1[:, i:i + 1], ss1[:, i:i + 1], ACT.Sqrt, bias=eps, scale=1.0 / D).then_inc(x1_sq, 1)

            for u in range(OU):
                c2, k = u // KD, u % KD
                if c2 == 2 and k >= 8 and k % 2 == 0:
                    row_stat(k // 2 - 4)
                th, ch, q = c2 // 2, c2 % 2, u // 2
                if ch == 0 and k % 2 == 0:
                    m = th * (KD // 2) + k // 2
                    act_e.wait_ge(ld_mix[m % MSL], 16 * (m // MSL + 1))
                    if th:
                        act_e.wait_ge(o_used, KD + k + 2)
                    sc.activation(mix[:, 0, K_ORDER[k]:K_ORDER[k] + 2, :], raw_m[:, m % MSL], ACT.Copy).then_inc(m_hi, 1)
                if k % 2 == 0:
                    act_e.wait_ge(ld_wo[q % OSL], 16 * (q // OSL + 1))
                if u >= OUL:
                    act_e.wait_ge(o_used, u - OUL + 1)
                sc.activation(o_unit[:, u % OUL, 0, :], raw_w[:, q % OSL, u % 2, :], ACT.Copy).then_inc(o_hi, 1)

            act_e.wait_ge(o_lo, OU)
            act_e.wait_ge(m_lo, KD)
            for i in range(NT):
                for q in range(4) if i < 4 else (0, 2):
                    act_e.wait_ge(r_tr, 4 * i + q + 1)
                    if i >= 2:
                        act_e.wait_ge(r_mm, i - 1)
                    sc.activation(xnT[:, i % 2, 4 * q:4 * q + 4, :], bank[q][:, :].rearrange("p (a b) -> p a b", a=4), ACT.Copy).then_inc(r_ev, 1)
                if i < 4:
                    row_stat(4 + i)
            act_e.wait_ge(sm_d, 1)
            sc.activation(L1, L0, ACT.Exp).then_inc(sm_a, 1)

            def high(e, u):
                if u % 2 == 0:
                    p = u // 2
                    act_e.wait_ge(ld_e[p % ESL], e * (16 * EPC // ESL) + 16 * (p // ESL + 1))
                act_e.wait_ge(e_used, e * EU + u + 1)
                sc.activation(e_unit[:, u % USL, 0, :], e_raw[:, (u // 2) % ESL, u % 2, :], ACT.Copy).then_inc(e_hi, 1)

            def xs_value():
                for k in range(KD // 2):
                    last = sc.activation(xs[:, k * P:(k + 1) * P], bank[4 + k // 4][:, (k % 4) * P:(k % 4 + 1) * P], ACT.Identity,
                                         bias=shift2[:, k:k + 1], scale=scale2[:, k:k + 1])
                last.then_inc(xs_vA, 1)

            def xs_high(n):
                act_e.wait_ge(xs_vA, n)
                act_e.wait_ge(xs_vD, n)
                sc.activation(xsT[:, 0], xs.rearrange("p (k t) -> p k t", k=KD), ACT.Copy).then_inc(xs_hi, 1)

            def expert(e, last):
                for u in range(AHEAD, EU):
                    if u == SIL:
                        act_e.wait_ge(e_used, e * EU + KD + USL)
                        for n in range(2):
                            ins = sc.activation(act[:, n * BN:(n + 1) * BN], bank[n][:, :], ACT.Silu)
                        ins.then_inc(g_act, 1)
                    if u == XV and not last:
                        act_e.wait_ge(xs_mm, e + 2)
                        xs_value()
                    if u == ACTP:
                        for n in range(2):
                            act_e.wait_ge(a_mm, e * 2 + n + 1)
                            sc.activation(actT[:, 0, 4 * n:4 * n + 4, :], bank[n][:, :].rearrange("p (a b) -> p a b", a=4),
                                          ACT.Copy).then_inc(a_hi, 1)
                    if u == XP and not last:
                        xs_high(e + 2)
                    high(e, u)
                if not last:
                    for u in range(AHEAD):
                        high(e + 1, u)

            for u in range(AHEAD):
                high(0, u)
            act_e.wait_ge(xs_mm, 1)
            xs_value()
            xs_high(1)
            with act_e.Fori(0, EXP - 1) as e:
                expert(e, False)
            expert(EXP - 1, True)
            act_e.wait_ge(scattered, 16 * EXP)
            for i in range(NT):
                act_e.wait_ge(ld_f[i], 16)
                link(sc.activation(f_squares, ft[i], ACT.Square, accum_out=ssf[:, i:i + 1]))
                sc.activation(rsf[:, i:i + 1], ssf[:, i:i + 1], ACT.Sqrt, bias=eps, scale=1.0 / D).then_inc(f_sq, 1)

        @block.tensor
        def _(pe):
            te = nc.tensor

            def product(banks, a, b, first, last):
                for step, (p, q) in enumerate(((0, 0), (0, 1), (1, 0))):
                    for n in range(2):
                        ins = te.matmul(banks[n][:, :], a[p], b[:, q, n * BN:(n + 1) * BN],
                                        start=(first and step == 0), stop=(last and step == 2))
                return ins

            pe.wait_ge(ld_r, 16)
            for k in range(KD):
                last = te.matmul(bank[7][0:1, 0:EXP], shift2[:, k:k + 1], wr[:, k, :], start=(k == 0), stop=(k == KD - 1))
            last.then_inc(r_bias, 1)
            for u in range(OU):
                c2, k = u // KD, u % KD
                if c2 % 2 == 0 and k % 2 == 0:
                    pe.wait_ge(m_lo, (c2 // 2) * (KD // 2) + k // 2 + 1)
                pe.wait_ge(o_lo, u + 1)
                for i in range(4):
                    if u == 0 and i == 3:
                        pe.wait_ge(r_log, 1)
                    if k == 0 and c2:
                        pe.wait_ge(o_ev, 8 * (c2 - 1) + 2 * i + 2)
                    last = product(bank[2 * i:2 * i + 2], [mix[:, s, K_ORDER[k], i * P:(i + 1) * P] for s in range(2)], o_unit[:, u % OUL],
                                   k == 0, k == KD - 1)
                    if k == KD - 1 and i < 3:
                        last.then_inc(o_tile, 1)
                last.then_inc(o_used, 1)
            def r_evacuated(i, q):
                if i < 4:
                    pe.wait_ge(r_ev, 4 * i + q + 1)
                elif q % 2 == 0:
                    pe.wait_ge(r_ev, 16 + 2 * (i - 4) + q // 2 + 1)
                else:
                    pe.wait_ge(rt_ev, 2 * (i - 4) + q // 2 + 1)

            def router_products(i):
                for q in range(4):
                    r_evacuated(i, q)
                for k in range(KD):
                    te.matmul(bank[4][:, i * EXP:(i + 1) * EXP], xnT[:, i % 2, k, :], wr[:, k, :], start=(k == 0), stop=False)
                te.matmul(bank[4][:, i * EXP:(i + 1) * EXP], ones_row[0:1, :], lb[0:1, :], start=False, stop=True).then_inc(r_mm, 1)

            pe.wait_ge(wr_s, 1)
            for i in range(NT):
                pe.wait_ge(x1_n, i + 1)
                for q in range(4):
                    if i:
                        r_evacuated(i - 1, q)
                    elif q % 2 == 0:
                        pe.wait_ge(o_ev, 3 * 8 + q + 2)
                    for k in range(4):
                        last = te.transpose(bank[q][:, k * P:(k + 1) * P], x1[:, i, (4 * q + k) * P:(4 * q + k + 1) * P], ident)
                    last.then_inc(r_tr, 1)
                if i == 1:
                    pe.wait_ge(o_ev, 3 * 8 + 6)
                if i:
                    router_products(i - 1)
            router_products(NT - 1)
            pe.wait_ge(sm_d, 2)
            for i in range(NT // 2):
                last = te.transpose(bank[0][0:HALF + EXP, i * P:(i + 1) * P], affinity[:, i, 0:HALF + EXP], ident)
                if i == 0:
                    last.then_inc(e_used, USL)
            last.then_inc(aff_mm, 1)
            pe.wait_ge(topk, 1)
            te.transpose(bank[2][:, 0:EXP], top_f[0:EXP, :], ident[0:EXP, 0:EXP])
            te.transpose(bank[2][:, EXP:2 * EXP], top_v[0:EXP, :], ident[0:EXP, 0:EXP]).then_inc(topk_mm, 1)

            def transpose_xs():
                for k in range(KD):
                    last = te.transpose(bank[4 + k // 4][:, (k % 4) * P:(k % 4 + 1) * P], xs[:, k * P:(k + 1) * P], ident)
                last.then_inc(xs_mm, 1)

            def expert(e, final):
                pe.wait_ge(xs_lo, e + 1)
                for u in range(2 * KD):
                    half, k = u // KD, u % KD
                    if u == SIL and not final:
                        pe.wait_ge(gathered, e * 16 + 32)
                        pe.wait_ge(y_ev, e + 1)
                        transpose_xs()
                    pe.wait_ge(e_lo, e * EU + u + 1)
                    last = product(bank[2 * half:2 * half + 2], [xsT[:, s, k, :] for s in range(2)], e_unit[:, u % USL],
                                   k == 0, k == KD - 1)
                    last.then_inc(e_used, 1)
                pe.wait_ge(a_rdy, e + 1)
                for k in range(KF):
                    last = te.transpose(bank[k // 4][:, (k % 4) * P:(k % 4 + 1) * P], act[:, k * P:(k + 1) * P], ident)
                    if k % 4 == 3:
                        last.then_inc(a_mm, 1)
                if not final:
                    pe.wait_ge(xs_vA, e + 2)
                    pe.wait_ge(xs_vD, e + 2)
                else:
                    pe.wait_ge(y_ev, EXP)
                for u in range(2 * KD, EU):
                    k, half = (u - 2 * KD) // 2, u % 2
                    if half == 0 and k % 4 == 0:
                        pe.wait_ge(a_lo, e * 2 + k // 4 + 1)
                    pe.wait_ge(e_lo, e * EU + u + 1)
                    last = product(bank[4 + 2 * half:6 + 2 * half], [actT[:, s, k, :] for s in range(2)], e_unit[:, u % USL],
                                   k == 0, k == KF - 1)
                    last.then_inc(e_used, 1)

            pe.wait_ge(topk_ev, 1)
            pe.wait_ge(gathered, 16)
            transpose_xs()
            with pe.Fori(0, EXP - 1) as e:
                expert(e, False)
            expert(EXP - 1, True)

        @block.vector
        def _(dve):
            ve = nc.vector

            def link(ins):
                chains["dve"] += 1
                ins.then_inc(dv, 1)
                dve.wait_ge(dv, chains["dve"])

            def add_block(c2):
                th, ch = c2 // 2, c2 % 2
                for b in range(8):
                    i, n = 4 * th + b // 2, 2 * ch + b % 2
                    if b == 6:
                        dve.wait_ge(o_used, (c2 + 1) * KD)
                    elif b % 2 == 0:
                        dve.wait_ge(o_tile, 3 * c2 + b // 2 + 1)
                    link(ve.tensor_tensor(tmp[:, b % 2, :], bank[b][:, :], gate1_b[:, n * BN:(n + 1) * BN], ALU.mult))
                    xb = x1[:, i, n * BN:(n + 1) * BN]
                    ve.tensor_tensor(xb, xb, tmp[:, b % 2, :], ALU.add).then_inc(o_ev, 1)

            def normalise_rows(i):
                dve.wait_ge(x1_sq, i + 1)
                link(ve.reciprocal(rs1[:, i:i + 1], rs1[:, i:i + 1]))
                dve.wait_ge(x1_st[i], 16)
                ve.tensor_scalar(x1[:, i, :], x1[:, i, :], rs1[:, i:i + 1], None, ALU.mult).then_inc(x1_n, 1)

            ROWS_K = HALF + EXP
            dve.wait_ge(ld_r, 16)
            link(ve.scalar_tensor_tensor(scale2, scale2, 1.0, norm_col[:, 1, :], ALU.add, ALU.mult))
            dve.wait_ge(r_bias, 1)
            ve.tensor_copy(lb[0:1, :], bank[7][0:1, 0:EXP]).then_inc(r_log, 1)
            for k in range(KD):
                last = ve.tensor_scalar(wr[:, k, :], wr[:, k, :], scale2[:, k:k + 1], None, ALU.mult)
            last.then_inc(wr_s, 1)
            for u in range(OU):
                c2, k = u // KD, u % KD
                th, ch, q = c2 // 2, c2 % 2, u // 2
                if c2 == 2 and k >= 9 and k % 2 == 1:
                    normalise_rows(k // 2 - 4)
                if ch == 0 and k % 2 == 0:
                    m = th * (KD // 2) + k // 2
                    dve.wait_ge(m_hi, m + 1)
                    kk = K_ORDER[k]
                    ve.tensor_tensor(mix[:, 1, kk:kk + 2, :], raw_m[:, m % MSL], mix[:, 0, kk:kk + 2, :].bitcast(fp32), ALU.subtract).then_inc(m_lo, 1)
                dve.wait_ge(o_hi, u + 1)
                ve.tensor_tensor(o_unit[:, u % OUL, 1, :], raw_w[:, q % OSL, u % 2, :], o_unit[:, u % OUL, 0, :].bitcast(fp32),
                                 ALU.subtract).then_inc(o_lo, 1)
                if u == KD + 1:
                    dve.wait_ge(ld_x1, 16)
                    dve.wait_ge(ld_g1, 16)
                if c2 and k == 1:
                    add_block(c2 - 1)
            add_block(3)
            for i in range(4, NT):
                normalise_rows(i)
            for i in range(4, NT):
                for q in (1, 3):
                    dve.wait_ge(r_tr, 4 * i + q + 1)
                    dve.wait_ge(r_mm, i - 1)
                    ve.tensor_copy(xnT[:, i % 2, 4 * q:4 * q + 4, :], bank[q][:, :].rearrange("p (a b) -> p a b", a=4)).then_inc(rt_ev, 1)
            ve.memset(affinity, 0.0)
            dve.wait_ge(r_mm, NT)
            logits = bank[4][:, 0:NT * EXP].rearrange("p (a b) -> p a b", a=NT)
            link(ve.tensor_reduce(lst[:, 0, :], logits, AX.X, ALU.max))
            ve.tensor_tensor(L0, logits, lst[:, 0, :].unsqueeze(2).to_broadcast([P, NT, EXP]), ALU.subtract).then_inc(sm_d, 1)
            dve.wait_ge(sm_a, 1)
            link(ve.tensor_reduce(lst[:, 1, :], L1, AX.X, ALU.add))
            link(ve.reciprocal(lst[:, 1, :], lst[:, 1, :]))
            for n in range(2):
                half = slice(n * NT // 2, (n + 1) * NT // 2)
                last = ve.tensor_tensor(affinity[:, :, n * HALF:n * HALF + EXP], L1[:, half, :],
                                        lst[:, 1, half].unsqueeze(2).to_broadcast([P, NT // 2, EXP]), ALU.mult)
            last.then_inc(sm_d, 1)
            dve.wait_ge(aff_mm, 1)
            link(ve.tensor_copy(aff[0:ROWS_K], bank[0][0:ROWS_K, :]))
            for r in range(CAP // 8):
                best, at8 = top_v[0:ROWS_K, 8 * r:8 * r + 8], top_i[0:ROWS_K, 8 * r:8 * r + 8]
                link(ve.max(best, aff[0:ROWS_K]))
                ve.max_index(at8, best, aff[0:ROWS_K])
                if r < CAP // 8 - 1:
                    link(ve.match_replace(aff[0:ROWS_K], best, aff[0:ROWS_K], -1.0))
            link(ve.memset(small[:, 121:122], 0.0))
            ve.tensor_copy(v_second[0:EXP], top_v[HALF:ROWS_K, ::-1])
            ve.tensor_copy(top_f[0:EXP], top_i[0:EXP])
            link(ve.tensor_copy(f_second[0:EXP], top_i[HALF:ROWS_K, ::-1]))
            ve.tensor_tensor(first_wins[0:EXP], top_v[0:EXP], v_second[0:EXP], ALU.is_ge)
            link(ve.tensor_scalar(f_second[0:EXP], f_second[0:EXP], float(T // 2), None, ALU.add))
            ve.tensor_tensor(top_v[0:EXP], top_v[0:EXP], v_second[0:EXP], ALU.max)
            link(ve.tensor_tensor(top_f[0:EXP], top_f[0:EXP], f_second[0:EXP], ALU.subtract))
            link(ve.tensor_tensor(top_f[0:EXP], top_f[0:EXP], first_wins[0:EXP], ALU.mult))
            ve.tensor_tensor(top_f[0:EXP], top_f[0:EXP], f_second[0:EXP], ALU.add).then_inc(topk, 1)
            dve.wait_ge(topk_mm, 1)
            ve.tensor_copy(idx_all[:, 0:EXP], bank[2][:, 0:EXP])
            ve.tensor_copy(idx_all[:, EXP:EXP + 1], bank[2][:, 0:1])
            ve.tensor_copy(gate_all[:, 0:EXP], bank[2][:, EXP:2 * EXP])
            link(ve.tensor_copy(gate_all[:, EXP:EXP + 1], bank[2][:, EXP:EXP + 1]))
            ve.tensor_copy(idx_gather, idx_all[:, 0:1]).then_inc(idx_r, 1)
            ve.memset(small[:, 122:123], 0.0).then_inc(topk_ev, 1)
            ve.memset(small[:, 124:125], 0.0).then_inc(y_ev, 1)

            def low(e, u):
                dve.wait_ge(e_hi, e * EU + u + 1)
                ve.tensor_tensor(e_unit[:, u % USL, 1, :], e_raw[:, (u // 2) % ESL, u % 2, :], e_unit[:, u % USL, 0, :].bitcast(fp32),
                                 ALU.subtract).then_inc(e_lo, 1)

            def xs_value():
                for k in range(KD // 2, KD):
                    last = ve.tensor_scalar(xs[:, k * P:(k + 1) * P], bank[4 + k // 4][:, (k % 4) * P:(k % 4 + 1) * P],
                                            scale2[:, k:k + 1], shift2[:, k:k + 1], ALU.mult, ALU.add)
                last.then_inc(xs_vD, 1)

            def xs_low(n):
                dve.wait_ge(xs_hi, n)
                ve.tensor_tensor(xsT[:, 1], xs.rearrange("p (k t) -> p k t", k=KD), xsT[:, 0].bitcast(fp32), ALU.subtract).then_inc(xs_lo, 1)

            def results(e):
                dve.wait_ge(y_free, e + 1)
                ve.memset(small[:, 123:124], 0.0)
                ve.tensor_copy(idx_scatter, idx_all[:, bass.ds(e, 1)])
                ve.tensor_copy(gate_now, gate_all[:, bass.ds(e, 1)]).then_inc(cols_set, 1)
                dve.wait_ge(cols_set, e + 1)
                dve.wait_ge(e_used, e * EU + EU + USL)
                for n in range(NB):
                    last = ve.scalar_tensor_tensor(y[:, n * BN:(n + 1) * BN], bank[4 + n][:, :], gate_now,
                                                   gate2_b[:, n * BN:(n + 1) * BN], ALU.mult, ALU.mult)
                last.then_inc(y_ev, 1)

            def expert(e, final):
                for u in range(AHEAD, EU + 1):
                    if u == XV and not final:
                        dve.wait_ge(xs_mm, e + 2)
                        xs_value()
                    if u == ACTP:
                        dve.wait_ge(g_act, e + 1)
                        dve.wait_ge(e_used, e * EU + 2 * KD + USL)
                        for n in range(2):
                            a_half = act[:, n * BN:(n + 1) * BN]
                            last = ve.tensor_tensor(a_half, a_half, bank[2 + n][:, :], ALU.mult)
                        last.then_inc(a_rdy, 1)
                        for n in range(2):
                            dve.wait_ge(a_hi, e * 2 + n + 1)
                            ve.tensor_tensor(actT[:, 1, 4 * n:4 * n + 4, :], bank[n][:, :].rearrange("p (a b) -> p a b", a=4),
                                             actT[:, 0, 4 * n:4 * n + 4, :].bitcast(fp32), ALU.subtract).then_inc(a_lo, 1)
                    if u == XP and not final:
                        xs_low(e + 2)
                        ve.memset(small[:, 123:124], 0.0)
                        ve.tensor_copy(idx_gather, idx_all[:, bass.ds(e + 2, 1)]).then_inc(idx_r, 1)
                    if u < EU:
                        low(e, u)
                if not final:
                    for u in range(AHEAD):
                        low(e + 1, u)
                results(e)

            for u in range(AHEAD):
                low(0, u)
            dve.wait_ge(xs_mm, 1)
            xs_value()
            xs_low(1)
            ve.tensor_copy(idx_gather, idx_all[:, 1:2]).then_inc(idx_r, 1)
            dve.wait_ge(ld_g2, 16)
            with dve.Fori(0, EXP - 1) as e:
                expert(e, False)
            expert(EXP - 1, True)
            dve.wait_ge(ld_nf, 16)
            for i in range(NT):
                dve.wait_ge(f_sq, i + 1)
                link(ve.reciprocal(rsf[:, i:i + 1], rsf[:, i:i + 1]))
                ve.scalar_tensor_tensor(ft[i], ft[i], rsf[:, i:i + 1], normf_b, ALU.mult, ALU.mult).then_inc(f_out, 1)
        stage.close()


def inverse_counts():
    import numpy as np
    grid_w, rows = 64, 16
    out = np.zeros((4, rows * grid_w), np.float32)
    for g, w in enumerate((2, 4, 8, 16)):
        def count(n):
            t = np.arange(n)
            return np.minimum(t + w // 2, n) - np.maximum(t - w // 2, 0)
        out[g] = (1.0 / (count(rows)[:, None] * count(grid_w)[None, :])).reshape(-1)
    return out


_INS = ["x", "c", "ctx", "c_ctx", "w_mod", "b_mod", "norm1", "w_in", "conv_q_w", "conv_k_w", "b_gates", "head_g",
        "pool_w", "pool_scale", "w_out", "norm2", "w_router", "w_gate", "w_up", "w_down", "norm_f"]


def kernel(**inputs):
    import numpy as _np
    import concourse.bacc as _bacc
    from concourse import mybir as _mybir
    from concourse.bass_utils import run_bass_kernel_spmd as _run

    nc = _bacc.Bacc("TRN2", target_bir_lowering=False, num_devices=1)
    arrays, args = {}, []
    for name in _INS + ["inv_count"]:
        a = inverse_counts() if name == "inv_count" else _np.ascontiguousarray(inputs[name])
        arrays[f"in_{name}_dram"] = a
        args.append(nc.dram_tensor(f"in_{name}_dram", a.shape, _mybir.dt.from_np(a.dtype), kind="ExternalInput").ap())
    shape = inputs["x"].shape
    args.append(nc.dram_tensor("out_0_dram", shape, _mybir.dt.float32, kind="ExternalOutput").ap())
    hybrid_layer_kernel(nc, *args)
    r = _run(nc, [arrays], core_ids=[0])
    return r.results[0]["out_0_dram"]
```
